# Optimizing a Trainium2 kernel written in Bass

```python
import jax, jax.numpy as jnp
from jax import lax
import numpy as np
import math

D_MODEL = 1024
BATCH = 1
SEQ = 512
DEPTH = 1

CHUNK = 64
Q_BLOCK = 128
A_HEADS = 8
A_HEAD_DIM = 64
A_WIDTH = A_HEADS * A_HEAD_DIM
B_HEADS = 8
B_Q_RANK = 256
B_KV_RANK = 128
B_NOPE = 64
B_ROPE = 32
B_V_DIM = 64
B_WIDTH = B_HEADS * B_V_DIM
ROPE_BASE = 10000.0
FFN_HIDDEN = 2816
NORM_EPS = 1e-6
NEG_INF = -1e30
IN_SIZES = (A_WIDTH, A_WIDTH, A_WIDTH, A_HEADS, B_Q_RANK, B_KV_RANK, B_ROPE, D_MODEL, D_MODEL)
IN_WIDTH = 3 * A_WIDTH + A_HEADS + B_Q_RANK + B_KV_RANK + B_ROPE + 2 * D_MODEL


def rms_norm(x, g):
    xf = x.astype(jnp.float32)
    y = xf * lax.rsqrt(jnp.mean(xf * xf, axis=-1, keepdims=True) + NORM_EPS)
    return (y * g.astype(jnp.float32)).astype(x.dtype)

def rope_cos_sin(positions):
    half = B_ROPE // 2
    inv_freq = ROPE_BASE ** (-jnp.arange(half, dtype=jnp.float32) / half)
    ang = positions.astype(jnp.float32)[..., None] * inv_freq
    return jnp.cos(ang), jnp.sin(ang)

def apply_rope(x, cos, sin):
    xf = x.astype(jnp.float32)
    x1, x2 = jnp.split(xf, 2, axis=-1)
    out = jnp.concatenate([x1 * cos - x2 * sin, x2 * cos + x1 * sin], axis=-1)
    return out.astype(x.dtype)

def to_blocks(t):
    b, s = t.shape[0], t.shape[1]
    return t.reshape((b, s // Q_BLOCK, Q_BLOCK) + t.shape[2:]).swapaxes(0, 1)

def from_blocks(t):
    t = t.swapaxes(0, 1)
    return t.reshape((t.shape[0], t.shape[1] * t.shape[2]) + t.shape[3:])

def forgetting_attention(q, k, v, log_f):
    s_len = q.shape[1]
    nb = s_len // Q_BLOCK
    scale = A_HEAD_DIM ** -0.5
    c = jnp.cumsum(log_f, axis=1)
    c_keys = c.transpose(0, 2, 1)
    k_pos = jnp.arange(s_len)

    def one_block(args):
        i, q_i, c_i = args
        q_pos = i * Q_BLOCK + jnp.arange(Q_BLOCK)
        s = jnp.einsum('bqhd,bkhd->bhqk', q_i, k, preferred_element_type=jnp.float32) * scale
        bias = c_i.transpose(0, 2, 1)[..., :, None] - c_keys[..., None, :]
        mask = k_pos[None, :] <= q_pos[:, None]
        s = jnp.where(mask, s + bias, NEG_INF)
        p = jax.nn.softmax(s, axis=-1).astype(v.dtype)
        return jnp.einsum('bhqk,bkhd->bqhd', p, v)

    out = lax.map(one_block, (jnp.arange(nb), to_blocks(q), to_blocks(c)))
    return from_blocks(out)

def latent_attention(q_nope, q_rope, k_nope, k_rope, v):
    s_len = q_nope.shape[1]
    nb = s_len // Q_BLOCK
    scale = (B_NOPE + B_ROPE) ** -0.5
    k_chunk = jnp.arange(s_len) // CHUNK

    def one_block(args):
        i, qn, qr = args
        q_chunk = (i * Q_BLOCK + jnp.arange(Q_BLOCK)) // CHUNK
        s = (jnp.einsum('bqhd,bkhd->bhqk', qn, k_nope, preferred_element_type=jnp.float32)
             + jnp.einsum('bqhr,bkr->bhqk', qr, k_rope, preferred_element_type=jnp.float32))
        s = jnp.where(k_chunk[None, :] <= q_chunk[:, None], s * scale, NEG_INF)
        p = jax.nn.softmax(s, axis=-1).astype(v.dtype)
        return jnp.einsum('bhqk,bkhd->bqhd', p, v)

    out = lax.map(one_block, (jnp.arange(nb), to_blocks(q_nope), to_blocks(q_rope)))
    return from_blocks(out)

def hybrid_mixer(xn, cos, sin, w_in, b_forget, q_a_norm_g, w_q_up, kv_a_norm_g, w_kv_up,
                 w_branch_a, w_branch_b, b_gate, w_out):
    bsz, s_len, _ = xn.shape
    splits = [int(v) for v in np.cumsum(IN_SIZES)[:-1]]
    proj = xn @ w_in
    qa, ka, va, fa, cq, ckv, kr, ga, gb = jnp.split(proj, splits, axis=-1)

    qa = qa.reshape(bsz, s_len, A_HEADS, A_HEAD_DIM)
    ka = ka.reshape(bsz, s_len, A_HEADS, A_HEAD_DIM)
    va = va.reshape(bsz, s_len, A_HEADS, A_HEAD_DIM)
    log_f = jax.nn.log_sigmoid((fa + b_forget).astype(jnp.float32))
    ya = forgetting_attention(qa, ka, va, log_f).reshape(bsz, s_len, A_WIDTH)

    qb = (rms_norm(cq, q_a_norm_g) @ w_q_up).reshape(bsz, s_len, B_HEADS, B_NOPE + B_ROPE)
    q_nope, q_rope = qb[..., :B_NOPE], qb[..., B_NOPE:]
    q_rope = apply_rope(q_rope, cos[:, :, None, :], sin[:, :, None, :])
    kv = (rms_norm(ckv, kv_a_norm_g) @ w_kv_up).reshape(bsz, s_len, B_HEADS, B_NOPE + B_V_DIM)
    k_nope, vb = kv[..., :B_NOPE], kv[..., B_NOPE:]
    k_rope = apply_rope(kr, cos, sin)
    yb = latent_attention(q_nope, q_rope, k_nope, k_rope, vb).reshape(bsz, s_len, B_WIDTH)

    gate_a = jax.nn.sigmoid(ga + b_gate[:D_MODEL])
    gate_b = jax.nn.sigmoid(gb + b_gate[D_MODEL:])
    merged = gate_a * (ya @ w_branch_a) + gate_b * (yb @ w_branch_b)
    return merged @ w_out

def swiglu(xn, w_gate, w_up, w_down):
    return (jax.nn.silu(xn @ w_gate) * (xn @ w_up)) @ w_down

def first_inputs(seed: int = 0) -> dict:
    key = jax.random.key(seed)
    ks = jax.random.split(key, 20)
    f32 = jnp.float32

    def w(k, shape, fan_in):
        return jax.random.normal(k, shape, f32) * (fan_in ** -0.5)

    def gain(k, shape):
        return 1.0 + 0.05 * jax.random.normal(k, shape, f32)

    x = jax.random.normal(ks[0], (BATCH, SEQ, D_MODEL), f32)
    offsets = jax.random.randint(ks[1], (BATCH, 1), 0, 100000, dtype=jnp.int32)
    positions = offsets + jnp.arange(SEQ, dtype=jnp.int32)[None, :]
    return {
        "x": x,
        "positions": positions,
        "norm_mix_g": gain(ks[2], (DEPTH, D_MODEL)),
        "w_in": w(ks[3], (DEPTH, D_MODEL, IN_WIDTH), D_MODEL),
        "b_forget": jax.random.uniform(ks[4], (DEPTH, A_HEADS), f32, 1.0, 5.0),
        "q_a_norm_g": gain(ks[5], (DEPTH, B_Q_RANK)),
        "w_q_up": w(ks[6], (DEPTH, B_Q_RANK, B_HEADS * (B_NOPE + B_ROPE)), B_Q_RANK),
        "kv_a_norm_g": gain(ks[7], (DEPTH, B_KV_RANK)),
        "w_kv_up": w(ks[8], (DEPTH, B_KV_RANK, B_HEADS * (B_NOPE + B_V_DIM)), B_KV_RANK),
        "w_branch_a": w(ks[9], (DEPTH, A_WIDTH, D_MODEL), A_WIDTH),
        "w_branch_b": w(ks[10], (DEPTH, B_WIDTH, D_MODEL), B_WIDTH),
        "b_gate": 0.02 * jax.random.normal(ks[11], (DEPTH, 2 * D_MODEL), f32),
        "w_out": w(ks[12], (DEPTH, D_MODEL, D_MODEL), D_MODEL),
        "norm_ffn_g": gain(ks[13], (DEPTH, D_MODEL)),
        "w_ffn_gate": w(ks[14], (DEPTH, D_MODEL, FFN_HIDDEN), D_MODEL),
        "w_ffn_up": w(ks[15], (DEPTH, D_MODEL, FFN_HIDDEN), D_MODEL),
        "w_ffn_down": w(ks[16], (DEPTH, FFN_HIDDEN, D_MODEL), FFN_HIDDEN),
        "norm_final_g": gain(ks[17], (D_MODEL,)),
    }

def first_block(x, positions, norm_mix_g, w_in, b_forget, q_a_norm_g, w_q_up, kv_a_norm_g,
              w_kv_up, w_branch_a, w_branch_b, b_gate, w_out, norm_ffn_g, w_ffn_gate,
              w_ffn_up, w_ffn_down, norm_final_g):
    cos, sin = rope_cos_sin(positions)
    h = x
    for l in range(DEPTH):
        xn = rms_norm(h, norm_mix_g[l])
        h = h + hybrid_mixer(xn, cos, sin, w_in[l], b_forget[l], q_a_norm_g[l], w_q_up[l],
                             kv_a_norm_g[l], w_kv_up[l], w_branch_a[l], w_branch_b[l],
                             b_gate[l], w_out[l])
        hn = rms_norm(h, norm_ffn_g[l])
        h = h + swiglu(hn, w_ffn_gate[l], w_ffn_up[l], w_ffn_down[l])
    return rms_norm(h, norm_final_g)


NSA_HEADS = 16
NSA_KV_GROUPS = 2
NSA_HEADS_PER_GROUP = NSA_HEADS // NSA_KV_GROUPS
NSA_HEAD_DIM = 64
CMP_BLOCK = 32
CMP_STRIDE = 16
CMP_HIDDEN = 256
SLC_BLOCK = 64
SLC_TOPN = 16
WINDOW = 512
ROPE_THETA = 500000.0
ROPE_DIM = NSA_HEAD_DIM // 4
FORCED_SCORE = 1.0e4

RET_HEADS = 8
RET_KEY_DIM = 64
RET_VAL_DIM = 128
RET_CHUNK = 128
RET_ROPE_THETA = 10000.0

D_FF = 2816
EPS = 1e-6
GN_EPS = 1e-5
NEG_INF_2 = -1e30

NSA_Q_W = NSA_HEADS * NSA_HEAD_DIM
NSA_KV_W = NSA_KV_GROUPS * NSA_HEAD_DIM
NSA_GATE_W = 3 * NSA_HEADS
RET_QK_W = RET_HEADS * RET_KEY_DIM
RET_V_W = RET_HEADS * RET_VAL_DIM
IN_WIDTHS = (NSA_Q_W, NSA_KV_W, NSA_KV_W, NSA_KV_W, NSA_KV_W, NSA_KV_W, NSA_KV_W,
             NSA_GATE_W, RET_QK_W, RET_QK_W, RET_V_W, RET_V_W, 2 * D_MODEL)
D_IN = sum(IN_WIDTHS)


def _rmsnorm(x, g):
    xf = x.astype(jnp.float32)
    y = xf * lax.rsqrt(jnp.mean(xf * xf, axis=-1, keepdims=True) + EPS)
    return (y * g.astype(jnp.float32)).astype(x.dtype)

def _swiglu(x, w_gate, w_up, w_down):
    return (jax.nn.silu(x @ w_gate) * (x @ w_up)) @ w_down

def _rope(x, pos, rot_dim, theta):
    half = rot_dim // 2
    freqs = theta ** (-(jnp.arange(half, dtype=jnp.float32) * 2.0 / rot_dim))
    ang = pos.astype(jnp.float32)[:, None] * freqs[None, :]
    cos = jnp.cos(ang).astype(x.dtype)
    sin = jnp.sin(ang).astype(x.dtype)
    x1 = x[..., :half]
    x2 = x[..., half:rot_dim]
    return jnp.concatenate([x1 * cos - x2 * sin, x2 * cos + x1 * sin, x[..., rot_dim:]], axis=-1)

def _masked_softmax(s, mask):
    s = jnp.where(mask, s.astype(jnp.float32), NEG_INF_2)
    m = jnp.max(s, axis=-1, keepdims=True)
    p = jnp.where(mask, jnp.exp(s - m), 0.0)
    return p / jnp.maximum(jnp.sum(p, axis=-1, keepdims=True), 1e-20)

def _nsa(q, k_cmp, v_cmp, k_slc, v_slc, k_win, v_win, gates, pos_emb, ck_w1, ck_w2, cv_w1, cv_w2):
    B, G, Hg, S, dh = q.shape
    scale = dh ** -0.5
    pos = jnp.arange(S)
    q = _rope(q, pos, ROPE_DIM, ROPE_THETA)
    k_slc = _rope(k_slc, pos, ROPE_DIM, ROPE_THETA)
    k_win = _rope(k_win, pos, ROPE_DIM, ROPE_THETA)

    n_cmp = (S - CMP_BLOCK) // CMP_STRIDE + 1
    cmp_start = jnp.arange(n_cmp) * CMP_STRIDE
    cmp_end = cmp_start + CMP_BLOCK - 1
    cmp_idx = cmp_start[:, None] + jnp.arange(CMP_BLOCK)[None, :]

    def compress(tok, w1, w2):
        blk = tok[:, :, cmp_idx] + pos_emb
        blk = blk.reshape(B, G, n_cmp, CMP_BLOCK * dh)
        return jax.nn.gelu(blk @ w1) @ w2

    kc = _rope(compress(k_cmp, ck_w1, ck_w2), cmp_end, ROPE_DIM, ROPE_THETA)
    vc = compress(v_cmp, cv_w1, cv_w2)

    n_slc = S // SLC_BLOCK
    s_start = jnp.arange(n_slc) * SLC_BLOCK
    overlap = jnp.clip(jnp.minimum(cmp_start[:, None] + CMP_BLOCK, s_start[None, :] + SLC_BLOCK)
                       - jnp.maximum(cmp_start[:, None], s_start[None, :]), 0, None)
    cmp_to_slc = overlap.astype(jnp.float32) / CMP_BLOCK
    top_n = min(SLC_TOPN, n_slc)

    k_blocks = k_slc.reshape(B, G, n_slc, SLC_BLOCK, dh)
    v_blocks = v_slc.reshape(B, G, n_slc, SLC_BLOCK, dh)
    k_pad = jnp.pad(k_win, ((0, 0), (0, 0), (WINDOW, 0), (0, 0)))
    v_pad = jnp.pad(v_win, ((0, 0), (0, 0), (WINDOW, 0), (0, 0)))
    b_ix = jnp.arange(B)[:, None, None, None]
    g_ix = jnp.arange(G)[None, :, None, None]
    sb = jnp.arange(n_slc)

    def one_block(c):
        q0 = c * Q_BLOCK
        qc = lax.dynamic_slice_in_dim(q, q0, Q_BLOCK, axis=3)
        gc = lax.dynamic_slice_in_dim(gates, q0, Q_BLOCK, axis=3)
        t = q0 + jnp.arange(Q_BLOCK)

        s_c = jnp.einsum('bghqd,bgnd->bghqn', qc, kc) * scale
        p_c = _masked_softmax(s_c, cmp_end[None, :] <= t[:, None])
        o_c = jnp.einsum('bghqn,bgnd->bghqd', p_c.astype(vc.dtype), vc)

        imp = jnp.einsum('bghqn,ns->bgqs', p_c, cmp_to_slc)
        cur = t // SLC_BLOCK
        forced = (sb[None, :] == 0) | (sb[None, :] == cur[:, None]) | (sb[None, :] == cur[:, None] - 1)
        future = sb[None, :] > cur[:, None]
        imp = jnp.where(forced, FORCED_SCORE, jnp.where(future, -FORCED_SCORE, imp))
        _, sel = lax.top_k(imp, top_n)
        k_sel = k_blocks[b_ix, g_ix, sel]
        v_sel = v_blocks[b_ix, g_ix, sel]
        kpos = sel[..., None] * SLC_BLOCK + jnp.arange(SLC_BLOCK)
        s_s = jnp.einsum('bghqd,bgqnkd->bghqnk', qc, k_sel) * scale
        s_s = s_s.reshape(B, G, Hg, Q_BLOCK, top_n * SLC_BLOCK)
        mask_s = (kpos <= t[:, None, None]).reshape(B, G, 1, Q_BLOCK, top_n * SLC_BLOCK)
        p_s = _masked_softmax(s_s, mask_s).reshape(B, G, Hg, Q_BLOCK, top_n, SLC_BLOCK)
        o_s = jnp.einsum('bghqnk,bgqnkd->bghqd', p_s.astype(v_sel.dtype), v_sel)

        kw = lax.dynamic_slice_in_dim(k_pad, q0, WINDOW + Q_BLOCK, axis=2)
        vw = lax.dynamic_slice_in_dim(v_pad, q0, WINDOW + Q_BLOCK, axis=2)
        wpos = q0 - WINDOW + jnp.arange(WINDOW + Q_BLOCK)
        dist = t[:, None] - wpos[None, :]
        mask_w = (wpos[None, :] >= 0) & (dist >= 0) & (dist < WINDOW)
        s_w = jnp.einsum('bghqd,bgkd->bghqk', qc, kw) * scale
        p_w = _masked_softmax(s_w, mask_w)
        o_w = jnp.einsum('bghqk,bgkd->bghqd', p_w.astype(vw.dtype), vw)

        return gc[..., 0:1] * o_c + gc[..., 1:2] * o_s + gc[..., 2:3] * o_w

    out = lax.map(one_block, jnp.arange(S // Q_BLOCK))
    return out.transpose(1, 0, 4, 2, 3, 5).reshape(B, S, G * Hg * dh)

def _retention(q, k, v, gn_gain):
    B, H, S, dk = q.shape
    dv = v.shape[-1]
    C = RET_CHUNK
    N = S // C
    dt = q.dtype
    pos = jnp.arange(S)
    q = _rope(q, pos, dk, RET_ROPE_THETA) * (dk ** -0.5)
    k = _rope(k, pos, dk, RET_ROPE_THETA)
    log_g = jnp.log(1.0 - 2.0 ** (-5.0 - jnp.arange(H, dtype=jnp.float32)))
    i = jnp.arange(C, dtype=jnp.float32)
    diff = i[:, None] - i[None, :]
    decay = jnp.where(diff >= 0, jnp.exp(jnp.maximum(diff, 0.0) * log_g[:, None, None]), 0.0)
    zeta = jnp.exp((C - 1.0 - i)[None, :] * log_g[:, None])
    xi = jnp.exp((i + 1.0)[None, :] * log_g[:, None])
    g_chunk = jnp.exp(C * log_g)

    qc = q.reshape(B, H, N, C, dk)
    kc = k.reshape(B, H, N, C, dk)
    vc = v.reshape(B, H, N, C, dv)
    inner = jnp.einsum('bhncd,bhnkd->bhnck', qc, kc) * decay[None, :, None].astype(dt)
    o_inner = jnp.einsum('bhnck,bhnke->bhnce', inner, vc)
    kv = jnp.einsum('bhncd,bhnce->nbhde', kc * zeta[None, :, None, :, None].astype(dt), vc)
    kv = kv.astype(jnp.float32)

    def step(R, kv_n):
        return g_chunk[None, :, None, None] * R + kv_n, R

    _, R_prev = lax.scan(step, jnp.zeros((B, H, dk, dv), jnp.float32), kv)
    o_cross = jnp.einsum('bhncd,nbhde->bhnce',
                         (qc * xi[None, :, None, :, None].astype(dt)).astype(jnp.float32), R_prev)
    o = (o_inner.astype(jnp.float32) + o_cross).reshape(B, H, S, dv)
    mu = jnp.mean(o, axis=-1, keepdims=True)
    var = jnp.mean(jnp.square(o - mu), axis=-1, keepdims=True)
    on = (o - mu) * lax.rsqrt(var + GN_EPS) * gn_gain.astype(jnp.float32)[None, :, None, :]
    return on.astype(dt).transpose(0, 2, 1, 3).reshape(B, S, H * dv)

def second_inputs(seed: int = 0) -> dict:
    key = jax.random.key(seed)
    ks = jax.random.split(key, 24)
    f32 = jnp.float32

    def w(k, shape, fan_in):
        return jax.random.normal(k, shape, f32) * (fan_in ** -0.5)

    def gain(k, shape):
        return 1.0 + 0.02 * jax.random.normal(k, shape, f32)

    L = DEPTH
    return {
        "x": jax.random.normal(ks[0], (BATCH, SEQ, D_MODEL), f32),
        "ffn1_norm": gain(ks[1], (L, D_MODEL)),
        "ffn1_w_gate": w(ks[2], (L, D_MODEL, D_FF), D_MODEL),
        "ffn1_w_up": w(ks[3], (L, D_MODEL, D_FF), D_MODEL),
        "ffn1_w_down": w(ks[4], (L, D_FF, D_MODEL), D_FF),
        "mix_norm": gain(ks[5], (L, D_MODEL)),
        "w_in": w(ks[6], (L, D_MODEL, D_IN), D_MODEL),
        "cmp_pos_emb": 0.1 * jax.random.normal(ks[7], (L, CMP_BLOCK, NSA_HEAD_DIM), f32),
        "cmp_k_w1": w(ks[8], (L, CMP_BLOCK * NSA_HEAD_DIM, CMP_HIDDEN), CMP_BLOCK * NSA_HEAD_DIM),
        "cmp_k_w2": w(ks[9], (L, CMP_HIDDEN, NSA_HEAD_DIM), CMP_HIDDEN),
        "cmp_v_w1": w(ks[10], (L, CMP_BLOCK * NSA_HEAD_DIM, CMP_HIDDEN), CMP_BLOCK * NSA_HEAD_DIM),
        "cmp_v_w2": w(ks[11], (L, CMP_HIDDEN, NSA_HEAD_DIM), CMP_HIDDEN),
        "ret_gn_gain": gain(ks[12], (L, RET_HEADS, RET_VAL_DIM)),
        "w_branch_nsa": w(ks[13], (L, NSA_Q_W, D_MODEL), NSA_Q_W),
        "w_branch_ret": w(ks[14], (L, RET_V_W, D_MODEL), RET_V_W),
        "w_out": w(ks[15], (L, D_MODEL, D_MODEL), D_MODEL),
        "ffn2_norm": gain(ks[16], (L, D_MODEL)),
        "ffn2_w_gate": w(ks[17], (L, D_MODEL, D_FF), D_MODEL),
        "ffn2_w_up": w(ks[18], (L, D_MODEL, D_FF), D_MODEL),
        "ffn2_w_down": w(ks[19], (L, D_FF, D_MODEL), D_FF),
        "final_norm": gain(ks[20], (D_MODEL,)),
    }

def second_block(x, ffn1_norm, ffn1_w_gate, ffn1_w_up, ffn1_w_down, mix_norm, w_in,
              cmp_pos_emb, cmp_k_w1, cmp_k_w2, cmp_v_w1, cmp_v_w2, ret_gn_gain,
              w_branch_nsa, w_branch_ret, w_out, ffn2_norm, ffn2_w_gate, ffn2_w_up,
              ffn2_w_down, final_norm):
    B, S, _ = x.shape
    G, Hg, dh = NSA_KV_GROUPS, NSA_HEADS_PER_GROUP, NSA_HEAD_DIM
    split_points = [int(p) for p in np.cumsum(IN_WIDTHS)[:-1]]

    def nsa_heads(t):
        return t.reshape(B, S, G, Hg, dh).transpose(0, 2, 3, 1, 4)

    def nsa_kv(t):
        return t.reshape(B, S, G, dh).transpose(0, 2, 1, 3)

    def ret_heads(t, d):
        return t.reshape(B, S, RET_HEADS, d).transpose(0, 2, 1, 3)

    for layer in range(DEPTH):
        h = _rmsnorm(x, ffn1_norm[layer])
        x = x + 0.5 * _swiglu(h, ffn1_w_gate[layer], ffn1_w_up[layer], ffn1_w_down[layer])

        h = _rmsnorm(x, mix_norm[layer])
        proj = h @ w_in[layer]
        (q_a, kc_a, vc_a, ks_a, vs_a, kw_a, vw_a, g_a,
         q_r, k_r, v_r, g_r, g_merge) = jnp.split(proj, split_points, axis=-1)

        nsa_gates = jax.nn.sigmoid(g_a.reshape(B, S, G, Hg, 3).transpose(0, 2, 3, 1, 4))
        a_out = _nsa(nsa_heads(q_a), nsa_kv(kc_a), nsa_kv(vc_a), nsa_kv(ks_a), nsa_kv(vs_a),
                     nsa_kv(kw_a), nsa_kv(vw_a), nsa_gates, cmp_pos_emb[layer],
                     cmp_k_w1[layer], cmp_k_w2[layer], cmp_v_w1[layer], cmp_v_w2[layer])
        r_out = _retention(ret_heads(q_r, RET_KEY_DIM), ret_heads(k_r, RET_KEY_DIM),
                           ret_heads(v_r, RET_VAL_DIM), ret_gn_gain[layer])
        r_out = jax.nn.silu(g_r) * r_out

        gate_a, gate_r = jnp.split(jax.nn.sigmoid(g_merge), 2, axis=-1)
        mixed = gate_a * (a_out @ w_branch_nsa[layer]) + gate_r * (r_out @ w_branch_ret[layer])
        x = x + mixed @ w_out[layer]

        h = _rmsnorm(x, ffn2_norm[layer])
        x = x + 0.5 * _swiglu(h, ffn2_w_gate[layer], ffn2_w_up[layer], ffn2_w_down[layer])

    return _rmsnorm(x, final_norm)


def setup_inputs(seed=0):
    out = dict(first_inputs(seed))
    for name, value in second_inputs(seed + 1).items():
        if name != "x":
            out[name + "_2"] = value
    return out


def reference(
    x, positions, norm_mix_g, w_in, b_forget, q_a_norm_g, w_q_up, kv_a_norm_g, w_kv_up,
    w_branch_a, w_branch_b, b_gate, w_out, norm_ffn_g, w_ffn_gate, w_ffn_up, w_ffn_down,
    norm_final_g, ffn1_norm_2, ffn1_w_gate_2, ffn1_w_up_2, ffn1_w_down_2, mix_norm_2, w_in_2,
    cmp_pos_emb_2, cmp_k_w1_2, cmp_k_w2_2, cmp_v_w1_2, cmp_v_w2_2, ret_gn_gain_2,
    w_branch_nsa_2, w_branch_ret_2, w_out_2, ffn2_norm_2, ffn2_w_gate_2, ffn2_w_up_2,
    ffn2_w_down_2, final_norm_2,
):
    x = first_block(
        x, positions, norm_mix_g, w_in, b_forget, q_a_norm_g, w_q_up, kv_a_norm_g, w_kv_up,
        w_branch_a, w_branch_b, b_gate, w_out, norm_ffn_g, w_ffn_gate, w_ffn_up, w_ffn_down,
        norm_final_g,
    )
    return second_block(
        x, ffn1_norm_2, ffn1_w_gate_2, ffn1_w_up_2, ffn1_w_down_2, mix_norm_2, w_in_2,
        cmp_pos_emb_2, cmp_k_w1_2, cmp_k_w2_2, cmp_v_w1_2, cmp_v_w2_2, ret_gn_gain_2,
        w_branch_nsa_2, w_branch_ret_2, w_out_2, ffn2_norm_2, ffn2_w_gate_2, ffn2_w_up_2,
        ffn2_w_down_2, final_norm_2,
    )


_drawn_inputs = setup_inputs


def setup_inputs(seed=0):
    import zlib

    import numpy as np

    out = dict(_drawn_inputs(seed))
    spreads = {}
    factors = {'q_a_norm_g': 8.0,
     'kv_a_norm_g': 6.924,
     'b_gate': 8.0,
     'ffn1_norm_2': 5.867,
     'mix_norm_2': 4.389,
     'cmp_pos_emb_2': 52.201,
     'ret_gn_gain_2': 23.613,
     'ffn2_norm_2': 20.52,
     'final_norm_2': 22.416}
    for name, (base, spread) in spreads.items():
        noise = np.random.default_rng([zlib.crc32(name.encode()), seed]).standard_normal(out[name].shape)
        drawn = base * np.exp(spread * noise) if base else spread * noise
        out[name] = __import__('jax').numpy.asarray(drawn.astype(out[name].dtype))
    for name, factor in factors.items():
        out[name] = (out[name] * factor).astype(out[name].dtype)
    return out
```

```python
from contextlib import ExitStack

import numpy as np

import concourse.bass as bass
from concourse import mybir

P = 128
D = 1024
S = 512
KT = D // P
TB = S // P
FF = 2816
FT = FF // P
RING = 4
LOOKAHEAD = 2
CW = KT * P
EPS = 1e-6
GN_EPS = 1e-5
OFF = [P * (b * (b + 1) // 2) for b in range(TB + 1)]
KOFF = [sum(S - P * j for j in range(b)) for b in range(TB + 1)]
ALU = mybir.AluOpType
ACT = mybir.ActivationFunctionType
AX = mybir.AxisListType
F32 = mybir.dt.float32
F32R = mybir.dt.float32r
I32 = mybir.dt.int32

TWO_PI = [6.28125, 0.00193023681640625, 5.0703634e-06, 2 * np.pi]
MAGIC = 12582912.0
PI_BELOW = 3.1415925
HALF_PI = float(np.float32(np.pi / 2))
SWAP16 = [(n + 16) % 32 for n in range(32)]
SWAP8 = [n + 8 if n < 8 else n - 8 if n < 16 else n for n in range(32)]

STAGES = [
    ("b1_qk", 8), ("b1_v", 4), ("b1_fk", 1), ("b1_c", 3), ("b1_up", 4),
    ("b1_merge", 24), ("b1_out", 8), ("f0_in", 2 * FT), ("f0_down", FT),
    ("f1_in", 2 * FT), ("f1_down", FT),
    ("b2_qk", 12), ("b2_cmp", 4), ("b2_v", 2), ("b2_g", 1), ("b2_w1", 8), ("b2_rqk", 8), ("b2_rv", 8),
    ("b2_gr", 8), ("b2_merge", 32), ("b2_out", 8), ("f2_in", 2 * FT), ("f2_down", FT),
]
FIRST = {}
_n = 0
for _name, _count in STAGES:
    FIRST[_name] = _n
    _n += _count
CHUNKS = _n

COLS = {}
_n = 0
for _name, _count in [("mix1", 8), ("qa", 2), ("kva", 1), ("bgate", 16), ("ffn0", 8), ("fin1", 8), ("ffn1", 8),
                      ("mix2", 8), ("ret", 8), ("ffn2", 8), ("fin2", 8), ("freq", 1), ("pos", 16), ("bf", 8),
                      ("sgn", 1), ("eps", 1),
                      ("one", 1), ("gneps", 1)]:
    COLS[_name] = _n
    _n += _count
NCOLS = _n


def build_program(nc, stream, xt, cols, tables, rows, decays, pos, w2, out):
    top = ExitStack()
    with top:
        origin = -(-nc.sbuf_base // 32) * 32
        top.enter_context(nc.sbuf_tensor("arena", [P, (nc.sbuf_top - nc.sbuf_base) // 4 - 16], F32))

        def sb(name, shape, dt, at):
            assert origin + at + 4 * int(np.prod(shape[1:])) <= nc.sbuf_usable_end, name
            return nc.alloc_sbuf_tensor_at(name, shape, dt, offset=origin + at)

        def sem(name):
            return top.enter_context(nc.semaphore(name))

        K = 1024
        T2 = 2 * K
        w_raw = sb("w_raw", [P, 2, CW], F32, 0)
        w_hi = sb("w_hi", [P, RING, CW], F32R, 8 * K)
        w_lo = sb("w_lo", [P, RING, CW], F32R, 24 * K)
        x = sb("x", [P, KT, S], F32, 40 * K)
        xn_hi = sb("xn_hi", [P, KT, S], F32R, 56 * K)
        xn_lo = sb("xn_lo", [P, KT, S], F32R, 72 * K)
        ident = sb("ident", [P, P], F32, 88 * K)
        ones = sb("ones", [P, P], F32, 88 * K + 512)
        col = sb("col", [P, P], F32, 89 * K)
        cumul = sb("cumul", [P, S], F32R, 90 * K)
        bias_tri = sb("bias_tri", [P, S], F32, 92 * K)
        bias_chunk = sb("bias_chunk", [P, S], F32, 94 * K)
        norm_r = sb("norm_r", [P, S], F32, 96 * K)
        small = sb("small", [P, 128], F32, 98 * K)
        w2_sb = sb("w2_sb", [P, 4, P], F32, 99 * K)
        A0 = 101 * K
        N0 = 199 * K
        cumul_raw = sb("cumul_raw", [P, S], F32, 195 * K)
        sq = sb("sq", [P, 2, S], F32, N0)
        xg = sb("xg", [P, 2, S], F32, N0 + 4 * K)
        h_hi = sb("h_hi", [P, FT * S], F32R, A0)
        h_lo = sb("h_lo", [P, FT * S], F32R, A0 + 44 * K)
        silu = sb("silu", [P, 2, S], F32, A0 + 88 * K)
        hid = sb("hid", [P, 2, S], F32, A0 + 92 * K)

        banks = [top.enter_context(nc.psum_tensor(f"bank{b}", [P, S], F32)) for b in range(8)]

        loaded = [sem("w_loaded0"), sem("w_loaded1")]
        split_hi = sem("w_split_hi")
        split_lo = sem("w_split_lo")
        used = sem("chunks_used")
        consts_in = sem("consts_in")
        consts_made = sem("consts_made")
        x_in = sem("x_in")
        passed = sem("passed")
        stored = sem("stored")

        def place(first, j, i=0, n=0):
            c = first + j
            return c // RING + i * (n // RING), c % RING

        def high_part(act, ring, slot):
            act.wait_ge(loaded[slot % 2], 32 * ring + 16 * (slot // 2 + 1))
            act.wait_ge(used, RING * ring + (slot + 1))
            nc.scalar.activation(w_hi[:, slot, :], w_raw[:, slot % 2, :], ACT.Copy).then_inc(split_hi, 1)

        def low_part(dve, ring, slot):
            dve.wait_ge(split_hi, RING * ring + (slot + 1))
            nc.vector.tensor_tensor(w_lo[:, slot, :], w_raw[:, slot % 2, :], w_hi[:, slot, :],
                                    ALU.subtract).then_inc(split_lo, 1)

        def ahead(part, eng, first, j, i=0, n=0):
            if n or first + j + LOOKAHEAD < CHUNKS:
                part(eng, *place(first, j + LOOKAHEAD, i, n))

        def apart(eng):
            eng.sem_inc(passed, 1)

        def finished(eng, first, j, i=0, n=0):
            ring, slot = place(first, j, i, n)
            eng.wait_ge(used, RING * ring + (slot + 1 + RING))

        def ready(pe, first, j, i=0, n=0):
            ring, slot = place(first, j, i, n)
            pe.wait_ge(split_lo, RING * ring + (slot + 1))
            return slot

        def mm3(to, a_hi, a_lo, b_hi, b_lo, start=True, stop=True):
            nc.tensor.matmul(to, a_hi, b_hi, start=start, stop=False, skip_group_check=True)
            nc.tensor.matmul(to, a_hi, b_lo, start=False, stop=False, skip_group_check=True)
            return nc.tensor.matmul(to, a_lo, b_hi, start=False, stop=stop, skip_group_check=True)

        def tile_chunk(slot, to, b_hi, b_lo, at=0, tiles=KT):
            for k in range(tiles):
                last = mm3(to, w_hi[:, slot, (at + k) * P:(at + k + 1) * P], w_lo[:, slot, (at + k) * P:(at + k + 1) * P],
                           b_hi[:, k, :], b_lo[:, k, :], k == 0, k == tiles - 1)
            return last

        norm_sems = {k: sem(f"norm_{k}") for k in ("squared", "summed", "root", "recip", "scaled", "hi", "lo")}
        norms = {"tiles": 0, "split": 0, "count": 0}

        def norm(name, src, order, gain, source_done, bank, width, dst=None, dma=False):
            s = norm_sems
            count = len(order)
            tiles, parts_made, before = norms["tiles"], norms["split"], norms["count"]
            norms["tiles"] += count
            norms["split"] += count if dst else 0
            norms["count"] += 1

            def act_part(act):
                for n, k in enumerate(order):
                    act.wait_ge(source_done[0], source_done[1] + (0 if dma else n))
                    if n >= 2:
                        act.wait_ge(s["summed"], tiles + n - 1)
                    nc.scalar.activation(sq[:, n % 2, :], src[:, k, :], ACT.Square).then_inc(s["squared"], 1)
                act.wait_ge(s["summed"], tiles + count)
                nc.scalar.activation(norm_r[:], banks[bank][:], ACT.Sqrt, bias=col[:, COLS["eps"]:COLS["eps"] + 1],
                                     scale=1.0 / width).then_inc(s["root"], 1)
                if dst:
                    for n, k in enumerate(order):
                        act.wait_ge(s["scaled"], tiles + n + 1)
                        nc.scalar.activation(dst[0][:, k, :], xg[:, n % 2, :], ACT.Copy).then_inc(s["hi"], 1)

            def pe_part(pe):
                for n in range(count):
                    pe.wait_ge(s["squared"], tiles + n + 1)
                    nc.tensor.matmul(banks[bank][:], ones[:], sq[:, n % 2, :], start=n == 0,
                                     stop=n == count - 1).then_inc(s["summed"], 1)

            def dve_part(dve):
                dve.wait_ge(s["root"], before + 1)
                nc.vector.reciprocal(norm_r[:], norm_r[:]).then_inc(s["recip"], 1)
                dve.wait_ge(s["recip"], before + 1)
                for n, k in enumerate(order):
                    if dst and n >= 2:
                        dve.wait_ge(s["lo"], parts_made + n - 1)
                    to = xg[:, n % 2, :] if dst else src[:, k, :]
                    nc.vector.scalar_tensor_tensor(to, src[:, k, :], col[:, gain + k:gain + k + 1], norm_r[:],
                                                   ALU.mult, ALU.mult).then_inc(s["scaled"], 1)

            def pool_part(pool):
                if dst:
                    for n, k in enumerate(order):
                        pool.wait_ge(s["hi"], parts_made + n + 1)
                        nc.gpsimd.tensor_tensor(dst[1][:, k, :], xg[:, n % 2, :], dst[0][:, k, :],
                                                ALU.subtract).then_inc(s["lo"], 1)

            done = (s["lo"], parts_made + count) if dst else (s["scaled"], tiles + count)
            return act_part, pe_part, dve_part, pool_part, done

        ORDER = [7, 0, 1, 2, 3, 4, 5, 6]

        ffn_sems = {k: sem(f"ffn_{k}") for k in ("silu", "product", "hi", "lo", "x")}
        ffns = [0]

        def feed_forward(name, factor, norm_done):
            first_in, first_down = FIRST[f"{name}_in"], FIRST[f"{name}_down"]
            s = ffn_sems
            first_one, b = ffns[0] == 0, FT * ffns[0]
            x_before = KT * ffns[0]
            ffns[0] += 1
            N_IN, N_DOWN = 4, 4

            def pe_part(pe):
                pe.wait_ge(*norm_done)
                with pe.Fori(0, FT // 2) as i:
                    for j in range(4):
                        slot = ready(pe, first_in, j, i, N_IN)
                        if j % 2 == 0:
                            pe.wait_ge(s["product"], 2 * i + (b + j // 2 + 1))
                        tile_chunk(slot, banks[j][:], xn_hi, xn_lo).then_inc(used, 1)

                def down(j, k, start, stop, i=0, n=0):
                    pe.wait_ge(s["lo"], k + (b + 3))
                    slot = ready(pe, first_down, j, i, n)
                    for o in (4, 5, 6, 7, 0, 1, 2, 3):
                        w = slice(o * P, (o + 1) * P)
                        last = mm3(banks[o][:], w_hi[:, slot, w], w_lo[:, slot, w], h_hi[:, bass.ds(k * S, S)],
                                   h_lo[:, bass.ds(k * S, S)], start, stop)
                    last.then_inc(used, 1)

                pe.wait_ge(s["product"], b + FT + 2)
                for j in range(4):
                    down(j, j, j == 0, False)
                with pe.Fori(0, FT // 4 - 1) as i:
                    for j in range(4):
                        down(j + 4, i * 4 + (j + 4), False, False, i, N_DOWN)
                for j in range(FT // 4 * 4, FT):
                    down(j, j, False, j == FT - 1)

            def act_part(act):
                with act.Fori(0, FT // 2) as i:
                    for t in range(2):
                        ahead(high_part, act, first_in, 2 * t, i, N_IN)
                        finished(act, first_in, 2 * t, i, N_IN)
                        act.wait_ge(s["product"], 2 * i + (b + t + 1))
                        nc.scalar.activation(silu[:, t, :], banks[2 * t][:], ACT.Silu).then_inc(s["silu"], 1)
                        ahead(high_part, act, first_in, 2 * t + 1, i, N_IN)
                        act.wait_ge(s["product"], 2 * i + (b + t + 3))
                        nc.scalar.activation(h_hi[:, bass.ds(i * 2 * S + t * S, S)], hid[:, t, :],
                                             ACT.Copy).then_inc(s["hi"], 1)
                stream_down(act, high_part)

            def stream_down(eng, part):
                with eng.Fori(0, FT // 4) as i:
                    for j in range(4):
                        ahead(part, eng, first_down, j, i, N_DOWN)
                for j in range(FT // 4 * 4, FT):
                    ahead(part, eng, first_down, j)

            def dve_part(dve):
                if first_one:
                    dve.sem_inc(s["product"], 2)
                with dve.Fori(0, FT // 2) as i:
                    for t in range(2):
                        ahead(low_part, dve, first_in, 2 * t, i, N_IN)
                        ahead(low_part, dve, first_in, 2 * t + 1, i, N_IN)
                        dve.wait_ge(s["silu"], 2 * i + (b + t + 1))
                        dve.wait_ge(s["lo"], 2 * i + (b + t + 1))
                        finished(dve, first_in, 2 * t + 1, i, N_IN)
                        nc.vector.tensor_tensor(hid[:, t, :], silu[:, t, :], banks[2 * t + 1][:],
                                                ALU.mult).then_inc(s["product"], 1)
                stream_down(dve, low_part)
                finished(dve, first_down, FT - 1)
                for k in ORDER:
                    nc.vector.scalar_tensor_tensor(x[:, k, :], banks[k][:], factor, x[:, k, :],
                                                   ALU.mult, ALU.add).then_inc(s["x"], 1)

            def pool_part(pool):
                if first_one:
                    pool.sem_inc(s["lo"], 2)
                with pool.Fori(0, FT // 2) as i:
                    for t in range(2):
                        pool.wait_ge(s["hi"], 2 * i + (b + t + 1))
                        nc.gpsimd.tensor_tensor(h_lo[:, bass.ds(i * 2 * S + t * S, S)], hid[:, t, :],
                                                h_hi[:, bass.ds(i * 2 * S + t * S, S)],
                                                ALU.subtract).then_inc(s["lo"], 1)

            return act_part, pe_part, dve_part, pool_part, (s["x"], x_before + 1)

        parts = []

        def link(eng, s):
            count = [0]

            def step(instruction):
                instruction.then_inc(s, 1)
                count[0] += 1
                eng.wait_ge(s, count[0])
            return step

        def skip(eng):
            pass

        W0 = A0 + 68 * K
        qs_hi = sb("qs_hi", [P, S], F32R, W0)
        qs_lo = sb("qs_lo", [P, S], F32R, W0 + T2)
        ks_hi = sb("ks_hi", [P, S], F32R, W0 + 2 * T2)
        ks_lo = sb("ks_lo", [P, S], F32R, W0 + 3 * T2)
        vs_hi = sb("vs_hi", [P, TB, P], F32R, W0 + 4 * T2)
        vs_lo = sb("vs_lo", [P, TB, P], F32R, W0 + 5 * T2)
        prob = sb("prob", [P, 2, OFF[TB]], F32, W0 + 6 * T2)
        pt_hi = sb("pt_hi", [P, OFF[TB]], F32R, W0 + 22 * K)
        pt_lo = sb("pt_lo", [P, OFF[TB]], F32R, W0 + 27 * K)
        bias_a = sb("bias_a", [P, OFF[TB]], F32, W0 + 32 * K)
        top_s, neg_top, total, inverse = (small[:, 8 * n:8 * n + 8] for n in range(4))

        def scores_rows(qb):
            return slice(OFF[qb], OFF[qb + 1])

        def attention(name, start, q_raw, k_raw, v_raw, y, y_tile, scale, latent):
            s = {k: sem(f"{name}_{k}") for k in ("staged_hi", "staged_lo", "v_hi", "v_lo", "scored", "biased", "negated",
                                                 "exp", "inverse", "scaled", "turned", "hi", "lo", "summed", "out",
                                                 "bias")}
            rows = [slice(0, P)] * 2 if latent else [slice(0, 64), slice(64, P)]
            krows = slice(0, 64) if latent else slice(0, P)
            pairs = 4

            def begin(eng):
                for w in start:
                    eng.wait_ge(*w)

            def pe_part(pe):
                begin(pe)
                pe.sem_inc(s["scored"], 4)
                pe.sem_inc(s["turned"], 8)
                pe.sem_inc(s["summed"], 4)
                with pe.Fori(0, pairs) as i:
                    def score(j):
                        if latent:
                            pe.wait_ge(s["staged_lo"], 4 * i + 2 * (j + 1))
                        elif j == 0:
                            pe.wait_ge(s["staged_lo"], 2 * i + 2)
                        for qb in range(TB):
                            pe.wait_ge(s["biased"], 8 * i + (4 * j + qb + 1))
                            at, n = slice(qb * P, (qb + 1) * P), (qb + 1) * P
                            mm3(banks[qb][:, 0:n], qs_hi[rows[j], at], qs_lo[rows[j], at], ks_hi[rows[j], 0:n],
                                ks_lo[rows[j], 0:n]).then_inc(s["scored"], 1)

                    def turn(j, kb):
                        if kb == 0:
                            pe.wait_ge(s["scaled"], 2 * i + (j + 1))
                        pe.wait_ge(s["lo"], 8 * i + (4 * j + kb + 1))
                        for qb in range(kb, TB):
                            last = nc.tensor.transpose(banks[4 + kb % 2][:, (qb - kb) * P:(qb - kb + 1) * P],
                                                       prob[:, j, OFF[qb] + kb * P:OFF[qb] + (kb + 1) * P], ident[:])
                        last.then_inc(s["turned"], 1)

                    def values(j, kb):
                        if kb == 0:
                            pe.wait_ge(s["out"], 2 * i + (j + 1))
                            pe.wait_ge(s["v_lo"], i + 1)
                        pe.wait_ge(s["lo"], 8 * i + (4 * j + kb + 3))
                        at = slice(KOFF[kb], KOFF[kb + 1])
                        mm3(banks[6 + j][:, kb * P:S], vs_hi[:, kb, :], vs_lo[:, kb, :], pt_hi[:, at], pt_lo[:, at],
                            kb == 0, kb == TB - 1).then_inc(s["summed"], 1)

                    score(0)
                    for j in range(2):
                        if j == 0:
                            score(1)
                        turn(j, 0)
                        for kb in range(1, TB):
                            turn(j, kb)
                            values(j, kb - 1)
                        values(j, TB - 1)

            def act_part(act):
                begin(act)
                act.sem_inc(s["out"], 2)
                with act.Fori(0, pairs) as i:
                    def stage(j):
                        tile = 2 * i + j if latent else i
                        act.wait_ge(s["scored"], 8 * i + (4 * j + 4))
                        nc.scalar.activation(qs_hi[:], q_raw[:, tile, :], ACT.Copy).then_inc(s["staged_hi"], 1)
                        nc.scalar.activation(ks_hi[krows, :], k_raw[krows, tile, :],
                                             ACT.Copy).then_inc(s["staged_hi"], 1)

                    def exps(j):
                        act.wait_ge(s["negated"], 2 * i + (j + 1))
                        for qb in range(TB):
                            at = prob[:, j, scores_rows(qb)]
                            n = 4 * j + qb
                            nc.scalar.activation(at, at, ACT.Exp, bias=neg_top[:, n:n + 1], scale=scale,
                                                 accum_out=total[:, n:n + 1]).then_inc(s["exp"], 1)

                    def highs(j):
                        for kb in range(TB):
                            act.wait_ge(s["turned"], 8 * i + (4 * j + kb + 9))
                            act.wait_ge(s["summed"], 8 * i + (4 * j + kb + 1))
                            nc.scalar.activation(pt_hi[:, KOFF[kb]:KOFF[kb + 1]], banks[4 + kb % 2][:, 0:S - kb * P],
                                                 ACT.Copy).then_inc(s["hi"], 1)

                    def output(j):
                        act.wait_ge(s["summed"], 8 * i + (4 * j + 8))
                        r = slice(64 * j, 64 * j + 64)
                        nc.scalar.activation(y[r, i + y_tile, :], banks[6 + j][r, :], ACT.Copy).then_inc(s["out"], 1)

                    stage(0)
                    act.wait_ge(s["summed"], 8 * i + 4)
                    nc.scalar.activation(vs_hi[:], v_raw[:, :, bass.ds(i * P, P)], ACT.Copy).then_inc(s["v_hi"], 1)
                    if latent:
                        stage(1)
                    exps(0)
                    exps(1)
                    highs(0)
                    output(0)
                    highs(1)
                    output(1)

            def dve_part(dve):
                begin(dve)
                dve.sem_inc(s["biased"], 4)
                dve.sem_inc(s["lo"], 2)
                with dve.Fori(0, pairs) as i:
                    def biased(j):
                        if not latent:
                            dve.wait_ge(s["bias"], 14 * i + 7 * (j + 1))
                        for qb in range(TB):
                            dve.wait_ge(s["scored"], 8 * i + (4 * j + qb + 5))
                            if qb == 0:
                                dve.wait_ge(s["turned"], 8 * i + (4 * j + 4))
                            apart(dve)
                            n = 4 * j + qb
                            width = (qb + 1) * P
                            bias = bias_chunk[:, S - width:S] if latent else bias_a[:, scores_rows(qb)]
                            nc.vector.tensor_tensor_reduce(prob[:, j, scores_rows(qb)], banks[qb][:, 0:width], bias, 1.0,
                                                           -3.0e38, ALU.add, ALU.max,
                                                           top_s[:, n:n + 1]).then_inc(s["biased"], 1)
                        dve.wait_ge(s["biased"], 8 * i + (4 * j + 8))
                        nc.vector.tensor_scalar(neg_top[:, 4 * j:4 * j + 4], top_s[:, 4 * j:4 * j + 4], -scale, None,
                                                ALU.mult).then_inc(s["negated"], 1)

                    def invert(j):
                        dve.wait_ge(s["exp"], 8 * i + (4 * j + 4))
                        nc.vector.reciprocal(inverse[:, 4 * j:4 * j + 4],
                                             total[:, 4 * j:4 * j + 4]).then_inc(s["inverse"], 1)

                    def lows(j):
                        for kb in range(TB):
                            dve.wait_ge(s["hi"], 8 * i + (4 * j + kb + 1))
                            at = slice(KOFF[kb], KOFF[kb + 1])
                            nc.vector.tensor_tensor(pt_lo[:, at], banks[4 + kb % 2][:, 0:S - kb * P], pt_hi[:, at],
                                                    ALU.subtract).then_inc(s["lo"], 1)

                    biased(0)
                    biased(1)
                    invert(0)
                    invert(1)
                    lows(0)
                    lows(1)

            def pool_part(pool):
                begin(pool)
                with pool.Fori(0, pairs) as i:
                    def stage(j, n):
                        tile = 2 * i + j if latent else i
                        pool.wait_ge(s["staged_hi"], 2 * n * i + (2 * j + 1))
                        nc.gpsimd.tensor_tensor(qs_lo[:], q_raw[:, tile, :], qs_hi[:], ALU.subtract).then_inc(s["staged_lo"], 1)
                        pool.wait_ge(s["staged_hi"], 2 * n * i + (2 * j + 2))
                        nc.gpsimd.tensor_tensor(ks_lo[krows, :], k_raw[krows, tile, :], ks_hi[krows, :],
                                                ALU.subtract).then_inc(s["staged_lo"], 1)

                    def bias(j):
                        pool.wait_ge(s["biased"], 8 * i + (4 * j + 4))
                        c = negc[:, 2 * i + j, :]
                        for qb in range(TB):
                            if qb:
                                nc.gpsimd.tensor_copy(bias_a[:, OFF[qb]:OFF[qb] + qb * P],
                                                      c[:, 0:qb * P]).then_inc(s["bias"], 1)
                            nc.gpsimd.tensor_tensor(bias_a[:, OFF[qb] + qb * P:OFF[qb + 1]], c[:, qb * P:(qb + 1) * P],
                                                    bias_tri[:, S - P:S], ALU.add).then_inc(s["bias"], 1)

                    def scaled(j):
                        pool.wait_ge(s["inverse"], 2 * i + (j + 1))
                        apart(pool)
                        for qb in range(TB):
                            at = prob[:, j, scores_rows(qb)]
                            n = 4 * j + qb
                            last = nc.gpsimd.tensor_scalar(at, at, inverse[:, n:n + 1], None, ALU.mult)
                        last.then_inc(s["scaled"], 1)

                    if not latent:
                        bias(0)
                    stage(0, 2 if latent else 1)
                    pool.wait_ge(s["v_hi"], i + 1)
                    nc.gpsimd.tensor_tensor(vs_lo[:], v_raw[:, :, bass.ds(i * P, P)], vs_hi[:],
                                            ALU.subtract).then_inc(s["v_lo"], 1)
                    if latent:
                        stage(1, 2)
                    else:
                        bias(1)
                    scaled(0)
                    scaled(1)

            return act_part, pe_part, dve_part, pool_part, (s["out"], 2 * pairs + 2)

        qk_raw = sb("qk_raw", [P, 2 * TB, S], F32, A0)
        v_raw = sb("v_raw", [P, TB, S], F32, A0 + 16 * K)
        negc = sb("negc", [P, 8, S], F32, A0 + 24 * K)
        mq = sb("mq", [P, 8, S], F32, A0)
        mk = sb("mk", [P, 8, S], F32, A0 + 16 * K)
        mv = sb("mv", [P, TB, S], F32, A0 + 32 * K)
        c_hi = sb("c_hi", [P, 3, S], F32R, A0 + 40 * K)
        c_lo = sb("c_lo", [P, 3, S], F32R, A0 + 46 * K)
        y1 = sb("y1", [P, KT, S], F32, A0 + 52 * K)
        forget = sb("forget", [8, 4, S], F32, W0)
        lft_hi = sb("lft_hi", [P, 32], F32R, W0 + 8 * K)
        lft_lo = sb("lft_lo", [P, 32], F32R, W0 + 9 * K)
        rope_c = sb("rope_c", [P, S], F32, W0 + 32 * K)
        rope_s = sb("rope_s", [P, S], F32, W0 + 34 * K)
        rope_t = sb("rope_t", [P, 4, S], F32, W0 + 14 * K)
        rope_i = sb("rope_i", [P, S], I32, W0 + 8 * K)
        rope_a = sb("rope_a", [P, S], F32, W0 + 10 * K)
        rope_k = sb("rope_k", [P, S], F32, W0 + 12 * K)

        def copies_out(name, first, count, dst, credit=True):
            s = sem(f"{name}_copied")

            def act_part(act):
                with act.Fori(0, count // 4) as i:
                    for j in range(4):
                        ahead(high_part, act, first, j, i, 4)

            def pe_part(pe):
                with pe.Fori(0, count // 4) as i:
                    for j in range(4):
                        slot = ready(pe, first, j, i, 4)
                        pe.wait_ge(s, 4 * i + (j + 1))
                        tile_chunk(slot, banks[j][:], xn_hi, xn_lo).then_inc(used, 1)

            def dve_part(dve):
                dve.sem_inc(s, 4)
                with dve.Fori(0, count // 4) as i:
                    for j in range(4):
                        ahead(low_part, dve, first, j, i, 4)
                        finished(dve, first, j, i, 4)
                        nc.vector.tensor_copy(dst[:, 4 * i + j, :], banks[j][:]).then_inc(s, 1)

            return act_part, pe_part, dve_part, skip, (s, count + 4)

        def mixer1(norm_done):
            qk = copies_out("b1_qk", FIRST["b1_qk"], 8, qk_raw)
            s = {k: sem(f"b1_{k}") for k in ("v", "fk", "c", "f_dve", "f_act", "lft_t", "lft_hi", "lft_lo", "cum",
                                             "negc")}
            cq = norm("b1_cq", y1, [0, 1], COLS["qa"], (s["c"], 1), 6, 256, (c_hi, c_lo))
            ckv = norm("b1_ckv", y1, [2], COLS["kva"] - 2, (s["c"], 3), 7, 128, (c_hi, c_lo))
            fv, ff, fc = FIRST["b1_v"], FIRST["b1_fk"], FIRST["b1_c"]

            def pe_part(pe):
                pe.wait_ge(*norm_done)
                qk[1](pe)
                for j in range(4):
                    slot = ready(pe, fv, j)
                    for t in range(2):
                        k, w = 2 * j + t, slice(t * S, (t + 1) * S)
                        for tb in range(TB):
                            at = slice(tb * P, (tb + 1) * P)
                            last = mm3(banks[4 + tb][:], xn_hi[:, k, at], xn_lo[:, k, at], w_hi[:, slot, w],
                                       w_lo[:, slot, w], k == 0, k == KT - 1)
                    last.then_inc(used, 1)
                slot = ready(pe, ff, 0)
                pe.wait_ge(qk[4][0], 8 + 1)
                tile_chunk(slot, banks[0][:], xn_hi, xn_lo).then_inc(used, 1)
                for j in range(3):
                    slot = ready(pe, fc, j)
                    pe.wait_ge(qk[4][0], 8 + 2 + j)
                    tile_chunk(slot, banks[1 + j][:], xn_hi, xn_lo).then_inc(used, 1)
                pe.wait_ge(s["f_dve"], 3)
                pe.wait_ge(s["v"], 4)
                for tb in range(TB):
                    last = nc.tensor.transpose(banks[4][:, 8 * tb:8 * tb + 8], forget[0:8, 0, tb * P:(tb + 1) * P],
                                               ident[0:8, 0:8])
                last.then_inc(s["lft_t"], 1)
                cq[1](pe)
                ckv[1](pe)
                pe.wait_ge(s["lft_lo"], 1)
                pe.wait_ge(s["c"], 3)
                pe.wait_ge(s["fk"], 1)
                for h in range(8):
                    if h >= 4:
                        pe.wait_ge(s["negc"], h - 3)
                    for tb in range(TB):
                        for n, part in enumerate((lft_hi, lft_lo)):
                            last = nc.tensor.matmul(banks[h % 4][:, tb * P:S],
                                                    part[:, 8 * tb + h:8 * tb + h + 1].to_broadcast([P, P]),
                                                    cumul[:, 0:S - tb * P], start=tb == 0 and n == 0,
                                                    stop=tb == TB - 1 and n == 1, skip_group_check=True)
                    last.then_inc(s["cum"], 1)

            def act_part(act):
                qk[0](act)
                for j in range(4):
                    ahead(high_part, act, fv, j)
                ahead(high_part, act, ff, 0)
                for j in range(3):
                    ahead(high_part, act, fc, j)
                act.wait_ge(s["f_dve"], 2)
                nc.scalar.activation(forget[0:8, 2, :], forget[0:8, 1, :], ACT.Exp).then_inc(s["f_act"], 1)
                act.wait_ge(s["f_act"], 1)
                nc.scalar.activation(forget[0:8, 3, :], forget[0:8, 2, :], ACT.Ln,
                                     bias=col[0:8, COLS["one"]:COLS["one"] + 1]).then_inc(s["f_act"], 1)
                act.wait_ge(s["lft_t"], 1)
                nc.scalar.activation(lft_hi[:], banks[4][:, 0:32], ACT.Copy).then_inc(s["lft_hi"], 1)
                cq[0](act)
                ckv[0](act)

            def dve_part(dve):
                qk[2](dve)
                for j in range(4):
                    ahead(low_part, dve, fv, j)
                finished(dve, fv, 3)
                for tb in range(TB):
                    nc.vector.tensor_copy(v_raw[:, tb, :], banks[4 + tb][:]).then_inc(s["v"], 1)
                ahead(low_part, dve, ff, 0)
                finished(dve, ff, 0)
                nc.vector.tensor_scalar(forget[0:8, 0, :], banks[0][0:8, :], col[0:8, COLS["bf"]:COLS["bf"] + 1], None,
                                        ALU.add).then_inc(s["f_dve"], 1)
                nc.vector.tensor_copy(y1[64:96, 7, :], banks[0][64:96, :]).then_inc(s["fk"], 1)
                dve.wait_ge(s["f_dve"], 1)
                nc.vector.scalar_tensor_tensor(forget[0:8, 1, :], forget[0:8, 0, :], -1.0, forget[0:8, 0, :], ALU.mult,
                                               ALU.min).then_inc(s["f_dve"], 1)
                for j in range(3):
                    ahead(low_part, dve, fc, j)
                    finished(dve, fc, j)
                    nc.vector.tensor_copy(y1[:, j, :], banks[1 + j][:]).then_inc(s["c"], 1)
                dve.wait_ge(s["f_act"], 2)
                nc.vector.scalar_tensor_tensor(forget[0:8, 0, :], forget[0:8, 0, :], 0.0, forget[0:8, 3, :], ALU.min,
                                               ALU.subtract).then_inc(s["f_dve"], 1)
                dve.wait_ge(s["lft_hi"], 1)
                nc.vector.tensor_tensor(lft_lo[:], banks[4][:, 0:32], lft_hi[:], ALU.subtract).then_inc(s["lft_lo"], 1)
                cq[2](dve)
                dve.wait_ge(*cq[4])
                ckv[2](dve)
                for h in range(8):
                    dve.wait_ge(s["cum"], h + 1)
                    nc.vector.tensor_copy(negc[:, h, :], banks[h % 4][:]).then_inc(s["negc"], 1)

            def pool_part(pool):
                cq[3](pool)
                ckv[3](pool)

            front = (act_part, pe_part, dve_part, pool_part)
            att = attention("b1_a", [(s["negc"], 8), (s["v"], 4), ckv[4], cq[4], qk[4]], qk_raw, qk_raw[:, 4:8, :],
                            v_raw, y1, 0, 0.125, False)

            fu = FIRST["b1_up"]
            u = {k: sem(f"b1_up_{k}") for k in ("copied", "v", "rope_dve", "rope_act", "rope_pool", "kr_hi", "ready",
                                                "pos")}

            def up_pe(pe):
                pe.wait_ge(*att[4])
                for j in range(4):
                    slot = ready(pe, fu, j)
                    if j < 3:
                        for n in range(4 if j < 2 else 8):
                            g = 4 * j + n
                            if g >= 4:
                                pe.wait_ge(u["copied"], g - 3)
                            if j < 2:
                                last = tile_chunk(slot, banks[g % 4][:], c_hi, c_lo, 2 * n, 2)
                            else:
                                w = slice(n * P, (n + 1) * P)
                                last = mm3(banks[g % 4][:], w_hi[:, slot, w], w_lo[:, slot, w], c_hi[:, 2, :],
                                           c_lo[:, 2, :])
                            last.then_inc(u["ready"] if n < (3 if j < 2 else 7) else used, 1)
                    else:
                        for tb in range(TB):
                            at = slice(tb * P, (tb + 1) * P)
                            last = mm3(banks[4 + tb][:], c_hi[:, 2, at], c_lo[:, 2, at], w_hi[:, slot, 0:S],
                                       w_lo[:, slot, 0:S])
                        last.then_inc(used, 1)

            def up_act(act):
                for j in range(4):
                    ahead(high_part, act, fu, j)
                act.wait_ge(u["rope_dve"], 8)
                nc.scalar.activation(rope_s[64:96, :], rope_a[64:96, :], ACT.Sin).then_inc(u["rope_act"], 1)
                act.wait_ge(u["rope_dve"], 10)
                nc.scalar.activation(rope_c[64:96, :], rope_k[64:96, :], ACT.Sin).then_inc(u["rope_act"], 1)
                act.wait_ge(u["rope_dve"], 14)
                nc.scalar.activation(ks_hi[64:96, :], y1[64:96, 7, :], ACT.Copy).then_inc(u["kr_hi"], 1)

            def up_dve(dve):
                dve.wait_ge(*att[4])
                r = slice(64, 96)
                c = [0]

                def step(instruction):
                    instruction.then_inc(u["rope_dve"], 1)
                    c[0] += 1
                    dve.wait_ge(u["rope_dve"], c[0])

                dve.wait_ge(u["pos"], 16)
                step(nc.vector.tensor_copy(rope_a[r, :], rope_i[r, :]))
                step(nc.vector.tensor_scalar(rope_a[r, :], rope_a[r, :], col[r, COLS["freq"]:COLS["freq"] + 1], None,
                                             ALU.mult))
                step(nc.vector.tensor_scalar(rope_k[r, :], rope_a[r, :], 1.0 / TWO_PI[3], MAGIC, ALU.mult, ALU.add))
                step(nc.vector.tensor_scalar(rope_k[r, :], rope_k[r, :], MAGIC, None, ALU.subtract))
                for part in TWO_PI[:3]:
                    step(nc.vector.scalar_tensor_tensor(rope_a[r, :], rope_k[r, :], -part, rope_a[r, :], ALU.mult,
                                                        ALU.add))
                step(nc.vector.tensor_scalar(rope_a[r, :], rope_a[r, :], -PI_BELOW, PI_BELOW, ALU.max, ALU.min))
                step(nc.vector.scalar_tensor_tensor(rope_k[r, :], rope_a[r, :], -1.0, rope_a[r, :], ALU.mult, ALU.max))
                step(nc.vector.tensor_scalar(rope_k[r, :], rope_k[r, :], -1.0, HALF_PI, ALU.mult, ALU.add))
                for j in range(3):
                    ahead(low_part, dve, fu, j)
                    for n in range(4 if j < 2 else 8):
                        g = 4 * j + n
                        if n < (3 if j < 2 else 7):
                            dve.wait_ge(u["ready"], g + 1 - j)
                        else:
                            finished(dve, fu, j)
                        to = mq[:, g, :] if g < 8 else mk[:, g - 8, :]
                        nc.vector.tensor_copy(to, banks[g % 4][:]).then_inc(u["copied"], 1)
                ahead(low_part, dve, fu, 3)
                finished(dve, fu, 3)
                for tb in range(TB):
                    nc.vector.tensor_copy(mv[:, tb, :], banks[4 + tb][:]).then_inc(u["v"], 1)
                dve.wait_ge(u["copied"], 16)
                dve.wait_ge(u["rope_act"], 2)
                step(nc.vector.tensor_scalar(rope_s[r, :], rope_s[r, :], col[r, COLS["sgn"]:COLS["sgn"] + 1], None,
                                             ALU.mult))
                step(nc.vector.stream_shuffle(rope_t[r, 0, :], y1[r, 7, :], SWAP16))
                nc.vector.tensor_tensor(rope_t[r, 0, :], rope_t[r, 0, :], rope_s[r, :], ALU.mult)
                step(nc.vector.tensor_tensor(y1[r, 7, :], y1[r, 7, :], rope_c[r, :], ALU.mult))
                step(nc.vector.tensor_tensor(y1[r, 7, :], y1[r, 7, :], rope_t[r, 0, :], ALU.add))
                dve.wait_ge(u["kr_hi"], 1)
                step(nc.vector.tensor_tensor(ks_lo[r, :], y1[r, 7, :], ks_hi[r, :], ALU.subtract))
                for b in range(2):
                    q = mq[r, 4 * b:4 * b + 4, :]
                    step(nc.vector.stream_shuffle(rope_t[r, :, :], q, SWAP16))
                    table = [t[r, :].rearrange("p (o s) -> p o s", o=1).to_broadcast([32, 4, S]) for t in (rope_c, rope_s)]
                    nc.vector.tensor_tensor(rope_t[r, :, :], rope_t[r, :, :], table[1], ALU.mult)
                    step(nc.vector.tensor_tensor(q, q, table[0], ALU.mult))
                    step(nc.vector.tensor_tensor(q, q, rope_t[r, :, :], ALU.add))

            def up_pool(pool):
                pool.wait_ge(*att[4])
                pool.dma_start(rope_i[64:96, :], pos.partition_broadcast(32)).then_inc(u["pos"], 16)
                nc.gpsimd.memset(ks_hi[96:P, :].bitcast(F32), 0.0).then_inc(u["rope_pool"], 1)
                nc.gpsimd.memset(ks_lo[96:P, :].bitcast(F32), 0.0).then_inc(u["rope_pool"], 1)

            up = (up_act, up_pe, up_dve, up_pool)
            lat = attention("b1_b", [(u["rope_dve"], 21), (u["copied"], 16), (u["v"], 4), (u["rope_pool"], 2)], mq, mk,
                            mv, y1, 4, 96.0 ** -0.5, True)
            return front, att, up, lat

        def merge(name, start, m_hi, m_lo, temps, branches, per, bias):
            s = {k: sem(f"{name}_merge_{k}") for k in ("y_hi", "y_lo", "gate", "gated", "sum", "hi", "lo", "x")}
            fm, fo = FIRST[f"{name}_merge"], FIRST[f"{name}_out"]
            turns = 4 if per == 3 else 2
            N = per * turns
            ny = sum(b[3].shape[1] for b in branches)

            def pe_part(pe):
                for w in start:
                    pe.wait_ge(*w)
                with pe.Fori(0, KT // turns) as i:
                    for t in range(turns):
                        base = 4 * (t % 2)
                        for g in range(2):
                            slot = ready(pe, fm, per * t + g, i, N)
                            if g == 0:
                                pe.wait_ge(s["gated"], 2 * turns * i + 2 * (t + 1))
                            tile_chunk(slot, banks[base + g][:], xn_hi, xn_lo).then_inc(used, 1)
                        pe.wait_ge(s["y_lo"], ny)
                        for chunk, at, bank, raw, y_hi, y_lo in branches:
                            tiles = raw.shape[1]
                            slot = ready(pe, fm, per * t + chunk, i, N)
                            last = tile_chunk(slot, banks[base + bank][:], y_hi, y_lo, at, tiles)
                            if at + tiles == KT:
                                last.then_inc(used, 1)
                with pe.Fori(0, 2) as i:
                    for j in range(4):
                        slot = ready(pe, fo, j, i, 4)
                        if j == 0:
                            pe.wait_ge(s["lo"], KT + 2)
                            pe.wait_ge(s["gated"], 2 * KT + 4)
                        pe.wait_ge(s["x"], 4 * i + (j + 1))
                        tile_chunk(slot, banks[j][:], m_hi, m_lo).then_inc(used, 1)

            def act_part(act):
                for w in start:
                    act.wait_ge(*w)
                for _, _, _, raw, y_hi, _ in branches:
                    for k in range(raw.shape[1]):
                        nc.scalar.activation(y_hi[:, k, :], raw[:, k, :], ACT.Copy).then_inc(s["y_hi"], 1)
                with act.Fori(0, KT // turns) as i:
                    for t in range(turns):
                        for g in range(2):
                            ahead(high_part, act, fm, per * t + g, i, N)
                            finished(act, fm, per * t + g, i, N)
                            act.wait_ge(s["lo"], turns * i + (t + 1))
                            if bias is None:
                                nc.scalar.activation(temps[:, t % 2, g, :], banks[4 * (t % 2) + g][:],
                                                     ACT.Sigmoid).then_inc(s["gate"], 1)
                            else:
                                nc.scalar.activation(temps[:, t % 2, g, :], banks[4 * (t % 2) + g][:], ACT.Sigmoid,
                                                     bias=col[:, bass.ds(i * turns + (bias + g * KT + t), 1)]
                                                     ).then_inc(s["gate"], 1)
                        for c in range(2, per):
                            ahead(high_part, act, fm, per * t + c, i, N)
                        act.wait_ge(s["sum"], turns * i + (t + 1))
                        nc.scalar.activation(m_hi[:, i * turns + t, :], temps[:, t % 2, 0, :],
                                             ACT.Copy).then_inc(s["hi"], 1)
                with act.Fori(0, 2) as i:
                    for j in range(4):
                        ahead(high_part, act, fo, j, i, 4)

            def dve_part(dve):
                for w in start:
                    dve.wait_ge(*w)
                dve.sem_inc(s["gated"], 4)
                tile = 0
                for _, _, _, raw, y_hi, y_lo in branches:
                    for k in range(raw.shape[1]):
                        tile += 1
                        dve.wait_ge(s["y_hi"], tile)
                        nc.vector.tensor_tensor(y_lo[:, k, :], raw[:, k, :], y_hi[:, k, :],
                                                ALU.subtract).then_inc(s["y_lo"], 1)
                with dve.Fori(0, KT // turns) as i:
                    for t in range(turns):
                        for c in range(per):
                            ahead(low_part, dve, fm, per * t + c, i, N)
                        dve.wait_ge(s["gate"], 2 * turns * i + 2 * (t + 1))
                        finished(dve, fm, per * t + per - 1, i, N)
                        for g in range(2):
                            nc.vector.tensor_tensor(temps[:, t % 2, g, :], temps[:, t % 2, g, :],
                                                    banks[4 * (t % 2) + 2 + g][:], ALU.mult).then_inc(s["gated"], 1)
                dve.sem_inc(s["x"], 4)
                with dve.Fori(0, 2) as i:
                    for j in range(4):
                        ahead(low_part, dve, fo, j, i, 4)
                        finished(dve, fo, j, i, 4)
                        nc.vector.tensor_tensor(x[:, 4 * i + j, :], x[:, 4 * i + j, :], banks[j][:],
                                                ALU.add).then_inc(s["x"], 1)

            def pool_part(pool):
                pool.sem_inc(s["lo"], 2)
                with pool.Fori(0, KT // turns) as i:
                    for t in range(turns):
                        pool.wait_ge(s["gated"], 2 * turns * i + 2 * (t + 1) + 4)
                        nc.gpsimd.tensor_tensor(temps[:, t % 2, 0, :], temps[:, t % 2, 0, :], temps[:, t % 2, 1, :],
                                                ALU.add).then_inc(s["sum"], 1)
                        pool.wait_ge(s["hi"], turns * i + (t + 1))
                        nc.gpsimd.tensor_tensor(m_lo[:, i * turns + t, :], temps[:, t % 2, 0, :],
                                                m_hi[:, i * turns + t, :], ALU.subtract).then_inc(s["lo"], 1)

            return act_part, pe_part, dve_part, pool_part, (s["x"], 5)

        y1_hi = sb("y1_hi", [P, KT, S], F32R, A0)
        y1_lo = sb("y1_lo", [P, KT, S], F32R, A0 + 52 * K)
        m1_hi = sb("m1_hi", [P, KT, S], F32R, A0 + 16 * K)
        m1_lo = sb("m1_lo", [P, KT, S], F32R, A0 + 32 * K)
        m1_temps = sb("m1_temps", [P, 2, 2, S], F32, W0)

        nsa_c = sb("nsa_c", [P, S], F32, A0)
        nsa_s = sb("nsa_s", [P, S], F32, A0 + 2 * K)
        ret_c = sb("ret_c", [P, S], F32, A0 + 4 * K)
        ret_s = sb("ret_s", [P, S], F32, A0 + 6 * K)
        cmp_c = sb("cmp_c", [P, 64], F32, A0 + 8 * K)
        cmp_s = sb("cmp_s", [P, 64], F32, A0 + 8 * K + 256)
        cmp_add = sb("cmp_add", [P, TB, 32], F32, A0 + 8 * K + 512)
        cmp_keep = sb("cmp_keep", [P, TB, 32], F32, A0 + 9 * K)
        gates = sb("gates", [P, TB, 48], F32, A0 + 10 * K)
        kc_hi = sb("kc_hi", [P, 32], F32R, A0 + 11 * K)
        kc_lo = sb("kc_lo", [P, 32], F32R, A0 + 11 * K + 256)
        vc_raw = sb("vc_raw", [P, 2, P], F32, A0 + 12 * K)
        vcs_hi = sb("vcs_hi", [P, P], F32R, A0 + 13 * K)
        vcs_lo = sb("vcs_lo", [P, P], F32R, A0 + 13 * K + 512)
        kc_raw = sb("kc_raw", [P, 64], F32, A0 + 14 * K)
        kc_sw = sb("kc_sw", [P, 64], F32, A0 + 14 * K + 256)
        hidden_k = sb("hidden_k", [P, 2, 64], F32, A0 + 15 * K)
        hidden_v = sb("hidden_v", [P, 2, 2, P], F32, A0 + 86 * K)
        a_raw = sb("a_raw", [P, KT, S], F32, A0 + 16 * K)
        nqk = sb("nqk", [P, 12, S], F32, A0 + 32 * K)
        nv = sb("nv", [P, TB, 256], F32, A0 + 56 * K)
        swapped = sb("swapped", [P, 2, S], F32, A0 + 80 * K)
        ck = sb("ck", [P, 4, S], F32, A0 + 60 * K)
        blk = sb("blk", [P, 16, 64], F32, A0 + 68 * K)
        blk_hi = sb("blk_hi", [P, 16, 64], F32R, A0 + 72 * K)
        blk_lo = sb("blk_lo", [P, 16, 64], F32R, A0 + 76 * K)
        gate_fm = sb("gate_fm", [P, S], F32, A0 + 84 * K)
        nq_hi = sb("nq_hi", [P, S], F32R, A0 + 60 * K)
        nq_lo = sb("nq_lo", [P, S], F32R, A0 + 62 * K)
        nk_hi = sb("nk_hi", [P, 2, S], F32R, A0 + 64 * K)
        nk_lo = sb("nk_lo", [P, 2, S], F32R, A0 + 68 * K)
        nvs_hi = sb("nvs_hi", [P, TB, 2, P], F32R, A0 + 72 * K)
        nvs_lo = sb("nvs_lo", [P, TB, 2, P], F32R, A0 + 76 * K)
        nprob = sb("nprob", [P, 2, OFF[TB]], F32, A0 + 80 * K)
        npt_hi = sb("npt_hi", [P, OFF[TB]], F32R, A0 + 90 * K)
        npt_lo = sb("npt_lo", [P, OFF[TB]], F32R, A0 + 95 * K)
        csc = sb("csc", [P, 2, TB, 32], F32, A0 + 100 * K)
        cpad = sb("cpad", [P, 2, TB * (P + 32)], F32, A0 + 101 * K)
        cpt_hi = sb("cpt_hi", [P, S], F32R, 90 * K)
        cpt_lo = sb("cpt_lo", [P, S], F32R, 94 * K)
        c_top, c_total, c_inverse, nguard = (small[:, 32 + 8 * n:40 + 8 * n] for n in range(4))
        r_qk = sb("r_qk", [P, KT, S], F32, A0 + 32 * K)
        r_v = sb("r_v", [P, TB, D], F32, A0 + 48 * K)
        r_raw = sb("r_raw", [P, KT, S], F32, A0 + 64 * K)
        r_swapped = sb("r_swapped", [P, 2, S], F32, A0 + 80 * K)
        rq_hi = sb("rq_hi", [P, S], F32R, A0 + 80 * K)
        rq_lo = sb("rq_lo", [P, S], F32R, A0 + 82 * K)
        rk_hi = sb("rk_hi", [P, S], F32R, A0 + 84 * K)
        rk_lo = sb("rk_lo", [P, S], F32R, A0 + 86 * K)
        rv_hi = sb("rv_hi", [P, TB, 2 * P], F32R, A0 + 88 * K)
        rv_lo = sb("rv_lo", [P, TB, 2 * P], F32R, A0 + 92 * K)
        decay = sb("decay", [P, 2, S], F32, A0 + 96 * K)
        weighted = sb("weighted", [P, 2, S], F32, A0 + 100 * K)
        ws_hi = sb("ws_hi", [P, 2, S], F32R, A0)
        ws_lo = sb("ws_lo", [P, 2, S], F32R, A0 + 4 * K)
        gn_sq = sb("gn_sq", [P, S], F32, A0 + 104 * K)
        gn_r = sb("gn_r", [P, S], F32, A0 + 8 * K)
        a_hi = sb("a_hi", [P, KT, S], F32R, A0 + 32 * K)
        a_lo = sb("a_lo", [P, KT, S], F32R, A0 + 16 * K)
        r_hi = sb("r_hi", [P, KT, S], F32R, A0 + 48 * K)
        r_lo = sb("r_lo", [P, KT, S], F32R, A0 + 64 * K)
        m2_hi = sb("m2_hi", [P, KT, S], F32R, A0 + 80 * K)
        m2_lo = sb("m2_lo", [P, KT, S], F32R, A0)
        m2_temps = sb("m2_temps", [P, 2, 2, S], F32, A0 + 96 * K)

        def roped_out(name, first, count, start, dst, sw, table_c, table_s, mask):
            s = {k: sem(f"{name}_{k}") for k in ("swapped", "out", "done")}

            def act_part(act):
                with act.Fori(0, count // 4) as i:
                    for j in range(4):
                        ahead(high_part, act, first, j, i, 4)

            def pe_part(pe):
                for w in start:
                    pe.wait_ge(*w)
                with pe.Fori(0, count // 4) as i:
                    for j in range(4):
                        slot = ready(pe, first, j, i, 4)
                        pe.wait_ge(s["out"], 4 * i + (j + 1))
                        tile_chunk(slot, banks[j][:], xn_hi, xn_lo).then_inc(used, 1)

            def dve_part(dve):
                for w in start:
                    dve.wait_ge(*w)
                dve.sem_inc(s["out"], 4)
                with dve.Fori(0, count // 4) as i:
                    for j in range(4):
                        ahead(low_part, dve, first, j, i, 4)
                        finished(dve, first, j, i, 4)
                        dve.wait_ge(s["done"], 4 * i + (j + 1))
                        apart(dve)
                        nc.vector.stream_shuffle(sw[:, j % 2, :], banks[j][:], mask).then_inc(s["swapped"], 1)
                        nc.vector.tensor_tensor(dst[:, 4 * i + j, :], banks[j][:], table_c[:],
                                                ALU.mult).then_inc(s["out"], 1)

            def pool_part(pool):
                for w in start:
                    pool.wait_ge(*w)
                pool.sem_inc(s["done"], 2)
                sines = sem(f"{name}_sines")
                with pool.Fori(0, count // 4) as i:
                    for j in range(4):
                        pool.wait_ge(s["swapped"], 4 * i + (j + 1))
                        nc.gpsimd.tensor_tensor(sw[:, j % 2, :], sw[:, j % 2, :], table_s[:],
                                                ALU.mult).then_inc(sines, 1)
                        pool.wait_ge(s["out"], 4 * i + (j + 5))
                        pool.wait_ge(sines, 4 * i + (j + 1))
                        nc.gpsimd.tensor_tensor(dst[:, 4 * i + j, :], dst[:, 4 * i + j, :], sw[:, j % 2, :],
                                                ALU.add).then_inc(s["done"], 1)

            return act_part, pe_part, dve_part, pool_part, (s["done"], count + 2)

        def mixer2(n_mix2, x_done):
            norm_done = n_mix2[4]
            t = {k: sem(f"b2_{k}") for k in ("tables", "v", "gate", "gate_t", "gates", "blk", "zero", "hi", "lo", "hid",
                                             "gelu", "kv", "kc", "pad")}

            def tables_in(pool):
                pool.wait_ge(*x_done)
                at = 0
                for tile in (nsa_c, nsa_s, ret_c, ret_s, cmp_c, cmp_s, cmp_add, cmp_keep):
                    n = int(np.prod(tile.shape[1:]))
                    to = tile[:].rearrange("p a b -> p (a b)") if len(tile.shape) == 3 else tile[:]
                    pool.dma_start(to, rows[:, at:at + n]).then_inc(t["tables"], 16)
                    at += n

            parts.append((skip, skip, skip, tables_in))
            parts.append(n_mix2)
            qk = roped_out("b2_qk", FIRST["b2_qk"], 12, [norm_done, (t["tables"], 128)], nqk, swapped, nsa_c, nsa_s,
                           SWAP8)
            cmp = copies_out("b2_cmp", FIRST["b2_cmp"], 4, ck)
            fv, fg, fw = FIRST["b2_v"], FIRST["b2_g"], FIRST["b2_w1"]

            def pe_part(pe):
                for j in range(2):
                    slot = ready(pe, fv, j)
                    for n in range(4):
                        k, w = 4 * j + n, slice(n * 256, (n + 1) * 256)
                        for tb in range(TB):
                            at = slice(tb * P, (tb + 1) * P)
                            last = mm3(banks[4 + tb][:, 0:256], xn_hi[:, k, at], xn_lo[:, k, at], w_hi[:, slot, w],
                                       w_lo[:, slot, w], k == 0, k == KT - 1)
                    last.then_inc(used, 1)
                slot = ready(pe, fg, 0)
                pe.wait_ge(*cmp[4])
                tile_chunk(slot, banks[0][:], xn_hi, xn_lo).then_inc(used, 1)
                pe.wait_ge(t["gate"], 1)
                for tb in range(TB):
                    last = nc.tensor.transpose(banks[1][:, 48 * tb:48 * tb + 48], gate_fm[0:48, tb * P:(tb + 1) * P],
                                               ident[0:48, 0:48])
                last.then_inc(t["gate_t"], 1)
                for kv in range(2):
                    pe.wait_ge(t["lo"], kv + 1)
                    if kv:
                        pe.wait_ge(t["v"], 4)
                    for half in range(2):
                        for j in range(2):
                            slot = ready(pe, fw, 4 * kv + 2 * half + j)
                            for n in range(8):
                                k, w = 8 * j + n, slice(n * P, (n + 1) * P)
                                last = mm3(banks[2 + 2 * kv + half][:, 0:64], w_hi[:, slot, w], w_lo[:, slot, w],
                                           blk_hi[:, k, :], blk_lo[:, k, :], k == 0, k == 15)
                            last.then_inc(used, 1)
                pe.wait_ge(t["gelu"], 4)
                pe.wait_ge(t["gates"], 1)
                for half in range(2):
                    last = nc.tensor.matmul(banks[0][:, 0:64], w2_sb[:, half, :], hidden_k[:, half, :],
                                            start=half == 0, stop=half == 1)
                last.then_inc(t["kv"], 1)
                for g in range(2):
                    for half in range(2):
                        last = nc.tensor.matmul(banks[1][:, g * P:(g + 1) * P],
                                                hidden_v[:, half, g, :],
                                                w2_sb[:, 2 + half, :], start=half == 0, stop=half == 1,
                                                skip_group_check=True)
                    last.then_inc(t["kv"], 1)

            def act_part(act):
                for j in range(2):
                    ahead(high_part, act, fv, j)
                ahead(high_part, act, fg, 0)
                finished(act, fg, 0)
                nc.scalar.activation(gate_fm[0:48, :], banks[0][0:48, :], ACT.Sigmoid).then_inc(t["gate"], 1)
                for kv in range(2):
                    act.wait_ge(t["blk"], 8 * (kv + 1))
                    if kv:
                        finished(act, fw, 3)
                    nc.scalar.activation(blk_hi[:], blk[:], ACT.Copy).then_inc(t["hi"], 1)
                    for half in range(2):
                        for j in range(2):
                            ahead(high_part, act, fw, 4 * kv + 2 * half + j)
                        finished(act, fw, 4 * kv + 2 * half + 1)
                        pre = banks[2 + 2 * kv + half][:, 0:64]
                        if kv == 0:
                            nc.scalar.activation(hidden_k[:, half, :], pre, ACT.Gelu_apprx_tanh).then_inc(t["gelu"], 1)
                        else:
                            nc.scalar.activation(
                                hidden_v[:, half].rearrange("p g (f n) -> p g f n", f=4),
                                pre.rearrange("p (g o n) -> p g o n", g=2, o=1).to_broadcast([P, 2, 4, 32]),
                                ACT.Gelu_apprx_tanh).then_inc(t["gelu"], 1)

            def dve_part(dve):
                for j in range(2):
                    ahead(low_part, dve, fv, j)
                finished(dve, fv, 1)
                for tb in range(TB):
                    nc.vector.tensor_copy(nv[:, tb, :], banks[4 + tb][:, 0:256]).then_inc(t["v"], 1)
                ahead(low_part, dve, fg, 0)
                dve.wait_ge(*cmp[4])
                dve.wait_ge(t["zero"], 1)
                for kv in range(2):
                    if kv:
                        dve.wait_ge(t["lo"], 1)
                    for g in range(2):
                        for half in range(2):
                            r = slice(64 * half, 64 * half + 64)
                            view = ck[r, 2 * kv + g, :].rearrange("p (n k two) -> p two k n", k=8, two=2)[:, half]
                            for a in range(2):
                                at = COLS["pos"] + 8 * a
                                emb = col[r, at:at + 8].rearrange("p (k o) -> p k o", o=1).to_broadcast([64, 8, 31])
                                nc.vector.tensor_tensor(blk[r, 8 * a:8 * a + 8, 32 * g:32 * g + 31],
                                                        view[:, :, a:a + 31], emb, ALU.add).then_inc(t["blk"], 1)
                    if kv == 0:
                        dve.wait_ge(t["gate_t"], 1)
                        nc.vector.tensor_copy(gates[:], banks[1][:, 0:192].rearrange("p (t h) -> p t h", t=TB)
                                              ).then_inc(t["gates"], 1)
                    for j in range(4):
                        ahead(low_part, dve, fw, 4 * kv + j)
                dve.wait_ge(t["kv"], 1)
                nc.vector.stream_shuffle(kc_sw[:], banks[0][:, 0:64], SWAP8).then_inc(t["kc"], 1)
                nc.vector.tensor_tensor(kc_raw[:], banks[0][:, 0:64], cmp_c[:], ALU.mult).then_inc(t["kc"], 1)
                dve.wait_ge(t["kc"], 1)
                nc.vector.tensor_tensor(kc_sw[:], kc_sw[:], cmp_s[:], ALU.mult).then_inc(t["kc"], 1)
                dve.wait_ge(t["kc"], 3)
                nc.vector.tensor_tensor(kc_raw[:], kc_raw[:], kc_sw[:], ALU.add).then_inc(t["kc"], 1)
                dve.wait_ge(t["kv"], 3)
                nc.vector.tensor_copy(vc_raw[:], banks[1][:, 0:256].rearrange("p (g d) -> p g d", g=2)
                                      ).then_inc(t["kc"], 1)

            def pool_part(pool):
                pool.wait_ge(*norm_done)
                nc.gpsimd.memset(blk[:], 0.0).then_inc(t["zero"], 1)
                for kv in range(2):
                    pool.wait_ge(t["hi"], kv + 1)
                    nc.gpsimd.tensor_tensor(blk_lo[:], blk[:], blk_hi[:], ALU.subtract).then_inc(t["lo"], 1)
                pool.wait_ge(t["kc"], 5)
                nc.gpsimd.memset(cpad[:], 0.0).then_inc(t["pad"], 1)

            prepare = (act_part, pe_part, dve_part, pool_part)
            nsa_out = sparse_attention([(t["kc"], 5), (t["pad"], 1), (t["v"], 4), qk[4]])
            rqk = roped_out("b2_rqk", FIRST["b2_rqk"], 8, [nsa_out[4]], r_qk, r_swapped, ret_c, ret_s, SWAP16)
            ret = retention(rqk[4])
            between = (skip, lambda pe: pe.wait_ge(*qk[4]), skip, skip)
            return [qk, between, cmp, prepare, nsa_out, rqk, *ret]

        def sparse_attention(start):
            s = {k: sem(f"nsa_{k}") for k in ("k_hi", "k_lo", "q_hi", "q_lo", "scored", "biased", "negated", "exp",
                                              "guard", "recip", "inverse", "scaled", "turned", "hi", "lo", "summed",
                                              "out", "c_scored", "c_dve", "c_exp", "c_turned", "c_hi", "c_lo")}
            units = [(0, 0), (0, 1), (1, 0), (1, 1)]

            def v_twice(g, m):
                return nv[:, :, bass.ds(g * 64 + 128 * m, 64)].rearrange("p t (o d) -> p t o d", o=1).to_broadcast(
                    [P, TB, 2, 64])

            def twice(tile, m):
                return tile[:, :, m, :].rearrange("p t (o d) -> p t o d", o=2)

            def begin(eng):
                for w in start:
                    eng.wait_ge(*w)

            def pe_part(pe):
                begin(pe)
                pe.sem_inc(s["scored"], 4)
                pe.sem_inc(s["turned"], 8)
                pe.sem_inc(s["summed"], 9)
                pe.sem_inc(s["c_turned"], 1)
                with pe.Fori(0, 2) as g:
                    pe.wait_ge(s["k_lo"], 6 * g + 6)
                    apart(pe)
                    with pe.Fori(0, 4) as p:
                        i = 4 * g + p

                        def score(u):
                            j, m = units[u]
                            r = slice(64 * j, 64 * j + 64)
                            for qb in range(TB):
                                pe.wait_ge(s["biased"], 16 * i + (4 * u + qb + 1))
                                at, n = slice(qb * P, (qb + 1) * P), (qb + 1) * P
                                mm3(banks[qb][:, 0:n], nq_hi[r, at], nq_lo[r, at], nk_hi[r, m, 0:n],
                                    nk_lo[r, m, 0:n]).then_inc(s["scored"], 1)

                        def turn(u, kb):
                            if kb == 0:
                                pe.wait_ge(s["scaled"], 4 * i + (u + 1))
                            pe.wait_ge(s["lo"], 16 * i + (4 * u + kb + 1))
                            for qb in range(kb, TB):
                                last = nc.tensor.transpose(banks[4 + kb % 2][:, (qb - kb) * P:(qb - kb + 1) * P],
                                                           nprob[:, u % 2, OFF[qb] + kb * P:OFF[qb] + (kb + 1) * P],
                                                           ident[:])
                            last.then_inc(s["turned"], 1)

                        def values(u, kb):
                            j, m = units[u]
                            pe.wait_ge(s["lo"], 16 * i + (4 * u + kb + 3))
                            at = slice(KOFF[kb], KOFF[kb + 1])
                            mm3(banks[6][:, kb * P:S], nvs_hi[:, kb, m, :], nvs_lo[:, kb, m, :], npt_hi[:, at], npt_lo[:, at], False,
                                m == 1 and kb == TB - 1).then_inc(s["summed"], 1)

                        def turns_and_values(u):
                            turn(u, 0)
                            for kb in range(1, TB):
                                turn(u, kb)
                                values(u, kb - 1)
                            values(u, TB - 1)

                        def compressed(j):
                            pe.wait_ge(s["c_lo"], 2 * i + (j + 1))
                            for qb in range(TB):
                                last = nc.tensor.transpose(banks[7][:, qb * P:(qb + 1) * P],
                                                           cpad[:, j, qb * P:(qb + 1) * P], ident[:])
                            last.then_inc(s["c_turned"], 1)
                            pe.wait_ge(s["c_lo"], 2 * i + (j + 2))
                            pe.wait_ge(s["out"], 2 * i + (j + 1))
                            mm3(banks[6][:], vcs_hi[:], vcs_lo[:], cpt_hi[:], cpt_lo[:], True,
                                False).then_inc(s["summed"], 1)

                        pe.wait_ge(s["q_lo"], i + 1)
                        pe.wait_ge(s["c_lo"], 2 * i + 1)
                        for j in range(2):
                            r = slice(64 * j, 64 * j + 64)
                            if j:
                                pe.wait_ge(s["c_scored"], 2 * i + 1)
                            for qb in range(TB):
                                at = slice(qb * P, (qb + 1) * P)
                                last = mm3(banks[7][:, (TB * j + qb) * 32:(TB * j + qb + 1) * 32], nq_hi[r, at],
                                           nq_lo[r, at], kc_hi[r, :], kc_lo[r, :])
                            last.then_inc(s["c_scored"], 1)
                        score(0)
                        score(1)
                        pe.wait_ge(s["c_dve"], 10 * i + 10)
                        compressed(0)
                        turns_and_values(0)
                        score(2)
                        turns_and_values(1)
                        compressed(1)
                        score(3)
                        turns_and_values(2)
                        turns_and_values(3)

            def act_part(act):
                begin(act)
                act.sem_inc(s["out"], 1)
                with act.Fori(0, 2) as g:
                    act.wait_ge(s["summed"], 72 * g + 9)
                    for m in range(2):
                        nc.scalar.activation(nk_hi[:, m, :], nqk[:, g + (8 + 2 * m), :], ACT.Copy).then_inc(s["k_hi"], 1)
                        nc.scalar.activation(twice(nvs_hi, m), v_twice(g, m),
                                             ACT.Copy).then_inc(s["k_hi"], 1)
                    nc.scalar.activation(vcs_hi[:], vc_raw[:, g, :], ACT.Copy).then_inc(s["k_hi"], 1)
                    nc.scalar.activation(kc_hi[:], kc_raw[:, bass.ds(g * 32, 32)], ACT.Copy).then_inc(s["k_hi"], 1)
                    with act.Fori(0, 4) as p:
                        i = 4 * g + p

                        def exps(u):
                            act.wait_ge(s["negated"], 4 * i + (u + 1))
                            for qb in range(TB):
                                at = nprob[:, u % 2, scores_rows(qb)]
                                n = 4 * (u % 2) + qb
                                nc.scalar.activation(at, at, ACT.Exp, bias=neg_top[:, n:n + 1], scale=0.125,
                                                     accum_out=total[:, n:n + 1]).then_inc(s["exp"], 1)

                        def highs(u):
                            for kb in range(TB):
                                act.wait_ge(s["turned"], 16 * i + (4 * u + kb + 9))
                                act.wait_ge(s["summed"], 18 * i + ((6, 11, 15, 20)[u] + kb))
                                nc.scalar.activation(npt_hi[:, KOFF[kb]:KOFF[kb + 1]],
                                                     banks[4 + kb % 2][:, 0:S - kb * P], ACT.Copy).then_inc(s["hi"], 1)

                        def c_high(j):
                            act.wait_ge(s["c_turned"], 2 * i + (j + 2))
                            act.wait_ge(s["summed"], 18 * i + 9 * j + 1)
                            nc.scalar.activation(cpt_hi[:], banks[7][:], ACT.Copy).then_inc(s["c_hi"], 1)

                        def output(j):
                            act.wait_ge(s["summed"], 18 * i + (9 * j + 18))
                            r = slice(64 * j, 64 * j + 64)
                            nc.scalar.activation(a_raw[r, i, :], banks[6][r, :], ACT.Copy).then_inc(s["out"], 1)

                        act.wait_ge(s["scored"], 16 * i + 4)
                        nc.scalar.activation(nq_hi[:], nqk[:, i, :], ACT.Copy).then_inc(s["q_hi"], 1)
                        act.wait_ge(s["c_dve"], 10 * i + 3)
                        nc.scalar.activation(csc[:], csc[:], ACT.Exp, scale=0.125).then_inc(s["c_exp"], 1)
                        exps(0)
                        exps(1)
                        c_high(0)
                        highs(0)
                        exps(2)
                        highs(1)
                        output(0)
                        c_high(1)
                        exps(3)
                        highs(2)
                        highs(3)
                        output(1)

            def dve_part(dve):
                begin(dve)
                dve.sem_inc(s["biased"], 4)
                dve.sem_inc(s["lo"], 2)
                dve.sem_inc(s["c_lo"], 1)
                with dve.Fori(0, 2) as g:
                    with dve.Fori(0, 4) as p:
                        i = 4 * g + p

                        def biased(u):
                            for qb in range(TB):
                                dve.wait_ge(s["scored"], 16 * i + (4 * u + qb + 5))
                                if qb == 0:
                                    dve.wait_ge(s["turned"], 16 * i + (4 * u + 4))
                                apart(dve)
                                n = 4 * (u % 2) + qb
                                width = (qb + 1) * P
                                nc.vector.tensor_tensor_reduce(nprob[:, u % 2, scores_rows(qb)], banks[qb][:, 0:width],
                                                               bias_tri[:, S - width:S], 1.0, -3.0e38, ALU.add, ALU.max,
                                                               top_s[:, n:n + 1]).then_inc(s["biased"], 1)
                            dve.wait_ge(s["biased"], 16 * i + (4 * u + 8))
                            n = 4 * (u % 2)
                            nc.vector.tensor_scalar(neg_top[:, n:n + 4], top_s[:, n:n + 4], -0.125, None,
                                                    ALU.mult).then_inc(s["negated"], 1)

                        def invert(u):
                            j, m = units[u]
                            n = slice(4 * (u % 2), 4 * (u % 2) + 4)
                            dve.wait_ge(s["exp"], 16 * i + (4 * u + 4))
                            nc.vector.tensor_scalar(nguard[:, n], total[:, n], 1e-20, None,
                                                    ALU.max).then_inc(s["guard"], 1)
                            dve.wait_ge(s["guard"], 4 * i + (u + 1))
                            nc.vector.reciprocal(nguard[:, n], nguard[:, n]).then_inc(s["recip"], 1)
                            dve.wait_ge(s["recip"], 4 * i + (u + 1))
                            nc.vector.tensor_tensor(inverse[:, n], nguard[:, n],
                                                    gates[:, :, i * 6 + (3 * j + 1 + m)],
                                                    ALU.mult).then_inc(s["inverse"], 1)

                        def lows(u):
                            for kb in range(TB):
                                dve.wait_ge(s["hi"], 16 * i + (4 * u + kb + 1))
                                at = slice(KOFF[kb], KOFF[kb + 1])
                                nc.vector.tensor_tensor(npt_lo[:, at], banks[4 + kb % 2][:, 0:S - kb * P], npt_hi[:, at],
                                                        ALU.subtract).then_inc(s["lo"], 1)

                        def c_low(j):
                            dve.wait_ge(s["c_hi"], 2 * i + (j + 1))
                            nc.vector.tensor_tensor(cpt_lo[:], banks[7][:], cpt_hi[:],
                                                    ALU.subtract).then_inc(s["c_lo"], 1)

                        dve.wait_ge(s["c_scored"], 2 * i + 2)
                        add = cmp_add[:].rearrange("p (o t) n -> p o t n", o=1).to_broadcast([P, 2, TB, 32])
                        keep = cmp_keep[:].rearrange("p (o t) n -> p o t n", o=1).to_broadcast([P, 2, TB, 32])
                        done = [0]

                        def step(instruction, wait=True):
                            instruction.then_inc(s["c_dve"], 1)
                            done[0] += 1
                            if wait:
                                dve.wait_ge(s["c_dve"], 10 * i + done[0])

                        over = [t.rearrange("p (h t o) -> p h t o", h=2, o=1).to_broadcast([P, 2, TB, 32])
                                for t in (c_top, c_inverse)]
                        step(nc.vector.tensor_tensor(csc[:], banks[7][:, 0:256].rearrange("p (h t n) -> p h t n", h=2, t=TB),
                                                     add, ALU.add))
                        step(nc.vector.tensor_reduce(c_top.rearrange("p (h t) -> p h t", h=2), csc[:], AX.X, ALU.max))
                        step(nc.vector.tensor_tensor(csc[:], csc[:], over[0], ALU.subtract), False)
                        biased(0)
                        dve.wait_ge(s["c_exp"], i + 1)
                        step(nc.vector.tensor_tensor(csc[:], csc[:], keep, ALU.mult))
                        step(nc.vector.tensor_reduce(c_total.rearrange("p (h t) -> p h t", h=2), csc[:], AX.X, ALU.add))
                        step(nc.vector.tensor_scalar(c_total, c_total, 1e-20, None, ALU.max))
                        step(nc.vector.reciprocal(c_total, c_total))
                        step(nc.vector.tensor_tensor(c_inverse.rearrange("p (h t) -> p h t", h=2),
                                                     c_total.rearrange("p (h t) -> p h t", h=2),
                                                     gates[:, :, bass.ds(i * 6, 6)].rearrange("p t (h c) -> p h t c", c=3)[:, :, :, 0],
                                                     ALU.mult))
                        for j in range(2):
                            diagonal = cpad[:, j, :].rearrange("p (t w) -> p t w", w=P + 32)[:, :, 0:32]
                            step(nc.vector.tensor_tensor(diagonal, csc[:, j, :, :], over[1][:, j, :, :],
                                                         ALU.mult), False)
                        biased(1)
                        c_low(0)
                        invert(0)
                        invert(1)
                        lows(0)
                        biased(2)
                        lows(1)
                        c_low(1)
                        biased(3)
                        invert(2)
                        lows(2)
                        invert(3)
                        lows(3)

            def pool_part(pool):
                begin(pool)
                with pool.Fori(0, 2) as g:
                    for m in range(2):
                        pool.wait_ge(s["k_hi"], 6 * g + (2 * m + 1))
                        nc.gpsimd.tensor_tensor(nk_lo[:, m, :], nqk[:, g + (8 + 2 * m), :], nk_hi[:, m, :],
                                                ALU.subtract).then_inc(s["k_lo"], 1)
                        pool.wait_ge(s["k_hi"], 6 * g + (2 * m + 2))
                        nc.gpsimd.tensor_tensor(twice(nvs_lo, m), v_twice(g, m), twice(nvs_hi, m), ALU.subtract).then_inc(s["k_lo"], 1)
                    pool.wait_ge(s["k_hi"], 6 * g + 5)
                    nc.gpsimd.tensor_tensor(vcs_lo[:], vc_raw[:, g, :], vcs_hi[:], ALU.subtract).then_inc(s["k_lo"], 1)
                    pool.wait_ge(s["k_hi"], 6 * g + 6)
                    nc.gpsimd.tensor_tensor(kc_lo[:], kc_raw[:, bass.ds(g * 32, 32)], kc_hi[:],
                                            ALU.subtract).then_inc(s["k_lo"], 1)
                    with pool.Fori(0, 4) as p:
                        i = 4 * g + p
                        pool.wait_ge(s["q_hi"], i + 1)
                        nc.gpsimd.tensor_tensor(nq_lo[:], nqk[:, i, :], nq_hi[:], ALU.subtract).then_inc(s["q_lo"], 1)
                        for u in range(4):
                            pool.wait_ge(s["inverse"], 4 * i + (u + 1))
                            apart(pool)
                            for qb in range(TB):
                                at = nprob[:, u % 2, scores_rows(qb)]
                                n = 4 * (u % 2) + qb
                                last = nc.gpsimd.tensor_scalar(at, at, inverse[:, n:n + 1], None, ALU.mult)
                            last.then_inc(s["scaled"], 1)

            return act_part, pe_part, dve_part, pool_part, (s["out"], 17)

        def retention(qk_done):
            s = {k: sem(f"ret_{k}") for k in ("v", "staged_hi", "staged_lo", "scored", "weighted", "hi", "lo", "summed",
                                              "out", "mean", "centred", "square", "var", "root", "recip", "done",
                                              "gate", "gated")}
            decay_in = sem("ret_decay_in")
            frv, fgr = FIRST["b2_rv"], FIRST["b2_gr"]

            def v_pe(pe):
                for c in range(2):
                    for j in range(4):
                        slot = ready(pe, frv, 4 * c + j)
                        if c and j == 0:
                            pe.wait_ge(s["v"], 4)
                        for t in range(2):
                            k, w = 2 * j + t, slice(t * S, (t + 1) * S)
                            for tb in range(TB):
                                at = slice(tb * P, (tb + 1) * P)
                                last = mm3(banks[4 + tb][:], xn_hi[:, k, at], xn_lo[:, k, at], w_hi[:, slot, w],
                                           w_lo[:, slot, w], k == 0, k == KT - 1)
                        last.then_inc(used, 1)

            def v_act(act):
                for j in range(8):
                    ahead(high_part, act, frv, j)

            def v_dve(dve):
                for c in range(2):
                    for j in range(4):
                        ahead(low_part, dve, frv, 4 * c + j)
                    finished(dve, frv, 4 * c + 3)
                    for tb in range(TB):
                        nc.vector.tensor_copy(r_v[:, tb, c * S:(c + 1) * S], banks[4 + tb][:]).then_inc(s["v"], 1)

            start = [qk_done, (s["v"], 8)]

            def begin(eng):
                for w in start:
                    eng.wait_ge(*w)

            def pe_part(pe):
                begin(pe)
                pe.sem_inc(s["summed"], 8)
                with pe.Fori(0, 4) as i:
                    def score(j):
                        r = slice(64 * j, 64 * j + 64)
                        for kb in range(TB):
                            pe.wait_ge(s["weighted"], 8 * i + (4 * j + kb + 1))
                            mm3(banks[kb][:, 0:S - kb * P], rk_hi[r, kb * P:(kb + 1) * P], rk_lo[r, kb * P:(kb + 1) * P],
                                rq_hi[r, kb * P:S], rq_lo[r, kb * P:S]).then_inc(s["scored"], 1)

                    def values(j):
                        pe.wait_ge(s["out"], 2 * i + (j + 1))
                        for kb in range(TB):
                            pe.wait_ge(s["lo"], 8 * i + (4 * j + kb + 3))
                            w = slice(P * j, P * j + P)
                            mm3(banks[6 + j][:, kb * P:S], rv_hi[:, kb, w], rv_lo[:, kb, w], ws_hi[:, kb % 2, 0:S - kb * P],
                                ws_lo[:, kb % 2, 0:S - kb * P], kb == 0, kb == TB - 1).then_inc(s["summed"], 1)

                    def mean(j):
                        pe.wait_ge(s["out"], 2 * i + (j + 3))
                        nc.tensor.matmul(banks[4][:], ones[:], r_raw[:, 2 * i + j, :], start=True,
                                         stop=True).then_inc(s["mean"], 1)

                    def var(j):
                        pe.wait_ge(s["square"], 2 * i + (j + 1))
                        nc.tensor.matmul(banks[5][:], ones[:], gn_sq[:], start=True, stop=True).then_inc(s["var"], 1)

                    pe.wait_ge(s["staged_lo"], 3 * i + 3)
                    score(0)
                    score(1)
                    values(0)
                    mean(0)
                    values(1)
                    var(0)
                    mean(1)
                    var(1)

            def act_part(act):
                begin(act)
                act.sem_inc(s["out"], 2)
                with act.Fori(0, 4) as i:
                    def highs(j):
                        for kb in range(TB):
                            act.wait_ge(s["weighted"], 8 * i + (4 * j + kb + 5))
                            act.wait_ge(s["summed"], 8 * i + (4 * j + kb + 7))
                            nc.scalar.activation(ws_hi[:, kb % 2, 0:S - kb * P], weighted[:, kb % 2, 0:S - kb * P],
                                                 ACT.Copy).then_inc(s["hi"], 1)

                    def output(j):
                        act.wait_ge(s["summed"], 8 * i + (4 * j + 12))
                        nc.scalar.activation(r_raw[:, 2 * i + j, :], banks[6 + j][:], ACT.Copy).then_inc(s["out"], 1)

                    def square(j):
                        act.wait_ge(s["centred"], 2 * i + (j + 1))
                        apart(act)
                        nc.scalar.activation(gn_sq[:], r_raw[:, 2 * i + j, :], ACT.Square).then_inc(s["square"], 1)

                    def root(j):
                        act.wait_ge(s["var"], 2 * i + (j + 1))
                        nc.scalar.activation(gn_r[:], banks[5][:], ACT.Sqrt, bias=col[:, COLS["gneps"]:COLS["gneps"] + 1],
                                             scale=1.0 / P).then_inc(s["root"], 1)

                    act.wait_ge(s["summed"], 8 * i + 8)
                    nc.scalar.activation(rq_hi[:], r_qk[:, i, :], ACT.Copy).then_inc(s["staged_hi"], 1)
                    nc.scalar.activation(rk_hi[:], r_qk[:, i + 4, :], ACT.Copy).then_inc(s["staged_hi"], 1)
                    nc.scalar.activation(rv_hi[:], r_v[:, :, bass.ds(i * 2 * P, 2 * P)], ACT.Copy).then_inc(s["staged_hi"], 1)
                    highs(0)
                    output(0)
                    highs(1)
                    square(0)
                    root(0)
                    output(1)
                    act.wait_ge(s["done"], 2 * i + 1)
                    square(1)
                    root(1)

            def dve_part(dve):
                begin(dve)
                dve.sem_inc(s["weighted"], 4)
                with dve.Fori(0, 4) as i:
                    dve.wait_ge(decay_in, 16 * i + 16)

                    def weigh(j):
                        for kb in range(TB):
                            dve.wait_ge(s["scored"], 8 * i + (4 * j + kb + 1))
                            dve.wait_ge(s["lo"], 8 * i + (4 * j + kb + 1))
                            nc.vector.tensor_tensor(weighted[:, kb % 2, 0:S - kb * P], banks[kb][:, 0:S - kb * P],
                                                    decay[:, j, 0:S - kb * P], ALU.mult).then_inc(s["weighted"], 1)

                    def centre(j):
                        dve.wait_ge(s["mean"], 2 * i + (j + 1))
                        nc.vector.scalar_tensor_tensor(r_raw[:, 2 * i + j, :], banks[4][:], -1.0 / P,
                                                       r_raw[:, 2 * i + j, :], ALU.mult, ALU.add).then_inc(s["centred"], 1)

                    def normalise(j):
                        dve.wait_ge(s["root"], 2 * i + (j + 1))
                        nc.vector.reciprocal(gn_r[:], gn_r[:]).then_inc(s["recip"], 1)
                        dve.wait_ge(s["recip"], 2 * i + (j + 1))
                        nc.vector.scalar_tensor_tensor(r_raw[:, 2 * i + j, :], r_raw[:, 2 * i + j, :],
                                                       col[:, bass.ds(i * 2 + (COLS["ret"] + j), 1)], gn_r[:], ALU.mult,
                                                       ALU.mult).then_inc(s["done"], 1)

                    weigh(0)
                    weigh(1)
                    centre(0)
                    normalise(0)
                    centre(1)
                    normalise(1)

            def pool_part(pool):
                begin(pool)
                pool.sem_inc(s["lo"], 2)
                with pool.Fori(0, 4) as i:
                    pool.wait_ge(s["weighted"], 8 * i + 4)
                    pool.dma_start(decay[:], decays[bass.ds(i * 2, 2)].rearrange("h p s -> p h s")).then_inc(decay_in, 16)
                    for n, (to, src, hi) in enumerate(((rq_lo, r_qk[:, i, :], rq_hi), (rk_lo, r_qk[:, i + 4, :], rk_hi),
                                                       (rv_lo, r_v[:, :, bass.ds(i * 2 * P, 2 * P)], rv_hi))):
                        pool.wait_ge(s["staged_hi"], 3 * i + (n + 1))
                        nc.gpsimd.tensor_tensor(to[:], src, hi[:], ALU.subtract).then_inc(s["staged_lo"], 1)
                    for j in range(2):
                        for kb in range(TB):
                            pool.wait_ge(s["hi"], 8 * i + (4 * j + kb + 1))
                            nc.gpsimd.tensor_tensor(ws_lo[:, kb % 2, 0:S - kb * P], weighted[:, kb % 2, 0:S - kb * P],
                                                    ws_hi[:, kb % 2, 0:S - kb * P], ALU.subtract).then_inc(s["lo"], 1)

            def g_pe(pe):
                pe.wait_ge(s["done"], 8)
                with pe.Fori(0, 2) as i:
                    for j in range(4):
                        slot = ready(pe, fgr, j, i, 4)
                        pe.wait_ge(s["gate"], 4 * i + (j + 1))
                        tile_chunk(slot, banks[j][:], xn_hi, xn_lo).then_inc(used, 1)

            def g_act(act):
                act.sem_inc(s["gate"], 4)
                with act.Fori(0, 2) as i:
                    for j in range(4):
                        ahead(high_part, act, fgr, j, i, 4)
                        finished(act, fgr, j, i, 4)
                        act.wait_ge(s["gated"], 4 * i + (j + 1))
                        nc.scalar.activation(weighted[:, j % 2, :], banks[j][:], ACT.Silu).then_inc(s["gate"], 1)

            def g_dve(dve):
                dve.sem_inc(s["gated"], 2)
                with dve.Fori(0, 2) as i:
                    for j in range(4):
                        ahead(low_part, dve, fgr, j, i, 4)
                        dve.wait_ge(s["gate"], 4 * i + (j + 5))
                        nc.vector.tensor_tensor(r_raw[:, 4 * i + j, :], r_raw[:, 4 * i + j, :], weighted[:, j % 2, :],
                                                ALU.mult).then_inc(s["gated"], 1)

            return [(v_act, v_pe, v_dve, skip), (act_part, pe_part, dve_part, pool_part),
                    (g_act, g_pe, g_dve, skip, (s["gated"], 10))]

        split = (xn_hi, xn_lo)
        natural = list(range(KT))

        n_mix1 = norm("n_mix1", x, natural, COLS["mix1"], (x_in, 16), 7, D, split, dma=True)
        parts.append(n_mix1)
        front = mixer1(n_mix1[4])
        parts.extend(front)
        m_b1 = merge("b1", [front[-1][4]], m1_hi, m1_lo, m1_temps,
                     [(2, 0, 2, y1[:, 0:4, :], y1_hi[:, 0:4, :], y1_lo[:, 0:4, :]),
                      (2, 4, 3, y1[:, 4:8, :], y1_hi[:, 4:8, :], y1_lo[:, 4:8, :])], 3, COLS["bgate"])
        n_ffn0 = norm("n_ffn0", x, natural, COLS["ffn0"], m_b1[4], 7, D, split)
        f0 = feed_forward("f0", 1.0, n_ffn0[4])
        n_fin1 = norm("n_fin1", x, ORDER, COLS["fin1"], f0[4], 7, D)
        n_ffn1 = norm("n_ffn1", x, ORDER, COLS["ffn1"], (n_fin1[4][0], n_fin1[4][1] - KT + 1), 7, D, split)
        f1 = feed_forward("f1", 0.5, n_ffn1[4])
        parts.extend([m_b1, n_ffn0, f0, n_fin1, n_ffn1, f1])
        n_mix2 = norm("n_mix2", x, ORDER, COLS["mix2"], f1[4], 7, D, split)
        second = mixer2(n_mix2, f1[4])
        parts.extend(second)
        m_b2 = merge("b2", [second[-1][4]], m2_hi, m2_lo, m2_temps,
                     [(2, 0, 2, a_raw[:, :, :], a_hi, a_lo), (3, 0, 3, r_raw[:, :, :], r_hi, r_lo)], 4, None)
        n_ffn2 = norm("n_ffn2", x, natural, COLS["ffn2"], m_b2[4], 7, D, split)
        f2 = feed_forward("f2", 0.5, n_ffn2[4])
        n_fin2 = norm("n_fin2", x, ORDER, COLS["fin2"], f2[4], 7, D)
        parts.extend([m_b2, n_ffn2, f2, n_fin2])
        final_done = n_fin2[4]

        block = top.enter_context(nc.Block())

        @block.sync
        def _(sp):
            sp.dma_start(x[:], xt.rearrange("p (k s) -> p k s", s=S)).then_inc(x_in, 16)
            for t, at in ((ident, 0), (col, 1)):
                sp.dma_start(t[:], cols[:, at * P:(at + 1) * P]).then_inc(consts_in, 16)
            for slot in range(2):
                sp.dma_start(w_raw[:, slot, :], stream[slot]).then_inc(loaded[slot], 16)
            sp.dma_start(bias_tri[:], tables[:, S:2 * S]).then_inc(consts_in, 16)
            sp.dma_start(bias_chunk[:], tables[:, 2 * S:3 * S]).then_inc(consts_in, 16)
            sp.dma_start(cumul_raw[:], tables[:, 0:S]).then_inc(consts_in, 16)
            sp.dma_start(w2_sb[:], w2.rearrange("p (t d) -> p t d", d=P)).then_inc(consts_in, 16)
            with sp.Fori(1, CHUNKS // 2) as i:
                for slot in range(2):
                    sp.wait_ge(split_lo, 2 * i + (slot - 1))
                    sp.dma_start(w_raw[:, slot, :], stream[2 * i + slot]).then_inc(loaded[slot], 16)
            if CHUNKS % 2:
                sp.wait_ge(split_lo, CHUNKS - 2)
                sp.dma_start(w_raw[:, 0, :], stream[CHUNKS - 1]).then_inc(loaded[0], 16)
            sp.wait_ge(final_done[0], final_done[1])
            sp.dma_start(out.rearrange("p (k s) -> p k s", s=S), x[:]).then_inc(stored, 16)
            sp.wait_ge(stored, 16)

        @block.scalar
        def _(act):
            act.wait_ge(consts_in, 96)
            for c in range(LOOKAHEAD):
                high_part(act, *place(0, c))
            for part in parts:
                part[0](act)

        @block.tensor
        def _(pe):
            pe.sem_inc(used, RING)
            pe.wait_ge(consts_in, 96)
            pe.wait_ge(consts_made, 2)
            for part in parts:
                part[1](pe)

        @block.vector
        def _(dve):
            nc.vector.memset(ones[:], 1.0).then_inc(consts_made, 1)
            dve.wait_ge(consts_in, 96)
            for c in range(LOOKAHEAD):
                low_part(dve, *place(0, c))
            for part in parts:
                part[2](dve)

        @block.gpsimd
        def _(pool):
            pool.wait_ge(consts_in, 96)
            nc.gpsimd.tensor_copy(cumul[:], cumul_raw[:]).then_inc(consts_made, 1)
            for part in parts:
                part[3](pool)


def _tiles(w):
    k, n = w.shape
    return w.reshape(k // P, P, n // P, P).transpose(2, 1, 0, 3).reshape(n // P, P, k)


def _token_major(w):
    k, n = w.shape
    per = CW // n
    return w.reshape(k // P // per, per, P, n).transpose(0, 2, 1, 3).reshape(-1, P, CW)


def _pad(w, n=P):
    return np.concatenate([w, np.zeros((w.shape[0], n - w.shape[1]), w.dtype)], 1)


def _gate_up(gate, up):
    return np.stack([_tiles(gate), _tiles(up)], 1).reshape(-1, P, CW)


def _column(v):
    return v.reshape(-1, P).T


def pack_first(a):
    w = a["w_in"][0]
    at = np.cumsum([0, 512, 512, 512, 8, 256, 128, 32, D, D])
    qa, ka, va, fa, cq, ckv, kr, ga, gb = (w[:, i:j] for i, j in zip(at[:-1], at[1:]))
    fk = np.concatenate([_pad(fa, 64), kr, kr], 1)
    wq = a["w_q_up"][0].reshape(256, 8, 96)
    q_up = np.concatenate([np.concatenate([wq, np.zeros((256, 8, 32), w.dtype)], 2).reshape(256, 1024)], 1)
    wkv = a["w_kv_up"][0].reshape(P, 8, P)
    k_up = np.concatenate([wkv[:, :, :64], np.zeros((P, 8, 64), w.dtype)], 2).reshape(P, CW)
    v_up = _pad(wkv[:, :, 64:].reshape(P, 512), CW)
    merge = np.stack([_tiles(ga), _tiles(gb),
                      np.concatenate([_tiles(a["w_branch_a"][0]), _tiles(a["w_branch_b"][0])], 2)], 1)
    return [_tiles(qa), _tiles(ka), _token_major(va), _tiles(fk), _tiles(cq), _tiles(ckv),
            _tiles(q_up).reshape(2, 4, P, 256).transpose(0, 2, 1, 3).reshape(2, P, CW), k_up[None], v_up[None],
            merge.reshape(-1, P, CW), _tiles(a["w_out"][0]),
            _gate_up(a["w_ffn_gate"][0], a["w_ffn_up"][0]), a["w_ffn_down"][0].reshape(FT, P, CW)]


def pack_cols(a):
    cols = np.zeros((P, P), np.float32)

    def put(name, v):
        cols[:v.shape[0], COLS[name]:COLS[name] + v.shape[1]] = v

    for name, key in (("mix1", "norm_mix_g"), ("qa", "q_a_norm_g"), ("kva", "kv_a_norm_g"), ("bgate", "b_gate"),
                      ("ffn0", "norm_ffn_g"), ("fin1", "norm_final_g"), ("ffn1", "ffn1_norm_2"),
                      ("mix2", "mix_norm_2"), ("ret", "ret_gn_gain_2"), ("ffn2", "ffn2_norm_2"),
                      ("fin2", "final_norm_2")):
        put(name, _column(a[key].reshape(-1)))
    cols[0:8, COLS["bf"]] = a["b_forget"].reshape(-1)
    half = np.float32(10000.0) ** (-np.arange(16, dtype=np.float32) / 16)
    cols[64:96, COLS["freq"]] = np.tile(half, 2)
    cols[64:96, COLS["sgn"]] = np.repeat(np.float32([-1, 1]), 16)
    cols[:, COLS["eps"]] = EPS
    cols[:, COLS["gneps"]] = GN_EPS
    cols[:, COLS["one"]] = 1.0
    put("pos", a["cmp_pos_emb_2"][0].reshape(16, P).T)
    return np.concatenate([np.eye(P, dtype=np.float32), cols], 1)


def shape_tables():
    row, at = np.arange(P)[:, None], np.arange(S)[None, :]
    cumul = np.where(at >= row, -8.0, 0.0)
    tri = np.where(at - (S - P) > row, -1e30, 0.0)
    chunk = np.where((at - (S - P)) // 64 > row // 64, -1e30, 0.0)
    return np.concatenate([cumul, tri, chunk], 1).astype(np.float32)


def _twice(w):
    return np.concatenate([w, w], 1)


def pack_second(a):
    w = a["w_in_2"][0]
    at = np.cumsum([0, D, P, P, P, P, P, P, 48, S, S, D, D, D, D])
    (q, kc, vc, ks, vs, kw, vw, g, rq, rk, rv, rg, ga, gr) = (w[:, i:j] for i, j in zip(at[:-1], at[1:]))

    def groups(w):
        return np.concatenate([_twice(w[:, :64]), _twice(w[:, 64:])], 1)

    order = np.concatenate([np.arange(0, 16), np.arange(32, 48), np.arange(16, 32), np.arange(48, 64)])
    order = (64 * np.arange(8)[:, None] + order).reshape(-1)
    merge = np.stack([_tiles(ga), _tiles(gr), _tiles(a["w_branch_nsa_2"][0]), _tiles(a["w_branch_ret_2"][0])], 1)

    def hidden(w):
        return _tiles(w).reshape(2, P, 2, CW).transpose(0, 2, 1, 3).reshape(4, P, CW)

    return [_gate_up(a["ffn1_w_gate_2"][0], a["ffn1_w_up_2"][0]), a["ffn1_w_down_2"][0].reshape(FT, P, CW),
            _tiles(q), _tiles(groups(ks)), _tiles(groups(kw)), _tiles(groups(kc)), _tiles(groups(vc)),
            _token_major(np.concatenate([vs, vw], 1)), _tiles(_pad(g)), hidden(a["cmp_k_w1_2"][0]),
            hidden(a["cmp_v_w1_2"][0]), _tiles(rq[:, order]), _tiles(rk[:, order]), _token_major(rv[:, :S]),
            _token_major(rv[:, S:]), _tiles(rg), merge.reshape(-1, P, CW), _tiles(a["w_out_2"][0]),
            _gate_up(a["ffn2_w_gate_2"][0], a["ffn2_w_up_2"][0]), a["ffn2_w_down_2"][0].reshape(FT, P, CW)]


def second_tables():
    row = np.arange(P) % 64

    def rope(positions, freq, sign, rotated):
        angle = positions.astype(np.float32)[None, :] * freq[:, None]
        cos = np.where(rotated[:, None], np.cos(angle), 1.0)
        sin = np.where(rotated[:, None], sign[:, None] * np.sin(angle), 0.0)
        return [cos, sin]

    f16 = np.float32(500000.0) ** (-(np.arange(8, dtype=np.float32) * np.float32(2.0) / np.float32(16)))
    f64 = np.float32(10000.0) ** (-(np.arange(32, dtype=np.float32) * np.float32(2.0) / np.float32(64)))
    nsa = (f16[row % 8], np.where(row < 8, -1.0, 1.0), row < 16)
    ret = (f64[(row // 32) * 16 + row % 16], np.where(row % 32 < 16, -1.0, 1.0), row < 64)
    tokens, windows = np.arange(S), np.tile(16 * np.arange(32) + 31, 2)
    query = np.arange(P)[:, None, None] + P * np.arange(TB)[None, :, None]
    seen = (16 * np.arange(32) + 31 <= query) & (np.arange(32) < 31)
    rows = [*rope(tokens, *nsa), *rope(tokens, *ret), *rope(windows, *nsa),
            np.where(seen, 0.0, -1e30).reshape(P, P), seen.reshape(P, P)]
    return np.concatenate([r.astype(np.float32) for r in rows], 1)


def decay_tables():
    head = np.arange(8)[:, None, None]
    gap = np.arange(S)[None, None, :] - np.arange(P)[None, :, None]
    return np.where(gap >= 0, 0.125 * (1.0 - 2.0 ** (-5.0 - head)) ** np.maximum(gap, 0), 0.0).astype(np.float32)


def kernel(**inputs):
    from concourse import bacc
    from concourse.bass_utils import run_bass_kernel_spmd

    a = {k: np.asarray(v) for k, v in inputs.items()}
    nc = bacc.Bacc("TRN2", target_bir_lowering=False, num_devices=1)
    data = {
        "stream": np.concatenate(pack_first(a) + pack_second(a)),
        "xt": np.ascontiguousarray(a["x"][0].T.reshape(KT, P, S).transpose(1, 0, 2).reshape(P, -1)),
        "cols": pack_cols(a),
        "tables": shape_tables(),
        "rows": second_tables(),
        "decays": decay_tables(),
        "pos": np.ascontiguousarray(a["positions"].reshape(-1)),
        "w2": np.concatenate([_twice(w[0].reshape(2, P, 64)[half]) for w in (a["cmp_k_w2_2"], a["cmp_v_w2_2"])
                              for half in range(2)], 1),
    }
    args = {n: nc.dram_tensor(n, v.shape, mybir.dt.from_np(v.dtype), kind="ExternalInput").ap()
            for n, v in data.items()}
    out = nc.dram_tensor("out", (P, KT * S), F32, kind="ExternalOutput").ap()
    build_program(nc, **args, out=out)
    got = run_bass_kernel_spmd(nc, [data], core_ids=[0]).results[0]["out"]
    return np.ascontiguousarray(got.reshape(P, KT, S).transpose(2, 1, 0).reshape(1, S, D))
```

```python
from contextlib import ExitStack

import numpy as np

import concourse.bass as bass
from concourse import mybir

P = 128
D = 1024
S = 512
KT = D // P
TB = S // P
FF = 2816
FT = FF // P
RING = 4
LOOKAHEAD = 2
CW = KT * P
EPS = 1e-6
GN_EPS = 1e-5
OFF = [P * (b * (b + 1) // 2) for b in range(TB + 1)]
KOFF = [sum(S - P * j for j in range(b)) for b in range(TB + 1)]
ALU = mybir.AluOpType
ACT = mybir.ActivationFunctionType
AX = mybir.AxisListType
F32 = mybir.dt.float32
F32R = mybir.dt.float32r
I32 = mybir.dt.int32

TWO_PI = [6.28125, 0.00193023681640625, 5.0703634e-06, 2 * np.pi]
MAGIC = 12582912.0
PI_BELOW = 3.1415925
HALF_PI = float(np.float32(np.pi / 2))
SWAP16 = [(n + 16) % 32 for n in range(32)]
SWAP8 = [n + 8 if n < 8 else n - 8 if n < 16 else n for n in range(32)]

STAGES = [
    ("b1_qk", 8), ("b1_v", 4), ("b1_fk", 1), ("b1_c", 3), ("b1_up", 4),
    ("b1_merge", 24), ("b1_out", 8), ("f0_in", 2 * FT), ("f0_down", FT),
    ("f1_in", 2 * FT), ("f1_down", FT),
    ("b2_qk", 12), ("b2_cmp", 4), ("b2_v", 2), ("b2_g", 1), ("b2_w1", 8), ("b2_rqk", 8), ("b2_rv", 8),
    ("b2_gr", 8), ("b2_merge", 32), ("b2_out", 8), ("f2_in", 2 * FT), ("f2_down", FT),
]
FIRST = {}
_n = 0
for _name, _count in STAGES:
    FIRST[_name] = _n
    _n += _count
CHUNKS = _n

COLS = {}
_n = 0
for _name, _count in [("mix1", 8), ("qa", 2), ("kva", 1), ("bgate", 16), ("ffn0", 8), ("fin1", 8), ("ffn1", 8),
                      ("mix2", 8), ("ret", 8), ("ffn2", 8), ("fin2", 8), ("freq", 1), ("pos", 16), ("bf", 8),
                      ("sgn", 1), ("eps", 1),
                      ("one", 1), ("gneps", 1)]:
    COLS[_name] = _n
    _n += _count
NCOLS = _n


def build_program(nc, stream, xt, cols, tables, rows, decays, pos, w2, out):
    top = ExitStack()
    with top:
        origin = -(-nc.sbuf_base // 32) * 32
        top.enter_context(nc.sbuf_tensor("arena", [P, (nc.sbuf_top - nc.sbuf_base) // 4 - 16], F32))

        def sb(name, shape, dt, at):
            assert origin + at + 4 * int(np.prod(shape[1:])) <= nc.sbuf_usable_end, name
            return nc.alloc_sbuf_tensor_at(name, shape, dt, offset=origin + at)

        def sem(name):
            return top.enter_context(nc.semaphore(name))

        K = 1024
        T2 = 2 * K
        w_raw = sb("w_raw", [P, 2, CW], F32, 0)
        w_hi = sb("w_hi", [P, RING, CW], F32R, 8 * K)
        w_lo = sb("w_lo", [P, RING, CW], F32R, 24 * K)
        x = sb("x", [P, KT, S], F32, 40 * K)
        xn_hi = sb("xn_hi", [P, KT, S], F32R, 56 * K)
        xn_lo = sb("xn_lo", [P, KT, S], F32R, 72 * K)
        ident = sb("ident", [P, P], F32, 88 * K)
        ones = sb("ones", [P, P], F32, 88 * K + 512)
        col = sb("col", [P, P], F32, 89 * K)
        cumul = sb("cumul", [P, S], F32R, 90 * K)
        bias_tri = sb("bias_tri", [P, S], F32, 92 * K)
        bias_chunk = sb("bias_chunk", [P, S], F32, 94 * K)
        norm_r = sb("norm_r", [P, S], F32, 96 * K)
        small = sb("small", [P, 128], F32, 98 * K)
        w2_sb = sb("w2_sb", [P, 4, P], F32, 99 * K)
        A0 = 101 * K
        N0 = 199 * K
        cumul_raw = sb("cumul_raw", [P, S], F32, 195 * K)
        sq = sb("sq", [P, 2, S], F32, N0)
        xg = sb("xg", [P, 2, S], F32, N0 + 4 * K)
        h_hi = sb("h_hi", [P, FT * S], F32R, A0)
        h_lo = sb("h_lo", [P, FT * S], F32R, A0 + 44 * K)
        silu = sb("silu", [P, 2, S], F32, A0 + 88 * K)
        hid = sb("hid", [P, 2, S], F32, A0 + 92 * K)

        banks = [top.enter_context(nc.psum_tensor(f"bank{b}", [P, S], F32)) for b in range(8)]

        loaded = [sem("w_loaded0"), sem("w_loaded1")]
        split_hi = sem("w_split_hi")
        split_lo = sem("w_split_lo")
        used = sem("chunks_used")
        consts_in = sem("consts_in")
        consts_made = sem("consts_made")
        x_in = sem("x_in")
        passed = sem("passed")
        stored = sem("stored")

        def place(first, j, i=0, n=0):
            c = first + j
            return c // RING + i * (n // RING), c % RING

        def high_part(act, ring, slot):
            act.wait_ge(loaded[slot % 2], 32 * ring + 16 * (slot // 2 + 1))
            act.wait_ge(used, RING * ring + (slot + 1))
            nc.scalar.activation(w_hi[:, slot, :], w_raw[:, slot % 2, :], ACT.Copy).then_inc(split_hi, 1)

        def low_part(dve, ring, slot):
            dve.wait_ge(split_hi, RING * ring + (slot + 1))
            nc.vector.tensor_tensor(w_lo[:, slot, :], w_raw[:, slot % 2, :], w_hi[:, slot, :],
                                    ALU.subtract).then_inc(split_lo, 1)

        def ahead(part, eng, first, j, i=0, n=0):
            if n or first + j + LOOKAHEAD < CHUNKS:
                part(eng, *place(first, j + LOOKAHEAD, i, n))

        def apart(eng):
            eng.sem_inc(passed, 1)

        def finished(eng, first, j, i=0, n=0):
            ring, slot = place(first, j, i, n)
            eng.wait_ge(used, RING * ring + (slot + 1 + RING))

        def ready(pe, first, j, i=0, n=0):
            ring, slot = place(first, j, i, n)
            pe.wait_ge(split_lo, RING * ring + (slot + 1))
            return slot

        def mm3(to, a_hi, a_lo, b_hi, b_lo, start=True, stop=True):
            nc.tensor.matmul(to, a_hi, b_hi, start=start, stop=False, skip_group_check=True)
            nc.tensor.matmul(to, a_hi, b_lo, start=False, stop=False, skip_group_check=True)
            return nc.tensor.matmul(to, a_lo, b_hi, start=False, stop=stop, skip_group_check=True)

        def tile_chunk(slot, to, b_hi, b_lo, at=0, tiles=KT):
            for k in range(tiles):
                last = mm3(to, w_hi[:, slot, (at + k) * P:(at + k + 1) * P], w_lo[:, slot, (at + k) * P:(at + k + 1) * P],
                           b_hi[:, k, :], b_lo[:, k, :], k == 0, k == tiles - 1)
            return last

        norm_sems = {k: sem(f"norm_{k}") for k in ("squared", "summed", "root", "recip", "scaled", "hi", "lo")}
        norms = {"tiles": 0, "split": 0, "count": 0}

        def norm(name, src, order, gain, source_done, bank, width, dst=None, dma=False):
            s = norm_sems
            count = len(order)
            tiles, parts_made, before = norms["tiles"], norms["split"], norms["count"]
            norms["tiles"] += count
            norms["split"] += count if dst else 0
            norms["count"] += 1

            def act_part(act):
                for n, k in enumerate(order):
                    act.wait_ge(source_done[0], source_done[1] + (0 if dma else n))
                    if n >= 2:
                        act.wait_ge(s["summed"], tiles + n - 1)
                    nc.scalar.activation(sq[:, n % 2, :], src[:, k, :], ACT.Square).then_inc(s["squared"], 1)
                act.wait_ge(s["summed"], tiles + count)
                nc.scalar.activation(norm_r[:], banks[bank][:], ACT.Sqrt, bias=col[:, COLS["eps"]:COLS["eps"] + 1],
                                     scale=1.0 / width).then_inc(s["root"], 1)
                if dst:
                    for n, k in enumerate(order):
                        act.wait_ge(s["scaled"], tiles + n + 1)
                        nc.scalar.activation(dst[0][:, k, :], xg[:, n % 2, :], ACT.Copy).then_inc(s["hi"], 1)

            def pe_part(pe):
                for n in range(count):
                    pe.wait_ge(s["squared"], tiles + n + 1)
                    nc.tensor.matmul(banks[bank][:], ones[:], sq[:, n % 2, :], start=n == 0,
                                     stop=n == count - 1).then_inc(s["summed"], 1)

            def dve_part(dve):
                dve.wait_ge(s["root"], before + 1)
                nc.vector.reciprocal(norm_r[:], norm_r[:]).then_inc(s["recip"], 1)
                dve.wait_ge(s["recip"], before + 1)
                for n, k in enumerate(order):
                    if dst and n >= 2:
                        dve.wait_ge(s["lo"], parts_made + n - 1)
                    to = xg[:, n % 2, :] if dst else src[:, k, :]
                    nc.vector.scalar_tensor_tensor(to, src[:, k, :], col[:, gain + k:gain + k + 1], norm_r[:],
                                                   ALU.mult, ALU.mult).then_inc(s["scaled"], 1)

            def pool_part(pool):
                if dst:
                    for n, k in enumerate(order):
                        pool.wait_ge(s["hi"], parts_made + n + 1)
                        nc.gpsimd.tensor_tensor(dst[1][:, k, :], xg[:, n % 2, :], dst[0][:, k, :],
                                                ALU.subtract).then_inc(s["lo"], 1)

            done = (s["lo"], parts_made + count) if dst else (s["scaled"], tiles + count)
            return act_part, pe_part, dve_part, pool_part, done

        ORDER = [7, 0, 1, 2, 3, 4, 5, 6]

        ffn_sems = {k: sem(f"ffn_{k}") for k in ("silu", "product", "hi", "lo", "x")}
        ffns = [0]

        def feed_forward(name, factor, norm_done):
            first_in, first_down = FIRST[f"{name}_in"], FIRST[f"{name}_down"]
            s = ffn_sems
            first_one, b = ffns[0] == 0, FT * ffns[0]
            x_before = KT * ffns[0]
            ffns[0] += 1
            N_IN, N_DOWN = 4, 4

            def pe_part(pe):
                pe.wait_ge(*norm_done)
                with pe.Fori(0, FT // 2) as i:
                    for j in range(4):
                        slot = ready(pe, first_in, j, i, N_IN)
                        if j % 2 == 0:
                            pe.wait_ge(s["product"], 2 * i + (b + j // 2 + 1))
                        tile_chunk(slot, banks[j][:], xn_hi, xn_lo).then_inc(used, 1)

                def down(j, k, start, stop, i=0, n=0):
                    pe.wait_ge(s["lo"], k + (b + 3))
                    slot = ready(pe, first_down, j, i, n)
                    for o in (4, 5, 6, 7, 0, 1, 2, 3):
                        w = slice(o * P, (o + 1) * P)
                        last = mm3(banks[o][:], w_hi[:, slot, w], w_lo[:, slot, w], h_hi[:, bass.ds(k * S, S)],
                                   h_lo[:, bass.ds(k * S, S)], start, stop)
                    last.then_inc(used, 1)

                pe.wait_ge(s["product"], b + FT + 2)
                for j in range(4):
                    down(j, j, j == 0, False)
                with pe.Fori(0, FT // 4 - 1) as i:
                    for j in range(4):
                        down(j + 4, i * 4 + (j + 4), False, False, i, N_DOWN)
                for j in range(FT // 4 * 4, FT):
                    down(j, j, False, j == FT - 1)

            def act_part(act):
                with act.Fori(0, FT // 2) as i:
                    for t in range(2):
                        ahead(high_part, act, first_in, 2 * t, i, N_IN)
                        finished(act, first_in, 2 * t, i, N_IN)
                        act.wait_ge(s["product"], 2 * i + (b + t + 1))
                        nc.scalar.activation(silu[:, t, :], banks[2 * t][:], ACT.Silu).then_inc(s["silu"], 1)
                        ahead(high_part, act, first_in, 2 * t + 1, i, N_IN)
                        act.wait_ge(s["product"], 2 * i + (b + t + 3))
                        nc.scalar.activation(h_hi[:, bass.ds(i * 2 * S + t * S, S)], hid[:, t, :],
                                             ACT.Copy).then_inc(s["hi"], 1)
                stream_down(act, high_part)

            def stream_down(eng, part):
                with eng.Fori(0, FT // 4) as i:
                    for j in range(4):
                        ahead(part, eng, first_down, j, i, N_DOWN)
                for j in range(FT // 4 * 4, FT):
                    ahead(part, eng, first_down, j)

            def dve_part(dve):
                if first_one:
                    dve.sem_inc(s["product"], 2)
                with dve.Fori(0, FT // 2) as i:
                    for t in range(2):
                        ahead(low_part, dve, first_in, 2 * t, i, N_IN)
                        ahead(low_part, dve, first_in, 2 * t + 1, i, N_IN)
                        dve.wait_ge(s["silu"], 2 * i + (b + t + 1))
                        dve.wait_ge(s["lo"], 2 * i + (b + t + 1))
                        finished(dve, first_in, 2 * t + 1, i, N_IN)
                        nc.vector.tensor_tensor(hid[:, t, :], silu[:, t, :], banks[2 * t + 1][:],
                                                ALU.mult).then_inc(s["product"], 1)
                stream_down(dve, low_part)
                finished(dve, first_down, FT - 1)
                for k in ORDER:
                    nc.vector.scalar_tensor_tensor(x[:, k, :], banks[k][:], factor, x[:, k, :],
                                                   ALU.mult, ALU.add).then_inc(s["x"], 1)

            def pool_part(pool):
                if first_one:
                    pool.sem_inc(s["lo"], 2)
                with pool.Fori(0, FT // 2) as i:
                    for t in range(2):
                        pool.wait_ge(s["hi"], 2 * i + (b + t + 1))
                        nc.gpsimd.tensor_tensor(h_lo[:, bass.ds(i * 2 * S + t * S, S)], hid[:, t, :],
                                                h_hi[:, bass.ds(i * 2 * S + t * S, S)],
                                                ALU.subtract).then_inc(s["lo"], 1)

            return act_part, pe_part, dve_part, pool_part, (s["x"], x_before + 1)

        parts = []

        def link(eng, s):
            count = [0]

            def step(instruction):
                instruction.then_inc(s, 1)
                count[0] += 1
                eng.wait_ge(s, count[0])
            return step

        def skip(eng):
            pass

        W0 = A0 + 68 * K
        qs_hi = sb("qs_hi", [P, S], F32R, W0)
        qs_lo = sb("qs_lo", [P, S], F32R, W0 + T2)
        ks_hi = sb("ks_hi", [P, S], F32R, W0 + 2 * T2)
        ks_lo = sb("ks_lo", [P, S], F32R, W0 + 3 * T2)
        vs_hi = sb("vs_hi", [P, TB, P], F32R, W0 + 4 * T2)
        vs_lo = sb("vs_lo", [P, TB, P], F32R, W0 + 5 * T2)
        prob = sb("prob", [P, 2, OFF[TB]], F32, W0 + 6 * T2)
        pt_hi = sb("pt_hi", [P, OFF[TB]], F32R, W0 + 22 * K)
        pt_lo = sb("pt_lo", [P, OFF[TB]], F32R, W0 + 27 * K)
        bias_row = sb("bias_row", [P, S], F32, W0 + 34 * K)
        ident_r = sb("ident_r", [P, P], F32R, W0 + 32 * K)
        tri_r = sb("tri_r", [P, P], F32R, W0 + 32 * K + 512)
        top_s, neg_top, total, inverse = (small[:, 8 * n:8 * n + 8] for n in range(4))

        def scores_rows(qb):
            return slice(OFF[qb], OFF[qb + 1])

        def turns(eng, count, body):
            with eng.Fori(0, count - 1) as i:
                body(i, True)
            body(count - 1, False)

        def attention(name, start, q_raw, k_raw, v_raw, y, y_tile, scale, latent):
            s = {k: sem(f"{name}_{k}") for k in ("staged_hi", "staged_lo", "v_hi", "v_lo", "scored", "biased", "negated",
                                                 "exp", "inverse", "scaled", "turned", "hi", "lo", "summed", "out",
                                                 "bias", "mask")}
            rows = [slice(0, P)] * 2 if latent else [slice(0, 64), slice(64, P)]
            krows = slice(0, 64) if latent else slice(0, P)
            pairs = 4

            def begin(eng):
                for w in start:
                    eng.wait_ge(*w)

            def pe_part(pe):
                begin(pe)
                pe.sem_inc(s["scored"], 4)
                pe.sem_inc(s["turned"], 8)
                pe.sem_inc(s["summed"], 4)
                if not latent:
                    pe.wait_ge(s["mask"], 2)

                def score(i, j):
                    if latent:
                        pe.wait_ge(s["staged_lo"], 4 * i + 2 * (j + 1))
                    elif j % 2 == 0:
                        pe.wait_ge(s["staged_lo"], 2 * i + (j + 2))
                    r = rows[j % 2]
                    for qb in range(TB):
                        pe.wait_ge(s["biased"], 8 * i + (4 * j + qb + 1))
                        at, n = slice(qb * P, (qb + 1) * P), (qb + 1) * P
                        last = mm3(banks[qb][:, 0:n], qs_hi[r, at], qs_lo[r, at], ks_hi[r, 0:n], ks_lo[r, 0:n], True,
                                   latent)
                        if not latent:
                            last = nc.tensor.matmul(banks[qb][:, qb * P:n], ident_r[:], tri_r[:], start=False,
                                                    stop=True, skip_group_check=True)
                        last.then_inc(s["scored"], 1)

                def turn(i, j, kb):
                    pe.wait_ge(s["lo"], 8 * i + (4 * j + kb + 1))
                    for qb in range(kb, TB):
                        if kb == 0:
                            pe.wait_ge(s["scaled"], 8 * i + (4 * j + qb + 1))
                        last = nc.tensor.transpose(banks[4 + kb % 2][:, (qb - kb) * P:(qb - kb + 1) * P],
                                                   prob[:, j, OFF[qb] + kb * P:OFF[qb] + (kb + 1) * P], ident[:])
                    last.then_inc(s["turned"], 1)

                def values(i, j, kb):
                    if kb == 0:
                        pe.wait_ge(s["out"], 2 * i + (j + 1))
                        pe.wait_ge(s["v_lo"], i + 1)
                    pe.wait_ge(s["lo"], 8 * i + (4 * j + kb + 3))
                    at = slice(KOFF[kb], KOFF[kb + 1])
                    mm3(banks[6 + j][:, kb * P:S], vs_hi[:, kb, :], vs_lo[:, kb, :], pt_hi[:, at], pt_lo[:, at],
                        kb == 0, kb == TB - 1).then_inc(s["summed"], 1)

                def body(i, more):
                    for j in range(2):
                        for kb in range(TB):
                            turn(i, j, kb)
                        if more:
                            score(i, j + 2)
                        for kb in range(TB):
                            values(i, j, kb)

                score(0, 0)
                score(0, 1)
                turns(pe, pairs, body)

            def act_part(act):
                begin(act)
                act.sem_inc(s["out"], 2)

                def stage(i, j):
                    tile = 2 * i + j if latent else i + j // 2
                    act.wait_ge(s["scored"], 8 * i + (4 * j + 4))
                    nc.scalar.activation(qs_hi[:], q_raw[:, tile, :], ACT.Copy).then_inc(s["staged_hi"], 1)
                    nc.scalar.activation(ks_hi[krows, :], k_raw[krows, tile, :], ACT.Copy).then_inc(s["staged_hi"], 1)

                def stage_v(i, n):
                    act.wait_ge(s["summed"], 8 * i + (8 * n + 4))
                    nc.scalar.activation(vs_hi[:], v_raw[:, :, bass.ds(i * P + n * P, P)], ACT.Copy).then_inc(s["v_hi"], 1)

                def exps(i, j, blocks):
                    act.wait_ge(s["negated"], 2 * i + (j + 1))
                    for qb in blocks:
                        at = prob[:, j % 2, scores_rows(qb)]
                        n = 4 * (j % 2) + qb
                        nc.scalar.activation(at, at, ACT.Exp, bias=neg_top[:, n:n + 1], scale=scale,
                                             accum_out=total[:, n:n + 1]).then_inc(s["exp"], 1)

                def highs(i, j, blocks):
                    for kb in blocks:
                        act.wait_ge(s["turned"], 8 * i + (4 * j + kb + 9))
                        act.wait_ge(s["summed"], 8 * i + (4 * j + kb + 1))
                        nc.scalar.activation(pt_hi[:, KOFF[kb]:KOFF[kb + 1]], banks[4 + kb % 2][:, 0:S - kb * P],
                                             ACT.Copy).then_inc(s["hi"], 1)

                def output(i, j):
                    act.wait_ge(s["summed"], 8 * i + (4 * j + 8))
                    r = slice(64 * j, 64 * j + 64)
                    nc.scalar.activation(y[r, i + y_tile, :], banks[6 + j][r, :], ACT.Copy).then_inc(s["out"], 1)

                def body(i, more):
                    for j in range(2):
                        if more and (latent or j == 0):
                            stage(i, j + 2)
                        highs(i, j, (0, 1))
                        if j == 0 or more:
                            exps(i, j + 1, (0, 1, 2))
                        highs(i, j, (2, 3))
                        if j == 0 or more:
                            exps(i, j + 1, (3,))
                        output(i, j)
                    if more:
                        stage_v(i, 1)

                stage(0, 0)
                stage_v(0, 0)
                if latent:
                    stage(0, 1)
                exps(0, 0, range(TB))
                turns(act, pairs, body)

            def dve_part(dve):
                begin(dve)
                dve.sem_inc(s["biased"], 4)
                dve.sem_inc(s["lo"], 2)

                def biased(i, j):
                    if not latent:
                        dve.wait_ge(s["bias"], 2 * i + (j + 1))
                    for qb in range(TB):
                        dve.wait_ge(s["scored"], 8 * i + (4 * j + qb + 5))
                        if qb == 0:
                            dve.wait_ge(s["turned"], 8 * i + (4 * j + 4))
                        apart(dve)
                        n = 4 * (j % 2) + qb
                        width = (qb + 1) * P
                        bias = bias_chunk[:, S - width:S] if latent else bias_row[:, 0:width]
                        nc.vector.tensor_tensor_reduce(prob[:, j % 2, scores_rows(qb)], banks[qb][:, 0:width], bias, 1.0,
                                                       -3.0e38, ALU.add, ALU.max,
                                                       top_s[:, n:n + 1]).then_inc(s["biased"], 1)
                    dve.wait_ge(s["biased"], 8 * i + (4 * j + 8))
                    n = 4 * (j % 2)
                    nc.vector.tensor_scalar(neg_top[:, n:n + 4], top_s[:, n:n + 4], -scale, None,
                                            ALU.mult).then_inc(s["negated"], 1)

                def scaled(i, j):
                    dve.wait_ge(s["exp"], 8 * i + (4 * j + 4))
                    nc.vector.reciprocal(inverse[:, 4 * j:4 * j + 4], total[:, 4 * j:4 * j + 4]).then_inc(s["inverse"], 1)
                    dve.wait_ge(s["inverse"], 2 * i + (j + 1))
                    for qb in range(TB):
                        at = prob[:, j, scores_rows(qb)]
                        n = 4 * j + qb
                        nc.vector.tensor_scalar(at, at, inverse[:, n:n + 1], None, ALU.mult).then_inc(s["scaled"], 1)

                def lows(i, j):
                    for kb in range(TB):
                        dve.wait_ge(s["hi"], 8 * i + (4 * j + kb + 1))
                        at = slice(KOFF[kb], KOFF[kb + 1])
                        nc.vector.tensor_tensor(pt_lo[:, at], banks[4 + kb % 2][:, 0:S - kb * P], pt_hi[:, at],
                                                ALU.subtract).then_inc(s["lo"], 1)

                def body(i, more):
                    for j in range(2):
                        scaled(i, j)
                        if j == 0 or more:
                            biased(i, j + 1)
                        lows(i, j)

                biased(0, 0)
                turns(dve, pairs, body)

            def pool_part(pool):
                begin(pool)
                if not latent:
                    nc.gpsimd.tensor_copy(ident_r[:], ident[:]).then_inc(s["mask"], 1)
                    nc.gpsimd.tensor_copy(tri_r[:], bias_tri[:, S - P:S]).then_inc(s["mask"], 1)

                def stage(i, j):
                    tile = 2 * i + j if latent else i + j // 2
                    n = 4 * i + 2 * j if latent else 2 * i + j
                    pool.wait_ge(s["staged_hi"], n + 1)
                    nc.gpsimd.tensor_tensor(qs_lo[:], q_raw[:, tile, :], qs_hi[:], ALU.subtract).then_inc(s["staged_lo"], 1)
                    pool.wait_ge(s["staged_hi"], n + 2)
                    nc.gpsimd.tensor_tensor(ks_lo[krows, :], k_raw[krows, tile, :], ks_hi[krows, :],
                                            ALU.subtract).then_inc(s["staged_lo"], 1)

                def stage_v(i, n):
                    pool.wait_ge(s["v_hi"], i + (n + 1))
                    nc.gpsimd.tensor_tensor(vs_lo[:], v_raw[:, :, bass.ds(i * P + n * P, P)], vs_hi[:],
                                            ALU.subtract).then_inc(s["v_lo"], 1)

                def bias(i, j):
                    pool.wait_ge(s["biased"], 8 * i + (4 * j + 4))
                    nc.gpsimd.tensor_copy(bias_row[:], negc[:, 2 * i + j, :]).then_inc(s["bias"], 1)

                def body(i, more):
                    if latent:
                        if more:
                            stage(i, 2)
                            stage(i, 3)
                            stage_v(i, 1)
                    else:
                        bias(i, 1)
                        if more:
                            stage(i, 2)
                            bias(i, 2)
                            stage_v(i, 1)

                if not latent:
                    bias(0, 0)
                stage(0, 0)
                stage_v(0, 0)
                if latent:
                    stage(0, 1)
                turns(pool, pairs, body)

            return act_part, pe_part, dve_part, pool_part, (s["out"], 2 * pairs + 2)

        qk_raw = sb("qk_raw", [P, 2 * TB, S], F32, A0)
        v_raw = sb("v_raw", [P, TB, S], F32, A0 + 16 * K)
        negc = sb("negc", [P, 8, S], F32, A0 + 24 * K)
        mq = sb("mq", [P, 8, S], F32, A0)
        mk = sb("mk", [P, 8, S], F32, A0 + 16 * K)
        mv = sb("mv", [P, TB, S], F32, A0 + 32 * K)
        c_hi = sb("c_hi", [P, 3, S], F32R, A0 + 40 * K)
        c_lo = sb("c_lo", [P, 3, S], F32R, A0 + 46 * K)
        y1 = sb("y1", [P, KT, S], F32, A0 + 52 * K)
        forget = sb("forget", [8, 4, S], F32, W0)
        lft_hi = sb("lft_hi", [P, 32], F32R, W0 + 8 * K)
        lft_lo = sb("lft_lo", [P, 32], F32R, W0 + 9 * K)
        rope_c = sb("rope_c", [P, S], F32, W0 + 32 * K)
        rope_s = sb("rope_s", [P, S], F32, W0 + 34 * K)
        rope_t = sb("rope_t", [P, 4, S], F32, W0 + 14 * K)
        rope_i = sb("rope_i", [P, S], I32, W0 + 8 * K)
        rope_a = sb("rope_a", [P, S], F32, W0 + 10 * K)
        rope_k = sb("rope_k", [P, S], F32, W0 + 12 * K)

        def copies_out(name, first, count, dst, credit=True):
            s = sem(f"{name}_copied")

            def act_part(act):
                with act.Fori(0, count // 4) as i:
                    for j in range(4):
                        ahead(high_part, act, first, j, i, 4)

            def pe_part(pe):
                with pe.Fori(0, count // 4) as i:
                    for j in range(4):
                        slot = ready(pe, first, j, i, 4)
                        pe.wait_ge(s, 4 * i + (j + 1))
                        tile_chunk(slot, banks[j][:], xn_hi, xn_lo).then_inc(used, 1)

            def dve_part(dve):
                dve.sem_inc(s, 4)
                with dve.Fori(0, count // 4) as i:
                    for j in range(4):
                        ahead(low_part, dve, first, j, i, 4)
                        finished(dve, first, j, i, 4)
                        nc.vector.tensor_copy(dst[:, 4 * i + j, :], banks[j][:]).then_inc(s, 1)

            return act_part, pe_part, dve_part, skip, (s, count + 4)

        def mixer1(norm_done):
            qk = copies_out("b1_qk", FIRST["b1_qk"], 8, qk_raw)
            s = {k: sem(f"b1_{k}") for k in ("v", "fk", "c", "f_dve", "f_act", "lft_t", "lft_hi", "lft_lo", "cum",
                                             "negc")}
            cq = norm("b1_cq", y1, [0, 1], COLS["qa"], (s["c"], 1), 6, 256, (c_hi, c_lo))
            ckv = norm("b1_ckv", y1, [2], COLS["kva"] - 2, (s["c"], 3), 7, 128, (c_hi, c_lo))
            fv, ff, fc = FIRST["b1_v"], FIRST["b1_fk"], FIRST["b1_c"]

            def pe_part(pe):
                pe.wait_ge(*norm_done)
                qk[1](pe)
                for j in range(4):
                    slot = ready(pe, fv, j)
                    for t in range(2):
                        k, w = 2 * j + t, slice(t * S, (t + 1) * S)
                        for tb in range(TB):
                            at = slice(tb * P, (tb + 1) * P)
                            last = mm3(banks[4 + tb][:], xn_hi[:, k, at], xn_lo[:, k, at], w_hi[:, slot, w],
                                       w_lo[:, slot, w], k == 0, k == KT - 1)
                    last.then_inc(used, 1)
                slot = ready(pe, ff, 0)
                pe.wait_ge(qk[4][0], 8 + 1)
                tile_chunk(slot, banks[0][:], xn_hi, xn_lo).then_inc(used, 1)
                for j in range(3):
                    slot = ready(pe, fc, j)
                    pe.wait_ge(qk[4][0], 8 + 2 + j)
                    tile_chunk(slot, banks[1 + j][:], xn_hi, xn_lo).then_inc(used, 1)
                pe.wait_ge(s["f_dve"], 3)
                pe.wait_ge(s["v"], 4)
                for tb in range(TB):
                    last = nc.tensor.transpose(banks[4][:, 8 * tb:8 * tb + 8], forget[0:8, 0, tb * P:(tb + 1) * P],
                                               ident[0:8, 0:8])
                last.then_inc(s["lft_t"], 1)
                cq[1](pe)
                ckv[1](pe)
                pe.wait_ge(s["lft_lo"], 1)
                pe.wait_ge(s["c"], 3)
                pe.wait_ge(s["fk"], 1)
                for h in range(8):
                    if h >= 4:
                        pe.wait_ge(s["negc"], h - 3)
                    for tb in range(TB):
                        for n, part in enumerate((lft_hi, lft_lo)):
                            last = nc.tensor.matmul(banks[h % 4][:, tb * P:S],
                                                    part[:, 8 * tb + h:8 * tb + h + 1].to_broadcast([P, P]),
                                                    cumul[:, 0:S - tb * P], start=tb == 0 and n == 0,
                                                    stop=tb == TB - 1 and n == 1, skip_group_check=True)
                    last.then_inc(s["cum"], 1)

            def act_part(act):
                qk[0](act)
                for j in range(4):
                    ahead(high_part, act, fv, j)
                ahead(high_part, act, ff, 0)
                for j in range(3):
                    ahead(high_part, act, fc, j)
                act.wait_ge(s["f_dve"], 2)
                nc.scalar.activation(forget[0:8, 2, :], forget[0:8, 1, :], ACT.Exp).then_inc(s["f_act"], 1)
                act.wait_ge(s["f_act"], 1)
                nc.scalar.activation(forget[0:8, 3, :], forget[0:8, 2, :], ACT.Ln,
                                     bias=col[0:8, COLS["one"]:COLS["one"] + 1]).then_inc(s["f_act"], 1)
                act.wait_ge(s["lft_t"], 1)
                nc.scalar.activation(lft_hi[:], banks[4][:, 0:32], ACT.Copy).then_inc(s["lft_hi"], 1)
                cq[0](act)
                ckv[0](act)

            def dve_part(dve):
                qk[2](dve)
                for j in range(4):
                    ahead(low_part, dve, fv, j)
                finished(dve, fv, 3)
                for tb in range(TB):
                    nc.vector.tensor_copy(v_raw[:, tb, :], banks[4 + tb][:]).then_inc(s["v"], 1)
                ahead(low_part, dve, ff, 0)
                finished(dve, ff, 0)
                nc.vector.tensor_scalar(forget[0:8, 0, :], banks[0][0:8, :], col[0:8, COLS["bf"]:COLS["bf"] + 1], None,
                                        ALU.add).then_inc(s["f_dve"], 1)
                nc.vector.tensor_copy(y1[64:96, 7, :], banks[0][64:96, :]).then_inc(s["fk"], 1)
                dve.wait_ge(s["f_dve"], 1)
                nc.vector.scalar_tensor_tensor(forget[0:8, 1, :], forget[0:8, 0, :], -1.0, forget[0:8, 0, :], ALU.mult,
                                               ALU.min).then_inc(s["f_dve"], 1)
                for j in range(3):
                    ahead(low_part, dve, fc, j)
                    finished(dve, fc, j)
                    nc.vector.tensor_copy(y1[:, j, :], banks[1 + j][:]).then_inc(s["c"], 1)
                dve.wait_ge(s["f_act"], 2)
                nc.vector.scalar_tensor_tensor(forget[0:8, 0, :], forget[0:8, 0, :], 0.0, forget[0:8, 3, :], ALU.min,
                                               ALU.subtract).then_inc(s["f_dve"], 1)
                dve.wait_ge(s["lft_hi"], 1)
                nc.vector.tensor_tensor(lft_lo[:], banks[4][:, 0:32], lft_hi[:], ALU.subtract).then_inc(s["lft_lo"], 1)
                cq[2](dve)
                dve.wait_ge(*cq[4])
                ckv[2](dve)
                for h in range(8):
                    dve.wait_ge(s["cum"], h + 1)
                    nc.vector.tensor_copy(negc[:, h, :], banks[h % 4][:]).then_inc(s["negc"], 1)

            def pool_part(pool):
                cq[3](pool)
                ckv[3](pool)

            front = (act_part, pe_part, dve_part, pool_part)
            att = attention("b1_a", [(s["negc"], 8), (s["v"], 4), ckv[4], cq[4], qk[4]], qk_raw, qk_raw[:, 4:8, :],
                            v_raw, y1, 0, 0.125, False)

            fu = FIRST["b1_up"]
            u = {k: sem(f"b1_up_{k}") for k in ("copied", "v", "rope_dve", "rope_act", "rope_pool", "kr_hi", "ready",
                                                "pos")}

            def up_pe(pe):
                pe.wait_ge(*att[4])
                for j in range(4):
                    slot = ready(pe, fu, j)
                    if j < 3:
                        for n in range(4 if j < 2 else 8):
                            g = 4 * j + n
                            if g >= 4:
                                pe.wait_ge(u["copied"], g - 3)
                            if j < 2:
                                last = tile_chunk(slot, banks[g % 4][:], c_hi, c_lo, 2 * n, 2)
                            else:
                                w = slice(n * P, (n + 1) * P)
                                last = mm3(banks[g % 4][:], w_hi[:, slot, w], w_lo[:, slot, w], c_hi[:, 2, :],
                                           c_lo[:, 2, :])
                            last.then_inc(u["ready"] if n < (3 if j < 2 else 7) else used, 1)
                    else:
                        for tb in range(TB):
                            at = slice(tb * P, (tb + 1) * P)
                            last = mm3(banks[4 + tb][:], c_hi[:, 2, at], c_lo[:, 2, at], w_hi[:, slot, 0:S],
                                       w_lo[:, slot, 0:S])
                        last.then_inc(used, 1)

            def up_act(act):
                for j in range(4):
                    ahead(high_part, act, fu, j)
                act.wait_ge(u["rope_dve"], 8)
                nc.scalar.activation(rope_s[64:96, :], rope_a[64:96, :], ACT.Sin).then_inc(u["rope_act"], 1)
                act.wait_ge(u["rope_dve"], 10)
                nc.scalar.activation(rope_c[64:96, :], rope_k[64:96, :], ACT.Sin).then_inc(u["rope_act"], 1)
                act.wait_ge(u["rope_dve"], 14)
                nc.scalar.activation(ks_hi[64:96, :], y1[64:96, 7, :], ACT.Copy).then_inc(u["kr_hi"], 1)

            def up_dve(dve):
                dve.wait_ge(*att[4])
                r = slice(64, 96)
                c = [0]

                def step(instruction):
                    instruction.then_inc(u["rope_dve"], 1)
                    c[0] += 1
                    dve.wait_ge(u["rope_dve"], c[0])

                dve.wait_ge(u["pos"], 16)
                step(nc.vector.tensor_copy(rope_a[r, :], rope_i[r, :]))
                step(nc.vector.tensor_scalar(rope_a[r, :], rope_a[r, :], col[r, COLS["freq"]:COLS["freq"] + 1], None,
                                             ALU.mult))
                step(nc.vector.tensor_scalar(rope_k[r, :], rope_a[r, :], 1.0 / TWO_PI[3], MAGIC, ALU.mult, ALU.add))
                step(nc.vector.tensor_scalar(rope_k[r, :], rope_k[r, :], MAGIC, None, ALU.subtract))
                for part in TWO_PI[:3]:
                    step(nc.vector.scalar_tensor_tensor(rope_a[r, :], rope_k[r, :], -part, rope_a[r, :], ALU.mult,
                                                        ALU.add))
                step(nc.vector.tensor_scalar(rope_a[r, :], rope_a[r, :], -PI_BELOW, PI_BELOW, ALU.max, ALU.min))
                step(nc.vector.scalar_tensor_tensor(rope_k[r, :], rope_a[r, :], -1.0, rope_a[r, :], ALU.mult, ALU.max))
                step(nc.vector.tensor_scalar(rope_k[r, :], rope_k[r, :], -1.0, HALF_PI, ALU.mult, ALU.add))
                for j in range(3):
                    ahead(low_part, dve, fu, j)
                    for n in range(4 if j < 2 else 8):
                        g = 4 * j + n
                        if n < (3 if j < 2 else 7):
                            dve.wait_ge(u["ready"], g + 1 - j)
                        else:
                            finished(dve, fu, j)
                        to = mq[:, g, :] if g < 8 else mk[:, g - 8, :]
                        nc.vector.tensor_copy(to, banks[g % 4][:]).then_inc(u["copied"], 1)
                ahead(low_part, dve, fu, 3)
                finished(dve, fu, 3)
                for tb in range(TB):
                    nc.vector.tensor_copy(mv[:, tb, :], banks[4 + tb][:]).then_inc(u["v"], 1)
                dve.wait_ge(u["copied"], 16)
                dve.wait_ge(u["rope_act"], 2)
                step(nc.vector.tensor_scalar(rope_s[r, :], rope_s[r, :], col[r, COLS["sgn"]:COLS["sgn"] + 1], None,
                                             ALU.mult))
                step(nc.vector.stream_shuffle(rope_t[r, 0, :], y1[r, 7, :], SWAP16))
                nc.vector.tensor_tensor(rope_t[r, 0, :], rope_t[r, 0, :], rope_s[r, :], ALU.mult)
                step(nc.vector.tensor_tensor(y1[r, 7, :], y1[r, 7, :], rope_c[r, :], ALU.mult))
                step(nc.vector.tensor_tensor(y1[r, 7, :], y1[r, 7, :], rope_t[r, 0, :], ALU.add))
                dve.wait_ge(u["kr_hi"], 1)
                step(nc.vector.tensor_tensor(ks_lo[r, :], y1[r, 7, :], ks_hi[r, :], ALU.subtract))
                for b in range(2):
                    q = mq[r, 4 * b:4 * b + 4, :]
                    step(nc.vector.stream_shuffle(rope_t[r, :, :], q, SWAP16))
                    table = [t[r, :].rearrange("p (o s) -> p o s", o=1).to_broadcast([32, 4, S]) for t in (rope_c, rope_s)]
                    nc.vector.tensor_tensor(rope_t[r, :, :], rope_t[r, :, :], table[1], ALU.mult)
                    step(nc.vector.tensor_tensor(q, q, table[0], ALU.mult))
                    step(nc.vector.tensor_tensor(q, q, rope_t[r, :, :], ALU.add))

            def up_pool(pool):
                pool.wait_ge(*att[4])
                pool.dma_start(rope_i[64:96, :], pos.partition_broadcast(32)).then_inc(u["pos"], 16)
                nc.gpsimd.memset(ks_hi[96:P, :].bitcast(F32), 0.0).then_inc(u["rope_pool"], 1)
                nc.gpsimd.memset(ks_lo[96:P, :].bitcast(F32), 0.0).then_inc(u["rope_pool"], 1)

            up = (up_act, up_pe, up_dve, up_pool)
            lat = attention("b1_b", [(u["rope_dve"], 21), (u["copied"], 16), (u["v"], 4), (u["rope_pool"], 2)], mq, mk,
                            mv, y1, 4, 96.0 ** -0.5, True)
            return front, att, up, lat

        def merge(name, start, m_hi, m_lo, temps, branches, per, bias):
            s = {k: sem(f"{name}_merge_{k}") for k in ("y_hi", "y_lo", "gate", "gated", "sum", "hi", "lo", "x")}
            fm, fo = FIRST[f"{name}_merge"], FIRST[f"{name}_out"]
            turns = 4 if per == 3 else 2
            N = per * turns
            ny = sum(b[3].shape[1] for b in branches)

            def pe_part(pe):
                for w in start:
                    pe.wait_ge(*w)
                with pe.Fori(0, KT // turns) as i:
                    for t in range(turns):
                        base = 4 * (t % 2)
                        for g in range(2):
                            slot = ready(pe, fm, per * t + g, i, N)
                            if g == 0:
                                pe.wait_ge(s["gated"], 2 * turns * i + 2 * (t + 1))
                            tile_chunk(slot, banks[base + g][:], xn_hi, xn_lo).then_inc(used, 1)
                        pe.wait_ge(s["y_lo"], ny)
                        for chunk, at, bank, raw, y_hi, y_lo in branches:
                            tiles = raw.shape[1]
                            slot = ready(pe, fm, per * t + chunk, i, N)
                            last = tile_chunk(slot, banks[base + bank][:], y_hi, y_lo, at, tiles)
                            if at + tiles == KT:
                                last.then_inc(used, 1)
                with pe.Fori(0, 2) as i:
                    for j in range(4):
                        slot = ready(pe, fo, j, i, 4)
                        if j == 0:
                            pe.wait_ge(s["lo"], KT + 2)
                            pe.wait_ge(s["gated"], 2 * KT + 4)
                        pe.wait_ge(s["x"], 4 * i + (j + 1))
                        tile_chunk(slot, banks[j][:], m_hi, m_lo).then_inc(used, 1)

            def act_part(act):
                for w in start:
                    act.wait_ge(*w)
                for _, _, _, raw, y_hi, _ in branches:
                    for k in range(raw.shape[1]):
                        nc.scalar.activation(y_hi[:, k, :], raw[:, k, :], ACT.Copy).then_inc(s["y_hi"], 1)
                with act.Fori(0, KT // turns) as i:
                    for t in range(turns):
                        for g in range(2):
                            ahead(high_part, act, fm, per * t + g, i, N)
                            finished(act, fm, per * t + g, i, N)
                            act.wait_ge(s["lo"], turns * i + (t + 1))
                            if bias is None:
                                nc.scalar.activation(temps[:, t % 2, g, :], banks[4 * (t % 2) + g][:],
                                                     ACT.Sigmoid).then_inc(s["gate"], 1)
                            else:
                                nc.scalar.activation(temps[:, t % 2, g, :], banks[4 * (t % 2) + g][:], ACT.Sigmoid,
                                                     bias=col[:, bass.ds(i * turns + (bias + g * KT + t), 1)]
                                                     ).then_inc(s["gate"], 1)
                        for c in range(2, per):
                            ahead(high_part, act, fm, per * t + c, i, N)
                        act.wait_ge(s["sum"], turns * i + (t + 1))
                        nc.scalar.activation(m_hi[:, i * turns + t, :], temps[:, t % 2, 0, :],
                                             ACT.Copy).then_inc(s["hi"], 1)
                with act.Fori(0, 2) as i:
                    for j in range(4):
                        ahead(high_part, act, fo, j, i, 4)

            def dve_part(dve):
                for w in start:
                    dve.wait_ge(*w)
                dve.sem_inc(s["gated"], 4)
                tile = 0
                for _, _, _, raw, y_hi, y_lo in branches:
                    for k in range(raw.shape[1]):
                        tile += 1
                        dve.wait_ge(s["y_hi"], tile)
                        nc.vector.tensor_tensor(y_lo[:, k, :], raw[:, k, :], y_hi[:, k, :],
                                                ALU.subtract).then_inc(s["y_lo"], 1)
                with dve.Fori(0, KT // turns) as i:
                    for t in range(turns):
                        for c in range(per):
                            ahead(low_part, dve, fm, per * t + c, i, N)
                        dve.wait_ge(s["gate"], 2 * turns * i + 2 * (t + 1))
                        finished(dve, fm, per * t + per - 1, i, N)
                        for g in range(2):
                            nc.vector.tensor_tensor(temps[:, t % 2, g, :], temps[:, t % 2, g, :],
                                                    banks[4 * (t % 2) + 2 + g][:], ALU.mult).then_inc(s["gated"], 1)
                dve.sem_inc(s["x"], 4)
                with dve.Fori(0, 2) as i:
                    for j in range(4):
                        ahead(low_part, dve, fo, j, i, 4)
                        finished(dve, fo, j, i, 4)
                        nc.vector.tensor_tensor(x[:, 4 * i + j, :], x[:, 4 * i + j, :], banks[j][:],
                                                ALU.add).then_inc(s["x"], 1)

            def pool_part(pool):
                pool.sem_inc(s["lo"], 2)
                with pool.Fori(0, KT // turns) as i:
                    for t in range(turns):
                        pool.wait_ge(s["gated"], 2 * turns * i + 2 * (t + 1) + 4)
                        nc.gpsimd.tensor_tensor(temps[:, t % 2, 0, :], temps[:, t % 2, 0, :], temps[:, t % 2, 1, :],
                                                ALU.add).then_inc(s["sum"], 1)
                        pool.wait_ge(s["hi"], turns * i + (t + 1))
                        nc.gpsimd.tensor_tensor(m_lo[:, i * turns + t, :], temps[:, t % 2, 0, :],
                                                m_hi[:, i * turns + t, :], ALU.subtract).then_inc(s["lo"], 1)

            return act_part, pe_part, dve_part, pool_part, (s["x"], 5)

        y1_hi = sb("y1_hi", [P, KT, S], F32R, A0)
        y1_lo = sb("y1_lo", [P, KT, S], F32R, A0 + 52 * K)
        m1_hi = sb("m1_hi", [P, KT, S], F32R, A0 + 16 * K)
        m1_lo = sb("m1_lo", [P, KT, S], F32R, A0 + 32 * K)
        m1_temps = sb("m1_temps", [P, 2, 2, S], F32, W0)

        nsa_c = sb("nsa_c", [P, S], F32, A0)
        nsa_s = sb("nsa_s", [P, S], F32, A0 + 2 * K)
        ret_c = sb("ret_c", [P, S], F32, A0 + 4 * K)
        ret_s = sb("ret_s", [P, S], F32, A0 + 6 * K)
        cmp_c = sb("cmp_c", [P, 64], F32, A0 + 8 * K)
        cmp_s = sb("cmp_s", [P, 64], F32, A0 + 8 * K + 256)
        cmp_add = sb("cmp_add", [P, TB, 32], F32, A0 + 8 * K + 512)
        cmp_keep = sb("cmp_keep", [P, TB, 32], F32, A0 + 9 * K)
        gates = sb("gates", [P, TB, 48], F32, A0 + 10 * K)
        kc_hi = sb("kc_hi", [P, 32], F32R, A0 + 11 * K)
        kc_lo = sb("kc_lo", [P, 32], F32R, A0 + 11 * K + 256)
        vc_raw = sb("vc_raw", [P, 2, P], F32, A0 + 12 * K)
        vcs_hi = sb("vcs_hi", [P, P], F32R, A0 + 13 * K)
        vcs_lo = sb("vcs_lo", [P, P], F32R, A0 + 13 * K + 512)
        kc_raw = sb("kc_raw", [P, 64], F32, A0 + 14 * K)
        kc_sw = sb("kc_sw", [P, 64], F32, A0 + 14 * K + 256)
        hidden_k = sb("hidden_k", [P, 2, 64], F32, A0 + 15 * K)
        hidden_v = sb("hidden_v", [P, 2, 2, P], F32, A0 + 86 * K)
        a_raw = sb("a_raw", [P, KT, S], F32, A0 + 16 * K)
        nqk = sb("nqk", [P, 12, S], F32, A0 + 32 * K)
        nv = sb("nv", [P, TB, 256], F32, A0 + 56 * K)
        swapped = sb("swapped", [P, 2, S], F32, A0 + 80 * K)
        ck = sb("ck", [P, 4, S], F32, A0 + 60 * K)
        blk = sb("blk", [P, 16, 64], F32, A0 + 68 * K)
        blk_hi = sb("blk_hi", [P, 16, 64], F32R, A0 + 72 * K)
        blk_lo = sb("blk_lo", [P, 16, 64], F32R, A0 + 76 * K)
        gate_fm = sb("gate_fm", [P, S], F32, A0 + 84 * K)
        nq_hi = sb("nq_hi", [P, 2, S], F32R, A0 + 60 * K)
        nq_lo = sb("nq_lo", [P, 2, S], F32R, A0)
        nk_hi = sb("nk_hi", [P, 2, S], F32R, A0 + 64 * K)
        nk_lo = sb("nk_lo", [P, 2, S], F32R, A0 + 68 * K)
        nvs_hi = sb("nvs_hi", [P, TB, 2, P], F32R, A0 + 72 * K)
        nvs_lo = sb("nvs_lo", [P, TB, 2, P], F32R, A0 + 76 * K)
        nprob = sb("nprob", [P, 2, OFF[TB]], F32, A0 + 80 * K)
        npt_hi = sb("npt_hi", [P, OFF[TB]], F32R, A0 + 90 * K)
        npt_lo = sb("npt_lo", [P, OFF[TB]], F32R, A0 + 95 * K)
        csc = sb("csc", [P, 2, TB, 32], F32, A0 + 100 * K)
        cpad = sb("cpad", [P, 2, TB * (P + 32)], F32, A0 + 101 * K)
        cpt_hi = sb("cpt_hi", [P, S], F32R, 90 * K)
        cpt_lo = sb("cpt_lo", [P, S], F32R, 94 * K)
        c_top, c_total, c_inverse, nguard = (small[:, 32 + 8 * n:40 + 8 * n] for n in range(4))
        r_qk = sb("r_qk", [P, KT, S], F32, A0 + 32 * K)
        r_v = sb("r_v", [P, TB, D], F32, A0 + 48 * K)
        r_raw = sb("r_raw", [P, KT, S], F32, A0 + 64 * K)
        r_swap = sb("r_swap", [P, S], F32, 99 * K)
        rq_hi = sb("rq_hi", [P, S], F32R, A0 + 80 * K)
        rq_lo = sb("rq_lo", [P, S], F32R, A0 + 82 * K)
        rk_hi = sb("rk_hi", [P, S], F32R, A0 + 84 * K)
        rk_lo = sb("rk_lo", [P, S], F32R, A0 + 86 * K)
        rv_hi = sb("rv_hi", [P, TB, 2 * P], F32R, A0 + 88 * K)
        rv_lo = sb("rv_lo", [P, TB, 2 * P], F32R, A0 + 92 * K)
        decay = sb("decay", [P, 2, S], F32, A0 + 96 * K)
        weighted = sb("weighted", [P, OFF[TB]], F32, A0 + 100 * K)
        ws_hi = sb("ws_hi", [P, OFF[TB]], F32R, A0)
        ws_lo = sb("ws_lo", [P, OFF[TB]], F32R, A0 + 5 * K)
        gn_sq = sb("gn_sq", [P, S], F32, A0 + 12 * K)
        gn_r = sb("gn_r", [P, S], F32, A0 + 10 * K)
        a_hi = sb("a_hi", [P, KT, S], F32R, A0 + 32 * K)
        a_lo = sb("a_lo", [P, KT, S], F32R, A0 + 16 * K)
        r_hi = sb("r_hi", [P, KT, S], F32R, A0 + 48 * K)
        r_lo = sb("r_lo", [P, KT, S], F32R, A0 + 64 * K)
        m2_hi = sb("m2_hi", [P, KT, S], F32R, A0 + 80 * K)
        m2_lo = sb("m2_lo", [P, KT, S], F32R, A0)
        m2_temps = sb("m2_temps", [P, 2, 2, S], F32, A0 + 96 * K)

        def roped_out(name, first, count, start, dst, sw, table_c, table_s, mask):
            s = {k: sem(f"{name}_{k}") for k in ("swapped", "out", "done")}

            def act_part(act):
                with act.Fori(0, count // 4) as i:
                    for j in range(4):
                        ahead(high_part, act, first, j, i, 4)

            def pe_part(pe):
                for w in start:
                    pe.wait_ge(*w)
                with pe.Fori(0, count // 4) as i:
                    for j in range(4):
                        slot = ready(pe, first, j, i, 4)
                        pe.wait_ge(s["out"], 4 * i + (j + 1))
                        tile_chunk(slot, banks[j][:], xn_hi, xn_lo).then_inc(used, 1)

            def dve_part(dve):
                for w in start:
                    dve.wait_ge(*w)
                dve.sem_inc(s["out"], 4)
                with dve.Fori(0, count // 4) as i:
                    for j in range(4):
                        ahead(low_part, dve, first, j, i, 4)
                        finished(dve, first, j, i, 4)
                        dve.wait_ge(s["done"], 4 * i + (j + 1))
                        apart(dve)
                        nc.vector.stream_shuffle(sw[:, j % 2, :], banks[j][:], mask).then_inc(s["swapped"], 1)
                        nc.vector.tensor_tensor(dst[:, 4 * i + j, :], banks[j][:], table_c[:],
                                                ALU.mult).then_inc(s["out"], 1)

            def pool_part(pool):
                for w in start:
                    pool.wait_ge(*w)
                pool.sem_inc(s["done"], 2)
                sines = sem(f"{name}_sines")
                with pool.Fori(0, count // 4) as i:
                    for j in range(4):
                        pool.wait_ge(s["swapped"], 4 * i + (j + 1))
                        nc.gpsimd.tensor_tensor(sw[:, j % 2, :], sw[:, j % 2, :], table_s[:],
                                                ALU.mult).then_inc(sines, 1)
                        pool.wait_ge(s["out"], 4 * i + (j + 5))
                        pool.wait_ge(sines, 4 * i + (j + 1))
                        nc.gpsimd.tensor_tensor(dst[:, 4 * i + j, :], dst[:, 4 * i + j, :], sw[:, j % 2, :],
                                                ALU.add).then_inc(s["done"], 1)

            return act_part, pe_part, dve_part, pool_part, (s["done"], count + 2)

        def mixer2(n_mix2, x_done):
            norm_done = n_mix2[4]
            t = {k: sem(f"b2_{k}") for k in ("tables", "v", "gate", "gate_t", "gates", "blk", "zero", "hi", "lo", "hid",
                                             "gelu", "kv", "kc", "pad")}

            def tables_in(pool):
                pool.wait_ge(*x_done)
                at = 0
                for tile in (nsa_c, nsa_s, ret_c, ret_s, cmp_c, cmp_s, cmp_add, cmp_keep):
                    n = int(np.prod(tile.shape[1:]))
                    to = tile[:].rearrange("p a b -> p (a b)") if len(tile.shape) == 3 else tile[:]
                    pool.dma_start(to, rows[:, at:at + n]).then_inc(t["tables"], 16)
                    at += n

            parts.append((skip, skip, skip, tables_in))
            parts.append(n_mix2)
            qk = roped_out("b2_qk", FIRST["b2_qk"], 12, [norm_done, (t["tables"], 128)], nqk, swapped, nsa_c, nsa_s,
                           SWAP8)
            cmp = copies_out("b2_cmp", FIRST["b2_cmp"], 4, ck)
            fv, fg, fw = FIRST["b2_v"], FIRST["b2_g"], FIRST["b2_w1"]

            def pe_part(pe):
                for j in range(2):
                    slot = ready(pe, fv, j)
                    for n in range(4):
                        k, w = 4 * j + n, slice(n * 256, (n + 1) * 256)
                        for tb in range(TB):
                            at = slice(tb * P, (tb + 1) * P)
                            last = mm3(banks[4 + tb][:, 0:256], xn_hi[:, k, at], xn_lo[:, k, at], w_hi[:, slot, w],
                                       w_lo[:, slot, w], k == 0, k == KT - 1)
                    last.then_inc(used, 1)
                slot = ready(pe, fg, 0)
                pe.wait_ge(*cmp[4])
                tile_chunk(slot, banks[0][:], xn_hi, xn_lo).then_inc(used, 1)
                pe.wait_ge(t["gate"], 1)
                for tb in range(TB):
                    last = nc.tensor.transpose(banks[1][:, 48 * tb:48 * tb + 48], gate_fm[0:48, tb * P:(tb + 1) * P],
                                               ident[0:48, 0:48])
                last.then_inc(t["gate_t"], 1)
                for kv in range(2):
                    pe.wait_ge(t["lo"], kv + 1)
                    if kv:
                        pe.wait_ge(t["v"], 4)
                    for half in range(2):
                        for j in range(2):
                            slot = ready(pe, fw, 4 * kv + 2 * half + j)
                            for n in range(8):
                                k, w = 8 * j + n, slice(n * P, (n + 1) * P)
                                last = mm3(banks[2 + 2 * kv + half][:, 0:64], w_hi[:, slot, w], w_lo[:, slot, w],
                                           blk_hi[:, k, :], blk_lo[:, k, :], k == 0, k == 15)
                            last.then_inc(used, 1)
                pe.wait_ge(t["gelu"], 4)
                pe.wait_ge(t["gates"], 1)
                for half in range(2):
                    last = nc.tensor.matmul(banks[0][:, 0:64], w2_sb[:, half, :], hidden_k[:, half, :],
                                            start=half == 0, stop=half == 1)
                last.then_inc(t["kv"], 1)
                for g in range(2):
                    for half in range(2):
                        last = nc.tensor.matmul(banks[1][:, g * P:(g + 1) * P],
                                                hidden_v[:, half, g, :],
                                                w2_sb[:, 2 + half, :], start=half == 0, stop=half == 1,
                                                skip_group_check=True)
                    last.then_inc(t["kv"], 1)

            def act_part(act):
                for j in range(2):
                    ahead(high_part, act, fv, j)
                ahead(high_part, act, fg, 0)
                finished(act, fg, 0)
                nc.scalar.activation(gate_fm[0:48, :], banks[0][0:48, :], ACT.Sigmoid).then_inc(t["gate"], 1)
                for kv in range(2):
                    act.wait_ge(t["blk"], 8 * (kv + 1))
                    if kv:
                        finished(act, fw, 3)
                    nc.scalar.activation(blk_hi[:], blk[:], ACT.Copy).then_inc(t["hi"], 1)
                    for half in range(2):
                        for j in range(2):
                            ahead(high_part, act, fw, 4 * kv + 2 * half + j)
                        finished(act, fw, 4 * kv + 2 * half + 1)
                        pre = banks[2 + 2 * kv + half][:, 0:64]
                        if kv == 0:
                            nc.scalar.activation(hidden_k[:, half, :], pre, ACT.Gelu_apprx_tanh).then_inc(t["gelu"], 1)
                        else:
                            nc.scalar.activation(
                                hidden_v[:, half].rearrange("p g (f n) -> p g f n", f=4),
                                pre.rearrange("p (g o n) -> p g o n", g=2, o=1).to_broadcast([P, 2, 4, 32]),
                                ACT.Gelu_apprx_tanh).then_inc(t["gelu"], 1)

            def dve_part(dve):
                for j in range(2):
                    ahead(low_part, dve, fv, j)
                finished(dve, fv, 1)
                for tb in range(TB):
                    nc.vector.tensor_copy(nv[:, tb, :], banks[4 + tb][:, 0:256]).then_inc(t["v"], 1)
                ahead(low_part, dve, fg, 0)
                dve.wait_ge(*cmp[4])
                dve.wait_ge(t["zero"], 1)
                for kv in range(2):
                    if kv:
                        dve.wait_ge(t["lo"], 1)
                    for g in range(2):
                        for half in range(2):
                            r = slice(64 * half, 64 * half + 64)
                            view = ck[r, 2 * kv + g, :].rearrange("p (n k two) -> p two k n", k=8, two=2)[:, half]
                            for a in range(2):
                                at = COLS["pos"] + 8 * a
                                emb = col[r, at:at + 8].rearrange("p (k o) -> p k o", o=1).to_broadcast([64, 8, 31])
                                nc.vector.tensor_tensor(blk[r, 8 * a:8 * a + 8, 32 * g:32 * g + 31],
                                                        view[:, :, a:a + 31], emb, ALU.add).then_inc(t["blk"], 1)
                    if kv == 0:
                        dve.wait_ge(t["gate_t"], 1)
                        nc.vector.tensor_copy(gates[:], banks[1][:, 0:192].rearrange("p (t h) -> p t h", t=TB)
                                              ).then_inc(t["gates"], 1)
                    for j in range(4):
                        ahead(low_part, dve, fw, 4 * kv + j)
                dve.wait_ge(t["kv"], 1)
                nc.vector.stream_shuffle(kc_sw[:], banks[0][:, 0:64], SWAP8).then_inc(t["kc"], 1)
                nc.vector.tensor_tensor(kc_raw[:], banks[0][:, 0:64], cmp_c[:], ALU.mult).then_inc(t["kc"], 1)
                dve.wait_ge(t["kc"], 1)
                nc.vector.tensor_tensor(kc_sw[:], kc_sw[:], cmp_s[:], ALU.mult).then_inc(t["kc"], 1)
                dve.wait_ge(t["kc"], 3)
                nc.vector.tensor_tensor(kc_raw[:], kc_raw[:], kc_sw[:], ALU.add).then_inc(t["kc"], 1)
                dve.wait_ge(t["kv"], 3)
                nc.vector.tensor_copy(vc_raw[:], banks[1][:, 0:256].rearrange("p (g d) -> p g d", g=2)
                                      ).then_inc(t["kc"], 1)

            def pool_part(pool):
                pool.wait_ge(*norm_done)
                nc.gpsimd.memset(blk[:], 0.0).then_inc(t["zero"], 1)
                for kv in range(2):
                    pool.wait_ge(t["hi"], kv + 1)
                    nc.gpsimd.tensor_tensor(blk_lo[:], blk[:], blk_hi[:], ALU.subtract).then_inc(t["lo"], 1)
                pool.wait_ge(t["kc"], 5)
                nc.gpsimd.memset(cpad[:], 0.0).then_inc(t["pad"], 1)

            prepare = (act_part, pe_part, dve_part, pool_part)
            nsa_out = sparse_attention([(t["kc"], 5), (t["pad"], 1), (t["v"], 4), qk[4]])
            ret = retention([nsa_out[4], nsa_out[5]])
            between = (skip, lambda pe: pe.wait_ge(*qk[4]), skip, skip)
            return [qk, between, cmp, prepare, nsa_out, *ret]

        def sparse_attention(start):
            s = {k: sem(f"nsa_{k}") for k in ("k_hi", "k_lo", "q_hi", "q_lo", "scored", "biased", "negated", "exp",
                                              "guard", "inverse", "scaled", "turned", "hi", "lo", "summed",
                                              "out", "c_scored", "c_dve", "c_exp", "c_turned", "c_hi", "c_lo", "r_swapped", "zero",
                                              "r_sines", "r_out", "r_done")}
            frqk = FIRST["b2_rqk"]
            SCORE_ORDER = (0, 2, 1, 3)

            def score_bank(qb):
                return (banks[0][:, 0:P], banks[1][:, 0:2 * P], banks[0][:, P:S], banks[2][:])[qb]

            units = [(0, 0), (0, 1), (1, 0), (1, 1)]

            def v_twice(g, m):
                return nv[:, :, bass.ds(g * 64 + 128 * m, 64)].rearrange("p t (o d) -> p t o d", o=1).to_broadcast(
                    [P, TB, 2, 64])

            def twice(tile, m):
                return tile[:, :, m, :].rearrange("p t (o d) -> p t o d", o=2)

            def begin(eng):
                for w in start:
                    eng.wait_ge(*w)

            def group_turns(g, body):
                for p in range(4):
                    body(4 * g + p, p < 3, p)

            def pe_part(pe):
                begin(pe)
                pe.sem_inc(s["scored"], 4)
                pe.sem_inc(s["turned"], 8)
                pe.sem_inc(s["summed"], 9)
                pe.sem_inc(s["c_turned"], 1)
                pe.wait_ge(s["zero"], 4)
                with pe.Fori(0, 2) as g:
                    pe.wait_ge(s["k_lo"], 6 * g + 6)
                    apart(pe)
                    def score(i, u):
                        j, m = units[u % 4]
                        for n, qb in enumerate(SCORE_ORDER):
                            pe.wait_ge(s["biased"], 16 * i + (4 * u + max(n, 1) + 1))
                            at = slice(qb * P, (qb + 1) * P)
                            mm3(score_bank(qb), nq_hi[:, j, at], nq_lo[:, j, at], nk_hi[:, m, 0:(qb + 1) * P],
                                nk_lo[:, m, 0:(qb + 1) * P]).then_inc(s["scored"], 1)

                    def turn(i, u, kb):
                        pe.wait_ge(s["lo"], 16 * i + (4 * u + kb + 1))
                        for qb in range(kb, TB):
                            if kb == 0:
                                pe.wait_ge(s["scaled"], 16 * i + (4 * u + qb + 1))
                            last = nc.tensor.transpose(banks[4 + kb % 2][:, (qb - kb) * P:(qb - kb + 1) * P],
                                                       nprob[:, u % 2, OFF[qb] + kb * P:OFF[qb] + (kb + 1) * P],
                                                       ident[:])
                        last.then_inc(s["turned"], 1)

                    def values(i, u, kb):
                        j, m = units[u]
                        pe.wait_ge(s["lo"], 16 * i + (4 * u + kb + 3))
                        at = slice(KOFF[kb], KOFF[kb + 1])
                        mm3(banks[6][:, kb * P:S], nvs_hi[:, kb, m, :], nvs_lo[:, kb, m, :], npt_hi[:, at], npt_lo[:, at], False,
                            m == 1 and kb == TB - 1).then_inc(s["summed"], 1)

                    def compressed_scores(i, n):
                        pe.wait_ge(s["q_lo"], 2 * i + (2 * n + 2))
                        pe.wait_ge(s["c_lo"], 2 * i + (2 * n + 1))
                        for j in range(2):
                            for qb in range(TB):
                                at = slice(qb * P, (qb + 1) * P)
                                last = mm3(banks[7][:, (TB * j + qb) * 32:(TB * j + qb + 1) * 32], nq_hi[:, j, at],
                                           nq_lo[:, j, at], kc_hi[:], kc_lo[:])
                            last.then_inc(s["c_scored"], 1)

                    def compressed_turn(i, j):
                        if j == 0:
                            pe.wait_ge(s["c_dve"], 10 * i + 10)
                        pe.wait_ge(s["c_lo"], 2 * i + (j + 1))
                        for qb in range(TB):
                            last = nc.tensor.transpose(banks[7][:, qb * P:(qb + 1) * P],
                                                       cpad[:, j, qb * P:(qb + 1) * P], ident[:])
                        last.then_inc(s["c_turned"], 1)

                    def compressed_values(i, j):
                        pe.wait_ge(s["c_lo"], 2 * i + (j + 2))
                        pe.wait_ge(s["out"], 2 * i + (j + 1))
                        mm3(banks[6][:], vcs_hi[:], vcs_lo[:], cpt_hi[:], cpt_lo[:], True,
                            False).then_inc(s["summed"], 1)

                    def body(i, more, p):
                        for u in range(4):
                            if u < 2:
                                compressed_turn(i, u)
                            turn(i, u, 0)
                            turn(i, u, 1)
                            if u == 0:
                                slot = ready(pe, frqk, p, g, 4)
                                pe.wait_ge(s["r_out"], i + 1)
                            for k in (2 * u, 2 * u + 1):
                                w = slice(k * P, (k + 1) * P)
                                last = mm3(banks[3][:], w_hi[:, slot, w], w_lo[:, slot, w], xn_hi[:, k, :],
                                           xn_lo[:, k, :], k == 0, k == KT - 1)
                            if u == 3:
                                last.then_inc(used, 1)
                            turn(i, u, 2)
                            turn(i, u, 3)
                            if u == 2 and more:
                                compressed_scores(i, 1)
                            if u < 2 or more:
                                score(i, u + 2)
                            if u % 2 == 0:
                                compressed_values(i, u // 2)
                            for kb in range(TB):
                                values(i, u, kb)

                    compressed_scores(4 * g, 0)
                    score(4 * g, 0)
                    score(4 * g, 1)
                    group_turns(g, body)

            def act_part(act):
                begin(act)
                act.sem_inc(s["out"], 1)
                with act.Fori(0, 2) as g:
                    act.wait_ge(s["summed"], 72 * g + 9)
                    for m in range(2):
                        nc.scalar.activation(nk_hi[:, m, :], nqk[:, g + (8 + 2 * m), :], ACT.Copy).then_inc(s["k_hi"], 1)
                        nc.scalar.activation(twice(nvs_hi, m), v_twice(g, m),
                                             ACT.Copy).then_inc(s["k_hi"], 1)
                    nc.scalar.activation(vcs_hi[:], vc_raw[:, g, :], ACT.Copy).then_inc(s["k_hi"], 1)
                    nc.scalar.activation(kc_hi[:], kc_raw[:, bass.ds(g * 32, 32)], ACT.Copy).then_inc(s["k_hi"], 1)
                    def stage(i, n):
                        act.wait_ge(s["scored"], 16 * i + (16 * n + 4))
                        for j in range(2):
                            r = slice(64 * j, 64 * j + 64)
                            nc.scalar.activation(nq_hi[r, j, :], nqk[r, i + n, :], ACT.Copy).then_inc(s["q_hi"], 1)

                    def compressed_exps(i, n):
                        act.wait_ge(s["c_dve"], 10 * i + (10 * n + 3))
                        nc.scalar.activation(csc[:], csc[:], ACT.Exp, scale=0.125).then_inc(s["c_exp"], 1)

                    def exps(i, u, blocks):
                        act.wait_ge(s["negated"], 4 * i + (u + 1))
                        for qb in blocks:
                            at = nprob[:, u % 2, scores_rows(qb)]
                            n = 4 * (u % 2) + qb
                            nc.scalar.activation(at, at, ACT.Exp, bias=neg_top[:, n:n + 1], scale=0.125,
                                                 accum_out=total[:, n:n + 1]).then_inc(s["exp"], 1)

                    def highs(i, u, blocks):
                        for kb in blocks:
                            act.wait_ge(s["turned"], 16 * i + (4 * u + kb + 9))
                            act.wait_ge(s["summed"], 18 * i + ((6, 11, 15, 20)[u] + kb))
                            nc.scalar.activation(npt_hi[:, KOFF[kb]:KOFF[kb + 1]],
                                                 banks[4 + kb % 2][:, 0:S - kb * P], ACT.Copy).then_inc(s["hi"], 1)

                    def compressed_high(i, j):
                        act.wait_ge(s["c_turned"], 2 * i + (j + 2))
                        act.wait_ge(s["summed"], 18 * i + 9 * j + 1)
                        nc.scalar.activation(cpt_hi[:], banks[7][:], ACT.Copy).then_inc(s["c_hi"], 1)

                    def output(i, j):
                        act.wait_ge(s["summed"], 18 * i + (9 * j + 18))
                        r = slice(64 * j, 64 * j + 64)
                        nc.scalar.activation(a_raw[r, i, :], banks[6][r, :], ACT.Copy).then_inc(s["out"], 1)

                    def body(i, more, p):
                        for u in range(4):
                            if u < 2:
                                compressed_high(i, u)
                            highs(i, u, (0, 1))
                            if u == 2:
                                output(i, 0)
                            if u < 3 or more:
                                exps(i, u + 1, (0, 1, 2))
                            highs(i, u, (2, 3))
                            if u < 3 or more:
                                exps(i, u + 1, (3,))
                            if u == 0:
                                ahead(high_part, act, frqk, p, g, 4)
                            if u == 1 and more:
                                stage(i, 1)
                        if more:
                            compressed_exps(i, 1)
                        output(i, 1)

                    stage(4 * g, 0)
                    compressed_exps(4 * g, 0)
                    exps(4 * g, 0, range(TB))
                    group_turns(g, body)

            def dve_part(dve):
                begin(dve)
                dve.sem_inc(s["biased"], 4)
                dve.sem_inc(s["lo"], 2)
                dve.sem_inc(s["c_lo"], 1)
                dve.sem_inc(s["r_out"], 1)
                for part in (nq_hi, nq_lo):
                    for j in range(2):
                        r = slice(64 - 64 * j, P - 64 * j)
                        nc.vector.memset(part[r, j, :].bitcast(F32), 0.0).then_inc(s["zero"], 1)
                with dve.Fori(0, 2) as g:
                    def biased(i, u):
                        for place_of, qb in enumerate(SCORE_ORDER):
                            dve.wait_ge(s["scored"], 16 * i + (4 * u + max(place_of, 1) + 5))
                            if place_of == 0:
                                dve.wait_ge(s["turned"], 16 * i + (4 * u + 4))
                            apart(dve)
                            n = 4 * (u % 2) + qb
                            width = (qb + 1) * P
                            nc.vector.tensor_tensor_reduce(nprob[:, u % 2, scores_rows(qb)], score_bank(qb),
                                                           bias_tri[:, S - width:S], 1.0, -3.0e38, ALU.add, ALU.max,
                                                           top_s[:, n:n + 1]).then_inc(s["biased"], 1)
                        dve.wait_ge(s["biased"], 16 * i + (4 * u + 8))
                        n = 4 * (u % 2)
                        nc.vector.tensor_scalar(neg_top[:, n:n + 4], top_s[:, n:n + 4], -0.125, None,
                                                ALU.mult).then_inc(s["negated"], 1)

                    def scaled(i, u):
                        j, m = units[u]
                        n = slice(4 * (u % 2), 4 * (u % 2) + 4)
                        dve.wait_ge(s["exp"], 16 * i + (4 * u + 4))
                        nc.vector.tensor_scalar(nguard[:, n], total[:, n], 1e-20, None,
                                                ALU.max).then_inc(s["guard"], 1)
                        dve.wait_ge(s["guard"], 8 * i + (2 * u + 1))
                        nc.vector.reciprocal(nguard[:, n], nguard[:, n]).then_inc(s["guard"], 1)
                        dve.wait_ge(s["guard"], 8 * i + (2 * u + 2))
                        nc.vector.tensor_tensor(inverse[:, n], nguard[:, n],
                                                gates[:, :, i * 6 + (3 * j + 1 + m)],
                                                ALU.mult).then_inc(s["inverse"], 1)
                        dve.wait_ge(s["inverse"], 4 * i + (u + 1))
                        for qb in range(TB):
                            at = nprob[:, u % 2, scores_rows(qb)]
                            n = 4 * (u % 2) + qb
                            nc.vector.tensor_scalar(at, at, inverse[:, n:n + 1], None, ALU.mult).then_inc(s["scaled"], 1)

                    def lows(i, u):
                        for kb in range(TB):
                            dve.wait_ge(s["hi"], 16 * i + (4 * u + kb + 1))
                            at = slice(KOFF[kb], KOFF[kb + 1])
                            nc.vector.tensor_tensor(npt_lo[:, at], banks[4 + kb % 2][:, 0:S - kb * P], npt_hi[:, at],
                                                    ALU.subtract).then_inc(s["lo"], 1)

                    def compressed_low(i, j):
                        dve.wait_ge(s["c_hi"], 2 * i + (j + 1))
                        nc.vector.tensor_tensor(cpt_lo[:], banks[7][:], cpt_hi[:],
                                                ALU.subtract).then_inc(s["c_lo"], 1)

                    add = cmp_add[:].rearrange("p (o t) n -> p o t n", o=1).to_broadcast([P, 2, TB, 32])
                    keep = cmp_keep[:].rearrange("p (o t) n -> p o t n", o=1).to_broadcast([P, 2, TB, 32])
                    over = [t.rearrange("p (h t o) -> p h t o", h=2, o=1).to_broadcast([P, 2, TB, 32])
                            for t in (c_top, c_inverse)]

                    def step(i, n, instruction, count, wait=True):
                        instruction.then_inc(s["c_dve"], 1)
                        if wait:
                            dve.wait_ge(s["c_dve"], 10 * i + (10 * n + count))

                    def compressed_shift(i, n):
                        dve.wait_ge(s["c_scored"], 2 * i + (2 * n + 2))
                        step(i, n, nc.vector.tensor_tensor(
                            csc[:], banks[7][:, 0:256].rearrange("p (h t n) -> p h t n", h=2, t=TB), add, ALU.add), 1)
                        step(i, n, nc.vector.tensor_reduce(c_top.rearrange("p (h t) -> p h t", h=2), csc[:], AX.X,
                                                           ALU.max), 2)
                        step(i, n, nc.vector.tensor_tensor(csc[:], csc[:], over[0], ALU.subtract), 3, False)

                    def compressed_scale(i, n):
                        dve.wait_ge(s["c_exp"], i + (n + 1))
                        step(i, n, nc.vector.tensor_tensor(csc[:], csc[:], keep, ALU.mult), 4)
                        step(i, n, nc.vector.tensor_reduce(c_total.rearrange("p (h t) -> p h t", h=2), csc[:], AX.X,
                                                           ALU.add), 5)
                        step(i, n, nc.vector.tensor_scalar(c_total, c_total, 1e-20, None, ALU.max), 6)
                        step(i, n, nc.vector.reciprocal(c_total, c_total), 7)
                        step(i, n, nc.vector.tensor_tensor(
                            c_inverse.rearrange("p (h t) -> p h t", h=2), c_total.rearrange("p (h t) -> p h t", h=2),
                            gates[:, :, bass.ds(i * 6 + 6 * n, 6)].rearrange("p t (h c) -> p h t c", c=3)[:, :, :, 0],
                            ALU.mult), 8)
                        for j in range(2):
                            diagonal = cpad[:, j, :].rearrange("p (t w) -> p t w", w=P + 32)[:, :, 0:32]
                            step(i, n, nc.vector.tensor_tensor(diagonal, csc[:, j, :, :], over[1][:, j, :, :],
                                                               ALU.mult), 9 + j, False)

                    def body(i, more, p):
                        for u in range(4):
                            scaled(i, u)
                            if u == 3 and more:
                                compressed_shift(i, 1)
                            if u < 3 or more:
                                biased(i, u + 1)
                            if u < 2:
                                compressed_low(i, u)
                            lows(i, u)
                            if u == 1:
                                ahead(low_part, dve, frqk, p, g, 4)
                        rotate(i, p)
                        if more:
                            compressed_scale(i, 1)

                    def rotate(i, p):
                        finished(dve, frqk, p, g, 4)
                        dve.wait_ge(s["r_done"], i + 1)
                        apart(dve)
                        nc.vector.stream_shuffle(r_swap[:], banks[3][:], SWAP16).then_inc(s["r_swapped"], 1)
                        nc.vector.tensor_tensor(r_qk[:, i, :], banks[3][:], ret_c[:], ALU.mult).then_inc(s["r_out"], 1)

                    compressed_shift(4 * g, 0)
                    biased(4 * g, 0)
                    compressed_scale(4 * g, 0)
                    group_turns(g, body)

            def pool_part(pool):
                begin(pool)
                pool.sem_inc(s["r_done"], 1)
                with pool.Fori(0, 2) as g:
                    for m in range(2):
                        pool.wait_ge(s["k_hi"], 6 * g + (2 * m + 1))
                        nc.gpsimd.tensor_tensor(nk_lo[:, m, :], nqk[:, g + (8 + 2 * m), :], nk_hi[:, m, :],
                                                ALU.subtract).then_inc(s["k_lo"], 1)
                        pool.wait_ge(s["k_hi"], 6 * g + (2 * m + 2))
                        nc.gpsimd.tensor_tensor(twice(nvs_lo, m), v_twice(g, m), twice(nvs_hi, m), ALU.subtract).then_inc(s["k_lo"], 1)
                    pool.wait_ge(s["k_hi"], 6 * g + 5)
                    nc.gpsimd.tensor_tensor(vcs_lo[:], vc_raw[:, g, :], vcs_hi[:], ALU.subtract).then_inc(s["k_lo"], 1)
                    pool.wait_ge(s["k_hi"], 6 * g + 6)
                    nc.gpsimd.tensor_tensor(kc_lo[:], kc_raw[:, bass.ds(g * 32, 32)], kc_hi[:],
                                            ALU.subtract).then_inc(s["k_lo"], 1)
                    def stage(i):
                        for j in range(2):
                            r = slice(64 * j, 64 * j + 64)
                            pool.wait_ge(s["q_hi"], 2 * i + (j + 1))
                            nc.gpsimd.tensor_tensor(nq_lo[r, j, :], nqk[r, i, :], nq_hi[r, j, :],
                                                    ALU.subtract).then_inc(s["q_lo"], 1)
                            pool.wait_ge(s["q_lo"], 2 * i + (j + 1))

                    pool.wait_ge(s["k_lo"], 6 * g + 6)
                    stage(4 * g)
                    for p in range(4):
                        i = 4 * g + p
                        if p < 3:
                            pool.wait_ge(s["r_done"], i + 1)
                            stage(4 * g + (p + 1))
                        pool.wait_ge(s["r_swapped"], i + 1)
                        nc.gpsimd.tensor_tensor(r_swap[:], r_swap[:], ret_s[:], ALU.mult).then_inc(s["r_sines"], 1)
                        pool.wait_ge(s["r_out"], i + 2)
                        pool.wait_ge(s["r_sines"], i + 1)
                        apart(pool)
                        nc.gpsimd.tensor_tensor(r_qk[:, i, :], r_qk[:, i, :], r_swap[:], ALU.add).then_inc(s["r_done"], 1)

            return act_part, pe_part, dve_part, pool_part, (s["out"], 17), (s["r_done"], 9)

        def retention(before):
            s = {k: sem(f"ret_{k}") for k in ("v", "staged_hi", "staged_lo", "scored", "weighted", "hi", "lo", "summed",
                                              "out", "mean", "centred", "square", "var", "root", "recip", "done",
                                              "gate", "gated")}
            decay_in = sem("ret_decay_in")
            frv, fgr = FIRST["b2_rv"], FIRST["b2_gr"]

            def v_pe(pe):
                for w in before:
                    pe.wait_ge(*w)
                for c in range(2):
                    for j in range(4):
                        slot = ready(pe, frv, 4 * c + j)
                        if c and j == 0:
                            pe.wait_ge(s["v"], 4)
                        for t in range(2):
                            k, w = 2 * j + t, slice(t * S, (t + 1) * S)
                            for tb in range(TB):
                                at = slice(tb * P, (tb + 1) * P)
                                last = mm3(banks[4 + tb][:], xn_hi[:, k, at], xn_lo[:, k, at], w_hi[:, slot, w],
                                           w_lo[:, slot, w], k == 0, k == KT - 1)
                        last.then_inc(used, 1)

            def v_act(act):
                for j in range(8):
                    ahead(high_part, act, frv, j)

            def v_dve(dve):
                for c in range(2):
                    for j in range(4):
                        ahead(low_part, dve, frv, 4 * c + j)
                    finished(dve, frv, 4 * c + 3)
                    for tb in range(TB):
                        nc.vector.tensor_copy(r_v[:, tb, c * S:(c + 1) * S], banks[4 + tb][:]).then_inc(s["v"], 1)

            start = [*before, (s["v"], 8)]
            ORDER_K = (0, 1, 3, 2)

            def begin(eng):
                for w in start:
                    eng.wait_ge(*w)

            def score_bank(kb):
                return (banks[0][:], banks[1][:, 0:384], banks[2][:, 0:256], banks[1][:, 384:S])[kb]

            def pe_part(pe):
                begin(pe)
                pe.sem_inc(s["summed"], 8)
                with pe.Fori(0, 2) as t:
                    def score(c):
                        r = slice(64 * (c % 2), 64 * (c % 2) + 64)
                        for n, kb in enumerate(ORDER_K):
                            pe.wait_ge(s["weighted"], 16 * t + (4 * c + (1, 3, 3, 4)[n]))
                            mm3(score_bank(kb), rk_hi[r, kb * P:(kb + 1) * P], rk_lo[r, kb * P:(kb + 1) * P],
                                rq_hi[r, kb * P:S], rq_lo[r, kb * P:S]).then_inc(s["scored"], 1)

                    def values(c):
                        pe.wait_ge(s["out"], 4 * t + (c + 1))
                        w = slice(P * (c % 2), P * (c % 2) + P)
                        for n, kb in enumerate(ORDER_K):
                            pe.wait_ge(s["lo"], 16 * t + (4 * c + n + 5))
                            mm3(banks[6 + c % 2][:, kb * P:S], rv_hi[:, kb, w], rv_lo[:, kb, w],
                                ws_hi[:, KOFF[kb]:KOFF[kb + 1]], ws_lo[:, KOFF[kb]:KOFF[kb + 1]], n == 0,
                                n == TB - 1).then_inc(s["summed"], 1)

                    def gates_half(slot, half):
                        for k in range(4 * half, 4 * half + 4):
                            w = slice(k * P, (k + 1) * P)
                            last = mm3(banks[3][:], w_hi[:, slot, w], w_lo[:, slot, w], xn_hi[:, k, :], xn_lo[:, k, :],
                                       k == 0, k == KT - 1)
                        return last

                    pe.wait_ge(s["staged_lo"], 6 * t + 3)
                    score(0)
                    for c in range(4):
                        if c == 1:
                            pe.wait_ge(s["staged_lo"], 6 * t + 5)
                        if c == 2:
                            pe.wait_ge(s["staged_lo"], 6 * t + 6)
                        if c < 3:
                            score(c + 1)
                        slot = ready(pe, fgr, c, t, 4)
                        values(c)
                        pe.wait_ge(s["gate"], 4 * t + (c + 1))
                        gates_half(slot, 0)
                        pe.wait_ge(s["out"], 4 * t + (c + 3))
                        nc.tensor.matmul(banks[4][:], ones[:], r_raw[:, 4 * t + c, :], start=True,
                                         stop=True).then_inc(s["mean"], 1)
                        gates_half(slot, 1).then_inc(used, 1)
                        pe.wait_ge(s["square"], 4 * t + (c + 1))
                        pe.wait_ge(s["root"], 4 * t + (c + 1))
                        nc.tensor.matmul(banks[5][:], ones[:], gn_sq[:], start=True, stop=True).then_inc(s["var"], 1)

            def act_part(act):
                begin(act)
                act.sem_inc(s["out"], 2)
                act.sem_inc(s["root"], 1)
                act.sem_inc(s["gate"], 1)
                with act.Fori(0, 2) as t:
                    def stage_qk(pair):
                        nc.scalar.activation(rq_hi[:], r_qk[:, 2 * t + pair, :], ACT.Copy).then_inc(s["staged_hi"], 1)
                        nc.scalar.activation(rk_hi[:], r_qk[:, 2 * t + (4 + pair), :], ACT.Copy).then_inc(s["staged_hi"], 1)

                    def stage_v(pair):
                        nc.scalar.activation(rv_hi[:], r_v[:, :, bass.ds(t * 4 * P + pair * 2 * P, 2 * P)],
                                             ACT.Copy).then_inc(s["staged_hi"], 1)

                    act.wait_ge(s["summed"], 16 * t + 8)
                    stage_qk(0)
                    stage_v(0)
                    def highs(c):
                        for n, kb in enumerate(ORDER_K):
                            act.wait_ge(s["weighted"], 16 * t + (4 * c + n + 5))
                            act.wait_ge(s["summed"], 16 * t + (4 * c + n + 5))
                            nc.scalar.activation(ws_hi[:, KOFF[kb]:KOFF[kb + 1]], weighted[:, KOFF[kb]:KOFF[kb + 1]],
                                                 ACT.Copy).then_inc(s["hi"], 1)

                    highs(0)
                    for c in range(4):
                        if c == 0:
                            act.wait_ge(s["scored"], 16 * t + 8)
                            stage_qk(1)
                        ahead(high_part, act, fgr, c, t, 4)
                        act.wait_ge(s["summed"], 16 * t + (4 * c + 12))
                        nc.scalar.activation(r_raw[:, 4 * t + c, :], banks[6 + c % 2][:], ACT.Copy).then_inc(s["out"], 1)
                        if c == 1:
                            stage_v(1)
                        act.wait_ge(s["centred"], 4 * t + (c + 1))
                        apart(act)
                        nc.scalar.activation(gn_sq[:], r_raw[:, 4 * t + c, :], ACT.Square).then_inc(s["square"], 1)
                        if c < 3:
                            highs(c + 1)
                        act.wait_ge(s["var"], 4 * t + (c + 1))
                        act.wait_ge(s["done"], 4 * t + (c + 1))
                        nc.scalar.activation(gn_r[:], banks[5][:], ACT.Sqrt, bias=col[:, COLS["gneps"]:COLS["gneps"] + 1],
                                             scale=1.0 / P).then_inc(s["root"], 1)
                        finished(act, fgr, c, t, 4)
                        apart(act)
                        nc.scalar.activation(r_qk[:, 2 * t + (c // 2 + 4 * (c % 2)), :], banks[3][:],
                                             ACT.Copy).then_inc(s["gate"], 1)
                for c in range(8):
                    tile = c // 2 + 4 * (c % 2)
                    act.wait_ge(s["gate"], c + 2)
                    nc.scalar.activation(r_qk[:, tile, :], r_qk[:, tile, :], ACT.Silu).then_inc(s["gate"], 1)

            def dve_part(dve):
                begin(dve)
                dve.sem_inc(s["weighted"], 4)
                dve.sem_inc(s["done"], 1)
                with dve.Fori(0, 2) as t:
                    def weigh(c, blocks):
                        for n in blocks:
                            kb = ORDER_K[n]
                            if n == 0:
                                dve.wait_ge(decay_in, 64 * t + (16 * c + 16))
                            dve.wait_ge(s["scored"], 16 * t + (4 * c + (1, 3, 3, 4)[n]))
                            dve.wait_ge(s["lo"], 16 * t + (4 * c + n + 1))
                            nc.vector.tensor_tensor(weighted[:, KOFF[kb]:KOFF[kb + 1]], score_bank(kb),
                                                    decay[:, c % 2, 0:S - kb * P], ALU.mult).then_inc(s["weighted"], 1)

                    weigh(0, range(TB))
                    for c in range(4):
                        ahead(low_part, dve, fgr, c, t, 4)
                        dve.wait_ge(s["mean"], 4 * t + (c + 1))
                        nc.vector.scalar_tensor_tensor(r_raw[:, 4 * t + c, :], banks[4][:], -1.0 / P,
                                                       r_raw[:, 4 * t + c, :], ALU.mult, ALU.add).then_inc(s["centred"], 1)
                        if c < 3:
                            weigh(c + 1, range(TB))
                        dve.wait_ge(s["root"], 4 * t + (c + 2))
                        nc.vector.reciprocal(gn_r[:], gn_r[:]).then_inc(s["recip"], 1)
                        dve.wait_ge(s["recip"], 4 * t + (c + 1))
                        nc.vector.scalar_tensor_tensor(r_raw[:, 4 * t + c, :], r_raw[:, 4 * t + c, :],
                                                       col[:, bass.ds(t * 4 + (COLS["ret"] + c), 1)], gn_r[:], ALU.mult,
                                                       ALU.mult).then_inc(s["done"], 1)
                for c in range(8):
                    dve.wait_ge(s["gate"], 10 + c)
                    dve.wait_ge(s["done"], c + 2)
                    nc.vector.tensor_tensor(r_raw[:, c, :], r_raw[:, c, :], r_qk[:, c // 2 + 4 * (c % 2), :],
                                            ALU.mult).then_inc(s["gated"], 1)

            def pool_part(pool):
                begin(pool)
                pool.sem_inc(s["lo"], 4)
                with pool.Fori(0, 2) as t:
                    def decays_in(c):
                        pool.wait_ge(s["weighted"], 16 * t + (4 * c + 1))
                        pool.dma_start(decay[:, c % 2, :], decays[4 * t + c]).then_inc(decay_in, 16)

                    def stage_qk(pair):
                        for n, (to, hi) in enumerate(((rq_lo, rq_hi), (rk_lo, rk_hi))):
                            pool.wait_ge(s["staged_hi"], 6 * t + (3 * pair + n + 1))
                            nc.gpsimd.tensor_tensor(to[:], r_qk[:, 2 * t + (4 * n + pair), :], hi[:],
                                                    ALU.subtract).then_inc(s["staged_lo"], 1)

                    def stage_v(pair):
                        pool.wait_ge(s["staged_hi"], 6 * t + (3 * pair + 3))
                        nc.gpsimd.tensor_tensor(rv_lo[:], r_v[:, :, bass.ds(t * 4 * P + pair * 2 * P, 2 * P)], rv_hi[:],
                                                ALU.subtract).then_inc(s["staged_lo"], 1)

                    decays_in(0)
                    stage_qk(0)
                    stage_v(0)
                    for c in range(4):
                        if c < 3:
                            decays_in(c + 1)
                        if c == 2:
                            stage_v(1)
                        for n, kb in enumerate(ORDER_K):
                            pool.wait_ge(s["hi"], 16 * t + (4 * c + n + 1))
                            nc.gpsimd.tensor_tensor(ws_lo[:, KOFF[kb]:KOFF[kb + 1]], weighted[:, KOFF[kb]:KOFF[kb + 1]],
                                                    ws_hi[:, KOFF[kb]:KOFF[kb + 1]], ALU.subtract).then_inc(s["lo"], 1)
                        if c == 0:
                            stage_qk(1)

            return [(v_act, v_pe, v_dve, skip), (act_part, pe_part, dve_part, pool_part, (s["gated"], 8))]

        split = (xn_hi, xn_lo)
        natural = list(range(KT))

        n_mix1 = norm("n_mix1", x, natural, COLS["mix1"], (x_in, 16), 7, D, split, dma=True)
        parts.append(n_mix1)
        front = mixer1(n_mix1[4])
        parts.extend(front)
        m_b1 = merge("b1", [front[-1][4]], m1_hi, m1_lo, m1_temps,
                     [(2, 0, 2, y1[:, 0:4, :], y1_hi[:, 0:4, :], y1_lo[:, 0:4, :]),
                      (2, 4, 3, y1[:, 4:8, :], y1_hi[:, 4:8, :], y1_lo[:, 4:8, :])], 3, COLS["bgate"])
        n_ffn0 = norm("n_ffn0", x, natural, COLS["ffn0"], m_b1[4], 7, D, split)
        f0 = feed_forward("f0", 1.0, n_ffn0[4])
        n_fin1 = norm("n_fin1", x, ORDER, COLS["fin1"], f0[4], 7, D)
        n_ffn1 = norm("n_ffn1", x, ORDER, COLS["ffn1"], (n_fin1[4][0], n_fin1[4][1] - KT + 1), 7, D, split)
        f1 = feed_forward("f1", 0.5, n_ffn1[4])
        parts.extend([m_b1, n_ffn0, f0, n_fin1, n_ffn1, f1])
        n_mix2 = norm("n_mix2", x, ORDER, COLS["mix2"], f1[4], 7, D, split)
        second = mixer2(n_mix2, f1[4])
        parts.extend(second)
        m_b2 = merge("b2", [second[-1][4]], m2_hi, m2_lo, m2_temps,
                     [(2, 0, 2, a_raw[:, :, :], a_hi, a_lo), (3, 0, 3, r_raw[:, :, :], r_hi, r_lo)], 4, None)
        n_ffn2 = norm("n_ffn2", x, natural, COLS["ffn2"], m_b2[4], 7, D, split)
        f2 = feed_forward("f2", 0.5, n_ffn2[4])
        n_fin2 = norm("n_fin2", x, ORDER, COLS["fin2"], f2[4], 7, D)
        parts.extend([m_b2, n_ffn2, f2, n_fin2])
        final_done = n_fin2[4]

        block = top.enter_context(nc.Block())

        @block.sync
        def _(sp):
            sp.dma_start(x[:], xt.rearrange("p (k s) -> p k s", s=S)).then_inc(x_in, 16)
            for t, at in ((ident, 0), (col, 1)):
                sp.dma_start(t[:], cols[:, at * P:(at + 1) * P]).then_inc(consts_in, 16)
            for slot in range(2):
                sp.dma_start(w_raw[:, slot, :], stream[slot]).then_inc(loaded[slot], 16)
            sp.dma_start(bias_tri[:], tables[:, S:2 * S]).then_inc(consts_in, 16)
            sp.dma_start(bias_chunk[:], tables[:, 2 * S:3 * S]).then_inc(consts_in, 16)
            sp.dma_start(cumul_raw[:], tables[:, 0:S]).then_inc(consts_in, 16)
            sp.dma_start(w2_sb[:], w2.rearrange("p (t d) -> p t d", d=P)).then_inc(consts_in, 16)
            with sp.Fori(1, CHUNKS // 2) as i:
                for slot in range(2):
                    sp.wait_ge(split_lo, 2 * i + (slot - 1))
                    sp.dma_start(w_raw[:, slot, :], stream[2 * i + slot]).then_inc(loaded[slot], 16)
            if CHUNKS % 2:
                sp.wait_ge(split_lo, CHUNKS - 2)
                sp.dma_start(w_raw[:, 0, :], stream[CHUNKS - 1]).then_inc(loaded[0], 16)
            sp.wait_ge(final_done[0], final_done[1])
            sp.dma_start(out.rearrange("p (k s) -> p k s", s=S), x[:]).then_inc(stored, 16)
            sp.wait_ge(stored, 16)

        @block.scalar
        def _(act):
            act.wait_ge(consts_in, 96)
            for c in range(LOOKAHEAD):
                high_part(act, *place(0, c))
            for part in parts:
                part[0](act)

        @block.tensor
        def _(pe):
            pe.sem_inc(used, RING)
            pe.wait_ge(consts_in, 96)
            pe.wait_ge(consts_made, 2)
            for part in parts:
                part[1](pe)

        @block.vector
        def _(dve):
            nc.vector.memset(ones[:], 1.0).then_inc(consts_made, 1)
            dve.wait_ge(consts_in, 96)
            for c in range(LOOKAHEAD):
                low_part(dve, *place(0, c))
            for part in parts:
                part[2](dve)

        @block.gpsimd
        def _(pool):
            pool.wait_ge(consts_in, 96)
            nc.gpsimd.tensor_copy(cumul[:], cumul_raw[:]).then_inc(consts_made, 1)
            for part in parts:
                part[3](pool)


def _tiles(w):
    k, n = w.shape
    return w.reshape(k // P, P, n // P, P).transpose(2, 1, 0, 3).reshape(n // P, P, k)


def _token_major(w):
    k, n = w.shape
    per = CW // n
    return w.reshape(k // P // per, per, P, n).transpose(0, 2, 1, 3).reshape(-1, P, CW)


def _pad(w, n=P):
    return np.concatenate([w, np.zeros((w.shape[0], n - w.shape[1]), w.dtype)], 1)


def _gate_up(gate, up):
    return np.stack([_tiles(gate), _tiles(up)], 1).reshape(-1, P, CW)


def _column(v):
    return v.reshape(-1, P).T


def pack_first(a):
    w = a["w_in"][0]
    at = np.cumsum([0, 512, 512, 512, 8, 256, 128, 32, D, D])
    qa, ka, va, fa, cq, ckv, kr, ga, gb = (w[:, i:j] for i, j in zip(at[:-1], at[1:]))
    fk = np.concatenate([_pad(fa, 64), kr, kr], 1)
    wq = a["w_q_up"][0].reshape(256, 8, 96)
    q_up = np.concatenate([np.concatenate([wq, np.zeros((256, 8, 32), w.dtype)], 2).reshape(256, 1024)], 1)
    wkv = a["w_kv_up"][0].reshape(P, 8, P)
    k_up = np.concatenate([wkv[:, :, :64], np.zeros((P, 8, 64), w.dtype)], 2).reshape(P, CW)
    v_up = _pad(wkv[:, :, 64:].reshape(P, 512), CW)
    merge = np.stack([_tiles(ga), _tiles(gb),
                      np.concatenate([_tiles(a["w_branch_a"][0]), _tiles(a["w_branch_b"][0])], 2)], 1)
    return [_tiles(qa), _tiles(ka), _token_major(va), _tiles(fk), _tiles(cq), _tiles(ckv),
            _tiles(q_up).reshape(2, 4, P, 256).transpose(0, 2, 1, 3).reshape(2, P, CW), k_up[None], v_up[None],
            merge.reshape(-1, P, CW), _tiles(a["w_out"][0]),
            _gate_up(a["w_ffn_gate"][0], a["w_ffn_up"][0]), a["w_ffn_down"][0].reshape(FT, P, CW)]


def pack_cols(a):
    cols = np.zeros((P, P), np.float32)

    def put(name, v):
        cols[:v.shape[0], COLS[name]:COLS[name] + v.shape[1]] = v

    for name, key in (("mix1", "norm_mix_g"), ("qa", "q_a_norm_g"), ("kva", "kv_a_norm_g"), ("bgate", "b_gate"),
                      ("ffn0", "norm_ffn_g"), ("fin1", "norm_final_g"), ("ffn1", "ffn1_norm_2"),
                      ("mix2", "mix_norm_2"), ("ret", "ret_gn_gain_2"), ("ffn2", "ffn2_norm_2"),
                      ("fin2", "final_norm_2")):
        put(name, _column(a[key].reshape(-1)))
    cols[0:8, COLS["bf"]] = a["b_forget"].reshape(-1)
    half = np.float32(10000.0) ** (-np.arange(16, dtype=np.float32) / 16)
    cols[64:96, COLS["freq"]] = np.tile(half, 2)
    cols[64:96, COLS["sgn"]] = np.repeat(np.float32([-1, 1]), 16)
    cols[:, COLS["eps"]] = EPS
    cols[:, COLS["gneps"]] = GN_EPS
    cols[:, COLS["one"]] = 1.0
    put("pos", a["cmp_pos_emb_2"][0].reshape(16, P).T)
    return np.concatenate([np.eye(P, dtype=np.float32), cols], 1)


def shape_tables():
    row, at = np.arange(P)[:, None], np.arange(S)[None, :]
    cumul = np.where(at >= row, -8.0, 0.0)
    tri = np.where(at - (S - P) > row, -1e30, 0.0)
    chunk = np.where((at - (S - P)) // 64 > row // 64, -1e30, 0.0)
    return np.concatenate([cumul, tri, chunk], 1).astype(np.float32)


def _twice(w):
    return np.concatenate([w, w], 1)


def pack_second(a):
    w = a["w_in_2"][0]
    at = np.cumsum([0, D, P, P, P, P, P, P, 48, S, S, D, D, D, D])
    (q, kc, vc, ks, vs, kw, vw, g, rq, rk, rv, rg, ga, gr) = (w[:, i:j] for i, j in zip(at[:-1], at[1:]))

    def groups(w):
        return np.concatenate([_twice(w[:, :64]), _twice(w[:, 64:])], 1)

    order = np.concatenate([np.arange(0, 16), np.arange(32, 48), np.arange(16, 32), np.arange(48, 64)])
    order = (64 * np.arange(8)[:, None] + order).reshape(-1)
    merge = np.stack([_tiles(ga), _tiles(gr), _tiles(a["w_branch_nsa_2"][0]), _tiles(a["w_branch_ret_2"][0])], 1)

    def hidden(w):
        return _tiles(w).reshape(2, P, 2, CW).transpose(0, 2, 1, 3).reshape(4, P, CW)

    return [_gate_up(a["ffn1_w_gate_2"][0], a["ffn1_w_up_2"][0]), a["ffn1_w_down_2"][0].reshape(FT, P, CW),
            _tiles(q), _tiles(groups(ks)), _tiles(groups(kw)), _tiles(groups(kc)), _tiles(groups(vc)),
            _token_major(np.concatenate([vs, vw], 1)), _tiles(_pad(g)), hidden(a["cmp_k_w1_2"][0]),
            hidden(a["cmp_v_w1_2"][0]), _tiles(rq[:, order]), _tiles(rk[:, order]), _token_major(rv[:, :S]),
            _token_major(rv[:, S:]), _tiles(rg), merge.reshape(-1, P, CW), _tiles(a["w_out_2"][0]),
            _gate_up(a["ffn2_w_gate_2"][0], a["ffn2_w_up_2"][0]), a["ffn2_w_down_2"][0].reshape(FT, P, CW)]


def second_tables():
    row = np.arange(P) % 64

    def rope(positions, freq, sign, rotated):
        angle = positions.astype(np.float32)[None, :] * freq[:, None]
        cos = np.where(rotated[:, None], np.cos(angle), 1.0)
        sin = np.where(rotated[:, None], sign[:, None] * np.sin(angle), 0.0)
        return [cos, sin]

    f16 = np.float32(500000.0) ** (-(np.arange(8, dtype=np.float32) * np.float32(2.0) / np.float32(16)))
    f64 = np.float32(10000.0) ** (-(np.arange(32, dtype=np.float32) * np.float32(2.0) / np.float32(64)))
    nsa = (f16[row % 8], np.where(row < 8, -1.0, 1.0), row < 16)
    ret = (f64[(row // 32) * 16 + row % 16], np.where(row % 32 < 16, -1.0, 1.0), row < 64)
    tokens, windows = np.arange(S), np.tile(16 * np.arange(32) + 31, 2)
    query = np.arange(P)[:, None, None] + P * np.arange(TB)[None, :, None]
    seen = (16 * np.arange(32) + 31 <= query) & (np.arange(32) < 31)
    rows = [*rope(tokens, *nsa), *rope(tokens, *ret), *rope(windows, *nsa),
            np.where(seen, 0.0, -1e30).reshape(P, P), seen.reshape(P, P)]
    return np.concatenate([r.astype(np.float32) for r in rows], 1)


def decay_tables():
    head = np.arange(8)[:, None, None]
    gap = np.arange(S)[None, None, :] - np.arange(P)[None, :, None]
    return np.where(gap >= 0, 0.125 * (1.0 - 2.0 ** (-5.0 - head)) ** np.maximum(gap, 0), 0.0).astype(np.float32)


def kernel(**inputs):
    from concourse import bacc
    from concourse.bass_utils import run_bass_kernel_spmd

    a = {k: np.asarray(v) for k, v in inputs.items()}
    nc = bacc.Bacc("TRN2", target_bir_lowering=False, num_devices=1)
    data = {
        "stream": np.concatenate(pack_first(a) + pack_second(a)),
        "xt": np.ascontiguousarray(a["x"][0].T.reshape(KT, P, S).transpose(1, 0, 2).reshape(P, -1)),
        "cols": pack_cols(a),
        "tables": shape_tables(),
        "rows": second_tables(),
        "decays": decay_tables(),
        "pos": np.ascontiguousarray(a["positions"].reshape(-1)),
        "w2": np.concatenate([_twice(w[0].reshape(2, P, 64)[half]) for w in (a["cmp_k_w2_2"], a["cmp_v_w2_2"])
                              for half in range(2)], 1),
    }
    args = {n: nc.dram_tensor(n, v.shape, mybir.dt.from_np(v.dtype), kind="ExternalInput").ap()
            for n, v in data.items()}
    out = nc.dram_tensor("out", (P, KT * S), F32, kind="ExternalOutput").ap()
    build_program(nc, **args, out=out)
    got = run_bass_kernel_spmd(nc, [data], core_ids=[0]).results[0]["out"]
    return np.ascontiguousarray(got.reshape(P, KT, S).transpose(2, 1, 0).reshape(1, S, D))
```

```python
from contextlib import ExitStack

import numpy as np

import concourse.bass as bass
from concourse import mybir

P = 128
D = 1024
S = 512
KT = D // P
TB = S // P
FF = 2816
FT = FF // P
RING = 4
LOOKAHEAD = 2
CW = KT * P
EPS = 1e-6
GN_EPS = 1e-5
OFF = [P * (b * (b + 1) // 2) for b in range(TB + 1)]
KOFF = [sum(S - P * j for j in range(b)) for b in range(TB + 1)]
ALU = mybir.AluOpType
ACT = mybir.ActivationFunctionType
AX = mybir.AxisListType
F32 = mybir.dt.float32
F32R = mybir.dt.float32r
I32 = mybir.dt.int32

TWO_PI = [6.28125, 0.00193023681640625, 5.0703634e-06, 2 * np.pi]
MAGIC = 12582912.0
PI_BELOW = 3.1415925
HALF_PI = float(np.float32(np.pi / 2))
SWAP16 = [(n + 16) % 32 for n in range(32)]
SWAP8 = [n + 8 if n < 8 else n - 8 if n < 16 else n for n in range(32)]

STAGES = [
    ("b1_qk", 8), ("b1_c", 3), ("b1_fk", 1), ("b1_v", 4), ("b1_up", 4),
    ("b1_gates", 16), ("b1_merge", 8), ("b1_out", 8), ("f0_in", 2 * FT), ("f0_down", FT),
    ("f1_in", 2 * FT), ("f1_down", FT),
    ("b2_cmp", 4), ("b2_v", 2), ("b2_g", 1), ("b2_w1_q", 16), ("b2_k", 4), ("b2_rqk", 8), ("b2_rv", 8),
    ("b2_gr", 8), ("b2_merge", 32), ("b2_out", 8), ("f2_in", 2 * FT), ("f2_down", FT),
]
FIRST = {}
_n = 0
for _name, _count in STAGES:
    FIRST[_name] = _n
    _n += _count
CHUNKS = _n

COLS = {}
_n = 0
for _name, _count in [("mix1", 8), ("qa", 2), ("kva", 1), ("bgate", 16), ("ffn0", 8), ("fin1", 8), ("ffn1", 8),
                      ("mix2", 8), ("ret", 8), ("ffn2", 8), ("fin2", 8), ("freq", 1), ("pos", 16), ("bf", 8),
                      ("sgn", 1), ("eps", 1),
                      ("one", 1), ("gneps", 1)]:
    COLS[_name] = _n
    _n += _count
NCOLS = _n


def build_program(nc, stream, xt, cols, tables, rows, decays, pos, w2, out):
    top = ExitStack()
    with top:
        origin = -(-nc.sbuf_base // 32) * 32
        top.enter_context(nc.sbuf_tensor("arena", [P, (nc.sbuf_top - nc.sbuf_base) // 4 - 16], F32))

        def sb(name, shape, dt, at):
            assert origin + at + 4 * int(np.prod(shape[1:])) <= nc.sbuf_usable_end, name
            return nc.alloc_sbuf_tensor_at(name, shape, dt, offset=origin + at)

        def sem(name):
            return top.enter_context(nc.semaphore(name))

        K = 1024
        T2 = 2 * K
        w_raw = sb("w_raw", [P, 2, CW], F32, 0)
        w_hi = sb("w_hi", [P, RING, CW], F32R, 8 * K)
        w_lo = sb("w_lo", [P, RING, CW], F32R, 24 * K)
        x = sb("x", [P, KT, S], F32, 40 * K)
        xn_hi = sb("xn_hi", [P, KT, S], F32R, 56 * K)
        xn_lo = sb("xn_lo", [P, KT, S], F32R, 72 * K)
        ident = sb("ident", [P, P], F32, 88 * K)
        ones = sb("ones", [P, P], F32, 88 * K + 512)
        col = sb("col", [P, P], F32, 89 * K)
        cumul = sb("cumul", [P, S], F32R, 90 * K)
        bias_tri = sb("bias_tri", [P, S], F32, 92 * K)
        bias_chunk = sb("bias_chunk", [P, S], F32, 94 * K)
        norm_r = sb("norm_r", [P, S], F32, 96 * K)
        small = sb("small", [P, 128], F32, 98 * K)
        w2_sb = sb("w2_sb", [P, 4, P], F32, 99 * K)
        A0 = 101 * K
        N0 = 199 * K
        cumul_raw = sb("cumul_raw", [P, S], F32, 195 * K)
        sq = sb("sq", [P, 2, S], F32, N0)
        xg = sb("xg", [P, 2, S], F32, N0 + 4 * K)
        h_hi = sb("h_hi", [P, FT * S], F32R, A0)
        h_lo = sb("h_lo", [P, FT * S], F32R, A0 + 44 * K)
        silu = sb("silu", [P, 2, S], F32, A0 + 88 * K)
        hid = sb("hid", [P, 2, S], F32, A0 + 92 * K)

        banks = [top.enter_context(nc.psum_tensor(f"bank{b}", [P, S], F32)) for b in range(8)]

        loaded = [sem("w_loaded0"), sem("w_loaded1")]
        split_hi = sem("w_split_hi")
        split_lo = sem("w_split_lo")
        used = sem("chunks_used")
        consts_in = sem("consts_in")
        consts_made = sem("consts_made")
        x_in = [sem("x_in0"), sem("x_in1")]
        passed = sem("passed")
        stored = sem("stored")

        def place(first, j, i=0, n=0):
            c = first + j
            return c // RING + i * (n // RING), c % RING

        def high_part(act, ring, slot):
            act.wait_ge(loaded[slot % 2], 32 * ring + 16 * (slot // 2 + 1))
            act.wait_ge(used, RING * ring + (slot + 1))
            nc.scalar.activation(w_hi[:, slot, :], w_raw[:, slot % 2, :], ACT.Copy).then_inc(split_hi, 1)

        def low_part(dve, ring, slot):
            dve.wait_ge(split_hi, RING * ring + (slot + 1))
            nc.vector.tensor_tensor(w_lo[:, slot, :], w_raw[:, slot % 2, :], w_hi[:, slot, :],
                                    ALU.subtract).then_inc(split_lo, 1)

        def ahead(part, eng, first, j, i=0, n=0):
            if n or first + j + LOOKAHEAD < CHUNKS:
                part(eng, *place(first, j + LOOKAHEAD, i, n))

        def apart(eng):
            eng.sem_inc(passed, 1)

        def finished(eng, first, j, i=0, n=0):
            ring, slot = place(first, j, i, n)
            eng.wait_ge(used, RING * ring + (slot + 1 + RING))

        def ready(pe, first, j, i=0, n=0):
            ring, slot = place(first, j, i, n)
            pe.wait_ge(split_lo, RING * ring + (slot + 1))
            return slot

        def mm3(to, a_hi, a_lo, b_hi, b_lo, start=True, stop=True):
            nc.tensor.matmul(to, a_hi, b_hi, start=start, stop=False, skip_group_check=True)
            nc.tensor.matmul(to, a_hi, b_lo, start=False, stop=False, skip_group_check=True)
            return nc.tensor.matmul(to, a_lo, b_hi, start=False, stop=stop, skip_group_check=True)

        def tile_chunk(slot, to, b_hi, b_lo, at=0, tiles=KT, normed=None):
            order = normed[1] if normed else list(range(tiles))
            for n, k in enumerate(order):
                if normed:
                    nc.tensor.wait_ge(normed[0][0], normed[0][1] - len(order) + n + 1)
                last = mm3(to, w_hi[:, slot, (at + k) * P:(at + k + 1) * P], w_lo[:, slot, (at + k) * P:(at + k + 1) * P],
                           b_hi[:, k, :], b_lo[:, k, :], n == 0, n == tiles - 1)
            return last

        norm_sems = {k: sem(f"norm_{k}") for k in ("squared", "summed", "root", "recip", "scaled", "hi", "lo", "low")}
        norms = dict.fromkeys(norm_sems, 0)

        def count_up(**added):
            before = dict(norms)
            for k, n in added.items():
                norms[k] += n
            return before

        def norm(name, src, order, gain, source_done, bank, width, dst=None,
                 between=None):
            s = norm_sems
            count = len(order)
            parts_of = count if dst else 0
            b = count_up(squared=count, summed=count, root=1, recip=1, scaled=count, hi=parts_of, lo=parts_of)

            def act_part(act):
                for n, k in enumerate(order):
                    if between:
                        act.wait_ge(x_in[n // 4], (32, 16)[n // 4])
                    else:
                        act.wait_ge(source_done[0], source_done[1] + n)
                    if n >= 2:
                        act.wait_ge(s["summed"], b["summed"] + n - 1)
                    nc.scalar.activation(sq[:, n % 2, :], src[:, k, :], ACT.Square).then_inc(s["squared"], 1)
                if between:
                    between(act)
                act.wait_ge(s["summed"], b["summed"] + count)
                nc.scalar.activation(norm_r[:], banks[bank][:], ACT.Sqrt, bias=col[:, COLS["eps"]:COLS["eps"] + 1],
                                     scale=1.0 / width).then_inc(s["root"], 1)
                if dst:
                    for n, k in enumerate(order):
                        act.wait_ge(s["scaled"], b["scaled"] + n + 1)
                        nc.scalar.activation(dst[0][:, k, :], xg[:, n % 2, :], ACT.Copy).then_inc(s["hi"], 1)

            def pe_part(pe):
                for n in range(count):
                    pe.wait_ge(s["squared"], b["squared"] + n + 1)
                    nc.tensor.matmul(banks[bank][:], ones[:], sq[:, n % 2, :], start=n == 0,
                                     stop=n == count - 1).then_inc(s["summed"], 1)

            def dve_part(dve):
                dve.wait_ge(s["root"], b["root"] + 1)
                nc.vector.reciprocal(norm_r[:], norm_r[:]).then_inc(s["recip"], 1)
                dve.wait_ge(s["recip"], b["recip"] + 1)
                for n, k in enumerate(order):
                    if dst and n >= 2:
                        dve.wait_ge(s["lo"], b["lo"] + n - 1)
                    to = xg[:, n % 2, :] if dst else src[:, k, :]
                    nc.vector.scalar_tensor_tensor(to, src[:, k, :], col[:, gain + k:gain + k + 1], norm_r[:],
                                                   ALU.mult, ALU.mult).then_inc(s["scaled"], 1)

            def pool_part(pool):
                if dst:
                    for n, k in enumerate(order):
                        pool.wait_ge(s["hi"], b["hi"] + n + 1)
                        nc.gpsimd.tensor_tensor(dst[1][:, k, :], xg[:, n % 2, :], dst[0][:, k, :],
                                                ALU.subtract).then_inc(s["lo"], 1)

            done = (s["lo"], b["lo"] + count) if dst else (s["scaled"], b["scaled"] + count)
            return act_part, pe_part, dve_part, pool_part, done

        ORDER = [7, 0, 1, 2, 3, 4, 5, 6]

        ffn_sems = {k: sem(f"ffn_{k}") for k in ("scaled", "silu", "product", "hi", "lo", "x")}
        ffns = [0]

        def feed_forward(name, factor, gain, source_done, order):
            first_in, first_down = FIRST[f"{name}_in"], FIRST[f"{name}_down"]
            s, m = ffn_sems, norm_sems
            nb = count_up(squared=KT, summed=KT, root=1, recip=1, hi=KT, low=KT)
            first_one, b = ffns[0] == 0, FT * ffns[0]
            x_before = KT * ffns[0]
            ffns[0] += 1
            N_IN, N_DOWN = 4, 4

            def pe_part(pe):
                slot = ready(pe, first_in, 0)
                pe.wait_ge(s["product"], b + 1)
                for n, k in enumerate(order):
                    pe.wait_ge(m["low"], nb["low"] + n + 1)
                    w = slice(k * P, (k + 1) * P)
                    last = mm3(banks[0][:], w_hi[:, slot, w], w_lo[:, slot, w], xn_hi[:, k, :], xn_lo[:, k, :], n == 0,
                               n == KT - 1)
                    if n == KT - 1:
                        last.then_inc(used, 1)
                    pe.wait_ge(m["squared"], nb["squared"] + n + 1)
                    nc.tensor.matmul(banks[7][:], ones[:], sq[:, n % 2, :], start=n == 0, stop=n == KT - 1,
                                     skip_group_check=True).then_inc(m["summed"], 1)
                for j in range(1, 4):
                    slot = ready(pe, first_in, j)
                    if j == 2:
                        pe.wait_ge(s["product"], b + 2)
                    tile_chunk(slot, banks[j][:], xn_hi, xn_lo).then_inc(used, 1)
                with pe.Fori(1, FT // 2) as i:
                    for j in range(4):
                        slot = ready(pe, first_in, j, i, N_IN)
                        if j % 2 == 0:
                            pe.wait_ge(s["product"], 2 * i + (b + j // 2 + 1))
                        tile_chunk(slot, banks[j][:], xn_hi, xn_lo).then_inc(used, 1)

                def down(j, k, start, stop, i=0, n=0):
                    pe.wait_ge(s["lo"], k + (b + 3))
                    slot = ready(pe, first_down, j, i, n)
                    for o in (4, 5, 6, 7, 0, 1, 2, 3):
                        w = slice(o * P, (o + 1) * P)
                        last = mm3(banks[o][:], w_hi[:, slot, w], w_lo[:, slot, w], h_hi[:, bass.ds(k * S, S)],
                                   h_lo[:, bass.ds(k * S, S)], start, stop)
                    last.then_inc(used, 1)

                pe.wait_ge(s["product"], b + FT + 2)
                for j in range(4):
                    down(j, j, j == 0, False)
                with pe.Fori(0, FT // 4 - 1) as i:
                    for j in range(4):
                        down(j + 4, i * 4 + (j + 4), False, False, i, N_DOWN)
                for j in range(FT // 4 * 4, FT):
                    down(j, j, False, j == FT - 1)

            def act_part(act):
                for n, k in enumerate(order):
                    act.wait_ge(source_done[0], source_done[1] + n)
                    if n >= 2:
                        act.wait_ge(m["summed"], nb["summed"] + n - 1)
                    nc.scalar.activation(sq[:, n % 2, :], x[:, k, :], ACT.Square).then_inc(m["squared"], 1)
                    nc.scalar.activation(xn_hi[:, k, :], x[:, k, :], ACT.Identity,
                                         scale=col[:, gain + k:gain + k + 1]).then_inc(m["hi"], 1)
                act.wait_ge(m["summed"], nb["summed"] + KT)
                nc.scalar.activation(norm_r[:], banks[7][:], ACT.Sqrt, bias=col[:, COLS["eps"]:COLS["eps"] + 1],
                                     scale=1.0 / D).then_inc(m["root"], 1)
                with act.Fori(0, FT // 2) as i:
                    for t in range(2):
                        ahead(high_part, act, first_in, 2 * t, i, N_IN)
                        act.wait_ge(s["scaled"], 4 * i + (2 * b + 2 * t + 1))
                        nc.scalar.activation(silu[:, t, :], silu[:, t, :], ACT.Silu).then_inc(s["silu"], 1)
                        ahead(high_part, act, first_in, 2 * t + 1, i, N_IN)
                        act.wait_ge(s["product"], 2 * i + (b + t + 3))
                        nc.scalar.activation(h_hi[:, bass.ds(i * 2 * S + t * S, S)], hid[:, t, :],
                                             ACT.Copy).then_inc(s["hi"], 1)
                stream_down(act, high_part)

            def stream_down(eng, part):
                with eng.Fori(0, FT // 4) as i:
                    for j in range(4):
                        ahead(part, eng, first_down, j, i, N_DOWN)
                for j in range(FT // 4 * 4, FT):
                    ahead(part, eng, first_down, j)

            def dve_part(dve):
                if first_one:
                    dve.sem_inc(s["product"], 2)
                for n, k in enumerate(order):
                    dve.wait_ge(m["hi"], nb["hi"] + n + 1)
                    nc.vector.scalar_tensor_tensor(xn_lo[:, k, :], x[:, k, :], col[:, gain + k:gain + k + 1],
                                                   xn_hi[:, k, :], ALU.mult, ALU.subtract).then_inc(m["low"], 1)
                dve.wait_ge(m["root"], nb["root"] + 1)
                nc.vector.reciprocal(norm_r[:], norm_r[:]).then_inc(m["recip"], 1)
                dve.wait_ge(m["recip"], nb["recip"] + 1)
                with dve.Fori(0, FT // 2) as i:
                    for t in range(2):
                        ahead(low_part, dve, first_in, 2 * t, i, N_IN)
                        dve.wait_ge(s["product"], 2 * i + (b + t + 1))
                        finished(dve, first_in, 2 * t, i, N_IN)
                        nc.vector.tensor_tensor(silu[:, t, :], banks[2 * t][:], norm_r[:], ALU.mult
                                                ).then_inc(s["scaled"], 1)
                        ahead(low_part, dve, first_in, 2 * t + 1, i, N_IN)
                        dve.wait_ge(s["lo"], 2 * i + (b + t + 1))
                        finished(dve, first_in, 2 * t + 1, i, N_IN)
                        nc.vector.tensor_tensor(hid[:, t, :], banks[2 * t + 1][:], norm_r[:], ALU.mult
                                                ).then_inc(s["scaled"], 1)
                        dve.wait_ge(s["scaled"], 4 * i + (2 * b + 2 * t + 2))
                        dve.wait_ge(s["silu"], 2 * i + (b + t + 1))
                        nc.vector.tensor_tensor(hid[:, t, :], silu[:, t, :], hid[:, t, :], ALU.mult
                                                ).then_inc(s["product"], 1)
                stream_down(dve, low_part)
                finished(dve, first_down, FT - 1)
                for k in ORDER:
                    nc.vector.scalar_tensor_tensor(x[:, k, :], banks[k][:], factor, x[:, k, :],
                                                   ALU.mult, ALU.add).then_inc(s["x"], 1)

            def pool_part(pool):
                if first_one:
                    pool.sem_inc(s["lo"], 2)
                with pool.Fori(0, FT // 2) as i:
                    for t in range(2):
                        pool.wait_ge(s["hi"], 2 * i + (b + t + 1))
                        nc.gpsimd.tensor_tensor(h_lo[:, bass.ds(i * 2 * S + t * S, S)], hid[:, t, :],
                                                h_hi[:, bass.ds(i * 2 * S + t * S, S)],
                                                ALU.subtract).then_inc(s["lo"], 1)

            return act_part, pe_part, dve_part, pool_part, (s["x"], x_before + 1)

        parts = []

        def link(eng, s):
            count = [0]

            def step(instruction):
                instruction.then_inc(s, 1)
                count[0] += 1
                eng.wait_ge(s, count[0])
            return step

        def skip(eng):
            pass

        W0 = A0 + 68 * K
        qs_hi = sb("qs_hi", [P, S], F32R, W0)
        qs_lo = sb("qs_lo", [P, S], F32R, W0 + T2)
        ks_hi = sb("ks_hi", [P, S], F32R, W0 + 2 * T2)
        ks_lo = sb("ks_lo", [P, S], F32R, W0 + 3 * T2)
        vs_hi = sb("vs_hi", [P, TB, P], F32R, W0 + 4 * T2)
        vs_lo = sb("vs_lo", [P, TB, P], F32R, W0 + 5 * T2)
        prob = sb("prob", [P, 2, OFF[TB]], F32, W0 + 6 * T2)
        pt_hi = sb("pt_hi", [P, OFF[TB]], F32R, W0 + 22 * K)
        pt_lo = sb("pt_lo", [P, OFF[TB]], F32R, W0 + 27 * K)
        bias_row = sb("bias_row", [P, S], F32, W0 + 34 * K)
        ident_r = sb("ident_r", [P, P], F32R, W0 + 32 * K)
        tri_r = sb("tri_r", [P, P], F32R, W0 + 32 * K + 512)
        top_s, neg_top, total, inverse = (small[:, 8 * n:8 * n + 8] for n in range(4))

        def scores_rows(qb):
            return slice(OFF[qb], OFF[qb + 1])

        SCORE_ORDER = (0, 2, 1, 3)

        def score_bank(qb):
            return (banks[0][:, 0:P], banks[1][:, 0:2 * P], banks[0][:, P:S], banks[2][:])[qb]

        def turns(eng, count, body):
            with eng.Fori(0, count - 1) as i:
                body(i, True)
            body(count - 1, False)

        def attention(name, start, q_raw, k_raw, v_raw, y, y_tile, scale, latent):
            s = {k: sem(f"{name}_{k}") for k in ("staged_hi", "staged_lo", "v_hi", "v_lo", "scored", "biased", "negated",
                                                 "exp", "inverse", "scaled", "turned", "hi", "lo", "summed", "out",
                                                 *(("gate",) if latent else ("bias", "mask")))}
            fg = FIRST["b1_gates"]
            rows = [slice(0, P)] * 2 if latent else [slice(0, 64), slice(64, P)]
            krows = slice(0, 64) if latent else slice(0, P)
            pairs = 4

            def begin(eng):
                for w in start:
                    eng.wait_ge(*w)

            def pe_part(pe):
                begin(pe)
                pe.sem_inc(s["scored"], 4)
                pe.sem_inc(s["turned"], 8)
                pe.sem_inc(s["summed"], 4)
                if not latent:
                    pe.wait_ge(s["mask"], 2)

                def score(i, j):
                    if latent:
                        pe.wait_ge(s["staged_lo"], 4 * i + 2 * (j + 1))
                    elif j % 2 == 0:
                        pe.wait_ge(s["staged_lo"], 2 * i + (j + 2))
                    r = rows[j % 2]
                    for place_of, qb in enumerate(SCORE_ORDER):
                        pe.wait_ge(s["biased"], 8 * i + (4 * j + max(place_of, 1) + 1))
                        at, n = slice(qb * P, (qb + 1) * P), (qb + 1) * P
                        last = mm3(score_bank(qb), qs_hi[r, at], qs_lo[r, at], ks_hi[r, 0:n], ks_lo[r, 0:n], True,
                                   latent)
                        if not latent:
                            last = nc.tensor.matmul(score_bank(qb)[:, qb * P:n], ident_r[:], tri_r[:], start=False,
                                                    stop=True, skip_group_check=True)
                        last.then_inc(s["scored"], 1)

                def turn(i, j, kb):
                    pe.wait_ge(s["lo"], 8 * i + (4 * j + kb + 1))
                    for qb in range(kb, TB):
                        if kb == 0:
                            pe.wait_ge(s["scaled"], 8 * i + (4 * j + qb + 1))
                        last = nc.tensor.transpose(banks[4 + kb % 2][:, (qb - kb) * P:(qb - kb + 1) * P],
                                                   prob[:, j, OFF[qb] + kb * P:OFF[qb] + (kb + 1) * P], ident[:])
                    last.then_inc(s["turned"], 1)

                def values(i, j, kb):
                    if kb == 0:
                        pe.wait_ge(s["out"], 2 * i + (j + 1))
                        pe.wait_ge(s["v_lo"], i + 1)
                    pe.wait_ge(s["lo"], 8 * i + (4 * j + kb + 3))
                    at = slice(KOFF[kb], KOFF[kb + 1])
                    mm3(banks[6 + j][:, kb * P:S], vs_hi[:, kb, :], vs_lo[:, kb, :], pt_hi[:, at], pt_lo[:, at],
                        kb == 0, kb == TB - 1).then_inc(s["summed"], 1)

                def gates(slot, tiles):
                    for k in tiles:
                        w = slice(k * P, (k + 1) * P)
                        last = mm3(banks[3][:], w_hi[:, slot, w], w_lo[:, slot, w], xn_hi[:, k, :], xn_lo[:, k, :],
                                   k == 0, k == KT - 1)
                    return last

                def body(i, more):
                    for j in range(2):
                        turn(i, j, 0)
                        turn(i, j, 1)
                        if latent:
                            slot = ready(pe, fg, 2 * j, i, 4)
                            pe.wait_ge(s["gate"], 4 * i + (2 * j + 1))
                            gates(slot, range(0, KT // 2))
                        turn(i, j, 2)
                        turn(i, j, 3)
                        if latent:
                            gates(slot, range(KT // 2, KT)).then_inc(used, 1)
                        if more:
                            score(i, j + 2)
                        for kb in range(TB):
                            values(i, j, kb)
                        if latent:
                            slot = ready(pe, fg, 2 * j + 1, i, 4)
                            pe.wait_ge(s["gate"], 4 * i + (2 * j + 2))
                            gates(slot, range(KT)).then_inc(used, 1)

                score(0, 0)
                score(0, 1)
                turns(pe, pairs, body)

            def act_part(act):
                begin(act)
                act.sem_inc(s["out"], 2)
                if latent:
                    act.sem_inc(s["gate"], 1)

                def stage(i, j):
                    tile = 2 * i + j if latent else i + j // 2
                    act.wait_ge(s["scored"], 8 * i + (4 * j + 4))
                    nc.scalar.activation(qs_hi[:], q_raw[:, tile, :], ACT.Copy).then_inc(s["staged_hi"], 1)
                    nc.scalar.activation(ks_hi[krows, :], k_raw[krows, tile, :], ACT.Copy).then_inc(s["staged_hi"], 1)

                def stage_v(i, n):
                    act.wait_ge(s["summed"], 8 * i + (8 * n + 4))
                    nc.scalar.activation(vs_hi[:], v_raw[:, :, bass.ds(i * P + n * P, P)], ACT.Copy).then_inc(s["v_hi"], 1)

                def exps(i, j, blocks):
                    act.wait_ge(s["negated"], 2 * i + (j + 1))
                    for qb in blocks:
                        at = prob[:, j % 2, scores_rows(qb)]
                        n = 4 * (j % 2) + qb
                        nc.scalar.activation(at, at, ACT.Exp, bias=neg_top[:, n:n + 1], scale=scale,
                                             accum_out=total[:, n:n + 1]).then_inc(s["exp"], 1)

                def highs(i, j, blocks):
                    for kb in blocks:
                        act.wait_ge(s["turned"], 8 * i + (4 * j + kb + 9))
                        act.wait_ge(s["summed"], 8 * i + (4 * j + kb + 1))
                        nc.scalar.activation(pt_hi[:, KOFF[kb]:KOFF[kb + 1]], banks[4 + kb % 2][:, 0:S - kb * P],
                                             ACT.Copy).then_inc(s["hi"], 1)

                def output(i, j):
                    act.wait_ge(s["summed"], 8 * i + (4 * j + 8))
                    r = slice(64 * j, 64 * j + 64)
                    nc.scalar.activation(y[r, i + y_tile, :], banks[6 + j][r, :], ACT.Copy).then_inc(s["out"], 1)

                def gate(i, j, n):
                    ahead(high_part, act, fg, 2 * j + n, i, 4)
                    finished(act, fg, 2 * j + n, i, 4)
                    apart(act)
                    nc.scalar.activation((q_raw, k_raw)[n][:, 2 * i + j, :], banks[3][:], ACT.Copy).then_inc(s["gate"], 1)

                def body(i, more):
                    for j in range(2):
                        if more and (latent or j == 0):
                            stage(i, j + 2)
                        highs(i, j, (0, 1))
                        if j == 0 or more:
                            exps(i, j + 1, (0, 1, 2))
                        highs(i, j, (2, 3))
                        if j == 0 or more:
                            exps(i, j + 1, (3,))
                        if latent:
                            gate(i, j, 0)
                        output(i, j)
                        if latent:
                            gate(i, j, 1)
                    if more:
                        stage_v(i, 1)

                stage(0, 0)
                stage_v(0, 0)
                if latent:
                    stage(0, 1)
                exps(0, 0, range(TB))
                turns(act, pairs, body)

            def dve_part(dve):
                begin(dve)
                dve.sem_inc(s["biased"], 4)
                dve.sem_inc(s["lo"], 2)

                def biased(i, j):
                    if not latent:
                        dve.wait_ge(s["bias"], 2 * i + (j + 1))
                    for place_of, qb in enumerate(SCORE_ORDER):
                        dve.wait_ge(s["scored"], 8 * i + (4 * j + max(place_of, 1) + 5))
                        if place_of == 0:
                            dve.wait_ge(s["turned"], 8 * i + (4 * j + 4))
                        apart(dve)
                        n = 4 * (j % 2) + qb
                        width = (qb + 1) * P
                        bias = bias_chunk[:, S - width:S] if latent else bias_row[:, 0:width]
                        nc.vector.tensor_tensor_reduce(prob[:, j % 2, scores_rows(qb)], score_bank(qb), bias, 1.0,
                                                       -3.0e38, ALU.add, ALU.max,
                                                       top_s[:, n:n + 1]).then_inc(s["biased"], 1)
                    dve.wait_ge(s["biased"], 8 * i + (4 * j + 8))
                    n = 4 * (j % 2)
                    nc.vector.tensor_scalar(neg_top[:, n:n + 4], top_s[:, n:n + 4], -scale, None,
                                            ALU.mult).then_inc(s["negated"], 1)

                def scaled(i, j):
                    dve.wait_ge(s["exp"], 8 * i + (4 * j + 4))
                    nc.vector.reciprocal(inverse[:, 4 * j:4 * j + 4], total[:, 4 * j:4 * j + 4]).then_inc(s["inverse"], 1)
                    dve.wait_ge(s["inverse"], 2 * i + (j + 1))
                    for qb in range(TB):
                        at = prob[:, j, scores_rows(qb)]
                        n = 4 * j + qb
                        nc.vector.tensor_scalar(at, at, inverse[:, n:n + 1], None, ALU.mult).then_inc(s["scaled"], 1)

                def lows(i, j):
                    for kb in range(TB):
                        dve.wait_ge(s["hi"], 8 * i + (4 * j + kb + 1))
                        at = slice(KOFF[kb], KOFF[kb + 1])
                        nc.vector.tensor_tensor(pt_lo[:, at], banks[4 + kb % 2][:, 0:S - kb * P], pt_hi[:, at],
                                                ALU.subtract).then_inc(s["lo"], 1)

                def body(i, more):
                    for j in range(2):
                        scaled(i, j)
                        if j == 0 or more:
                            biased(i, j + 1)
                        lows(i, j)
                        if latent:
                            for n in range(2):
                                ahead(low_part, dve, fg, 2 * j + n, i, 4)

                biased(0, 0)
                turns(dve, pairs, body)

            def pool_part(pool):
                begin(pool)
                if not latent:
                    nc.gpsimd.tensor_copy(ident_r[:], ident[:]).then_inc(s["mask"], 1)
                    nc.gpsimd.tensor_copy(tri_r[:], bias_tri[:, S - P:S]).then_inc(s["mask"], 1)

                def stage(i, j):
                    tile = 2 * i + j if latent else i + j // 2
                    n = 4 * i + 2 * j if latent else 2 * i + j
                    pool.wait_ge(s["staged_hi"], n + 1)
                    nc.gpsimd.tensor_tensor(qs_lo[:], q_raw[:, tile, :], qs_hi[:], ALU.subtract).then_inc(s["staged_lo"], 1)
                    pool.wait_ge(s["staged_hi"], n + 2)
                    nc.gpsimd.tensor_tensor(ks_lo[krows, :], k_raw[krows, tile, :], ks_hi[krows, :],
                                            ALU.subtract).then_inc(s["staged_lo"], 1)

                def stage_v(i, n):
                    pool.wait_ge(s["v_hi"], i + (n + 1))
                    nc.gpsimd.tensor_tensor(vs_lo[:], v_raw[:, :, bass.ds(i * P + n * P, P)], vs_hi[:],
                                            ALU.subtract).then_inc(s["v_lo"], 1)

                def bias(i, j):
                    pool.wait_ge(s["biased"], 8 * i + (4 * j + 4))
                    nc.gpsimd.tensor_copy(bias_row[:], negc[:, 2 * i + j, :]).then_inc(s["bias"], 1)

                def body(i, more):
                    if latent:
                        if more:
                            stage(i, 2)
                            stage(i, 3)
                            stage_v(i, 1)
                    elif more:
                        stage(i, 2)
                        bias(i, 2)
                        bias(i, 3)
                        stage_v(i, 1)

                if not latent:
                    bias(0, 0)
                stage(0, 0)
                stage_v(0, 0)
                if latent:
                    stage(0, 1)
                else:
                    bias(0, 1)
                turns(pool, pairs, body)

            return act_part, pe_part, dve_part, pool_part, (s["out"], 2 * pairs + 2), (s["gate"], 4 * pairs + 1) if latent else None

        qk_raw = sb("qk_raw", [P, 2 * TB, S], F32, A0)
        v_raw = sb("v_raw", [P, TB, S], F32, A0 + 16 * K)
        negc = sb("negc", [P, 8, S], F32, A0 + 24 * K)
        mq = sb("mq", [P, 8, S], F32, A0)
        mk = sb("mk", [P, 8, S], F32, A0 + 16 * K)
        mv = sb("mv", [P, TB, S], F32, A0 + 32 * K)
        c_hi = sb("c_hi", [P, 3, S], F32R, A0 + 40 * K)
        c_lo = sb("c_lo", [P, 3, S], F32R, A0 + 46 * K)
        y1 = sb("y1", [P, KT, S], F32, A0 + 52 * K)
        forget = sb("forget", [8, 4, S], F32, W0)
        lft_hi = sb("lft_hi", [P, 32], F32R, W0 + 8 * K)
        lft_lo = sb("lft_lo", [P, 32], F32R, W0 + 9 * K)
        rope_c = sb("rope_c", [P, S], F32, W0 + 32 * K)
        rope_s = sb("rope_s", [P, S], F32, W0 + 34 * K)
        rope_t = sb("rope_t", [P, S], F32, W0 + 14 * K)
        rope_i = sb("rope_i", [P, S], I32, W0 + 8 * K)
        rope_a = sb("rope_a", [P, S], F32, W0 + 10 * K)
        rope_k = sb("rope_k", [P, S], F32, W0 + 12 * K)

        def copies_out(name, first, count, dst, normed=None):
            s = sem(f"{name}_copied")

            def act_part(act):
                with act.Fori(0, count // 4) as i:
                    for j in range(4):
                        ahead(high_part, act, first, j, i, 4)

            def pe_part(pe):
                with pe.Fori(0, count // 4) as i:
                    for j in range(4):
                        slot = ready(pe, first, j, i, 4)
                        pe.wait_ge(s, 4 * i + (j + 1))
                        tile_chunk(slot, banks[j][:], xn_hi, xn_lo, normed=normed if j == 0 else None
                                   ).then_inc(used, 1)

            def dve_part(dve):
                dve.sem_inc(s, 4)
                with dve.Fori(0, count // 4) as i:
                    for j in range(4):
                        ahead(low_part, dve, first, j, i, 4)
                        finished(dve, first, j, i, 4)
                        nc.vector.tensor_copy(dst[:, 4 * i + j, :], banks[j][:]).then_inc(s, 1)

            return act_part, pe_part, dve_part, skip, (s, count + 4)

        def mixer1(norm_done):
            qk = copies_out("b1_qk", FIRST["b1_qk"], 8, qk_raw, (norm_done, list(range(KT))))
            s = {k: sem(f"b1_{k}") for k in ("v", "fk", "c", "f_dve", "f_act", "lft_t", "lft_hi", "lft_lo", "cum",
                                             "negc")}
            cq = norm("b1_cq", y1, [0, 1], COLS["qa"], (s["c"], 1), 1, 256, (c_hi, c_lo))
            ckv = norm("b1_ckv", y1, [2], COLS["kva"] - 2, (s["c"], 3), 2, 128, (c_hi, c_lo))
            fv, ff, fc = FIRST["b1_v"], FIRST["b1_fk"], FIRST["b1_c"]

            def pe_part(pe):
                qk[1](pe)
                for j in range(3):
                    slot = ready(pe, fc, j)
                    pe.wait_ge(qk[4][0], 8 + 2 + j)
                    tile_chunk(slot, banks[1 + j][:], xn_hi, xn_lo).then_inc(used, 1)
                slot = ready(pe, ff, 0)
                pe.wait_ge(qk[4][0], 8 + 1)
                tile_chunk(slot, banks[0][:], xn_hi, xn_lo).then_inc(used, 1)
                for j in range(4):
                    slot = ready(pe, fv, j)
                    for t in range(2):
                        k, w = 2 * j + t, slice(t * S, (t + 1) * S)
                        for tb in range(TB):
                            at = slice(tb * P, (tb + 1) * P)
                            last = mm3(banks[4 + tb][:], xn_hi[:, k, at], xn_lo[:, k, at], w_hi[:, slot, w],
                                       w_lo[:, slot, w], k == 0, k == KT - 1)
                    last.then_inc(used, 1)
                    if j == 1:
                        pe.wait_ge(s["c"], 3)
                        cq[1](pe)
                        ckv[1](pe)
                        pe.wait_ge(s["f_dve"], 3)
                        for tb in range(TB):
                            last = nc.tensor.transpose(banks[3][:, 8 * tb:8 * tb + 8],
                                                       forget[0:8, 0, tb * P:(tb + 1) * P], ident[0:8, 0:8])
                        last.then_inc(s["lft_t"], 1)
                pe.wait_ge(s["lft_lo"], 1)
                pe.wait_ge(s["fk"], 1)
                pe.wait_ge(*cq[4])
                pe.wait_ge(*ckv[4])
                for h in range(8):
                    if h >= 4:
                        pe.wait_ge(s["negc"], h - 3)
                    for tb in range(TB):
                        for n, part in enumerate((lft_hi, lft_lo)):
                            last = nc.tensor.matmul(banks[h % 4][:, tb * P:S],
                                                    part[:, 8 * tb + h:8 * tb + h + 1].to_broadcast([P, P]),
                                                    cumul[:, 0:S - tb * P], start=tb == 0 and n == 0,
                                                    stop=tb == TB - 1 and n == 1, skip_group_check=True)
                    last.then_inc(s["cum"], 1)

            def act_part(act):
                qk[0](act)
                for j in range(3):
                    ahead(high_part, act, fc, j)
                ahead(high_part, act, ff, 0)
                ahead(high_part, act, fv, 0)
                ahead(high_part, act, fv, 1)
                act.wait_ge(s["f_dve"], 2)
                nc.scalar.activation(forget[0:8, 2, :], forget[0:8, 1, :], ACT.Exp).then_inc(s["f_act"], 1)
                act.wait_ge(s["f_act"], 1)
                nc.scalar.activation(forget[0:8, 3, :], forget[0:8, 2, :], ACT.Ln,
                                     bias=col[0:8, COLS["one"]:COLS["one"] + 1]).then_inc(s["f_act"], 1)
                cq[0](act)
                ckv[0](act)
                act.wait_ge(s["lft_t"], 1)
                nc.scalar.activation(lft_hi[:], banks[3][:, 0:32], ACT.Copy).then_inc(s["lft_hi"], 1)
                ahead(high_part, act, fv, 2)
                ahead(high_part, act, fv, 3)

            def dve_part(dve):
                qk[2](dve)
                for j in range(3):
                    ahead(low_part, dve, fc, j)
                    finished(dve, fc, j)
                    nc.vector.tensor_copy(y1[:, j, :], banks[1 + j][:]).then_inc(s["c"], 1)
                ahead(low_part, dve, ff, 0)
                finished(dve, ff, 0)
                nc.vector.tensor_scalar(forget[0:8, 0, :], banks[0][0:8, :], col[0:8, COLS["bf"]:COLS["bf"] + 1], None,
                                        ALU.add).then_inc(s["f_dve"], 1)
                nc.vector.tensor_copy(y1[64:P, 7, :], banks[0][64:P, :]).then_inc(s["fk"], 1)
                dve.wait_ge(s["f_dve"], 1)
                nc.vector.scalar_tensor_tensor(forget[0:8, 1, :], forget[0:8, 0, :], -1.0, forget[0:8, 0, :], ALU.mult,
                                               ALU.min).then_inc(s["f_dve"], 1)
                ahead(low_part, dve, fv, 0)
                ahead(low_part, dve, fv, 1)
                dve.wait_ge(s["f_act"], 2)
                nc.vector.scalar_tensor_tensor(forget[0:8, 0, :], forget[0:8, 0, :], 0.0, forget[0:8, 3, :], ALU.min,
                                               ALU.subtract).then_inc(s["f_dve"], 1)
                cq[2](dve)
                dve.wait_ge(*cq[4])
                ckv[2](dve)
                dve.wait_ge(s["lft_hi"], 1)
                nc.vector.tensor_tensor(lft_lo[:], banks[3][:, 0:32], lft_hi[:], ALU.subtract).then_inc(s["lft_lo"], 1)
                ahead(low_part, dve, fv, 2)
                ahead(low_part, dve, fv, 3)
                finished(dve, fv, 3)
                for tb in range(TB):
                    nc.vector.tensor_copy(v_raw[:, tb, :], banks[4 + tb][:]).then_inc(s["v"], 1)
                for h in range(8):
                    dve.wait_ge(s["cum"], h + 1)
                    nc.vector.tensor_copy(negc[:, h, :], banks[h % 4][:]).then_inc(s["negc"], 1)

            def pool_part(pool):
                cq[3](pool)
                ckv[3](pool)

            front = (act_part, pe_part, dve_part, pool_part)
            att = attention("b1_a", [(s["negc"], 8), (s["v"], 4), ckv[4], cq[4], qk[4]], qk_raw, qk_raw[:, 4:8, :],
                            v_raw, y1, 0, 0.125, False)

            fu = FIRST["b1_up"]
            u = {k: sem(f"b1_up_{k}") for k in ("copied", "v", "rope_dve", "rope_act", "kr_hi", "ready",
                                                "pos")}

            def up_pe(pe):
                pe.wait_ge(*att[4])
                for j in range(4):
                    slot = ready(pe, fu, j)
                    if j < 3:
                        for n in range(4 if j < 2 else 8):
                            g = 4 * j + n
                            if g >= 4:
                                pe.wait_ge(u["copied"], g - 3)
                            if j < 2:
                                last = tile_chunk(slot, banks[g % 4][:], c_hi, c_lo, 2 * n, 2)
                            else:
                                w = slice(n * P, (n + 1) * P)
                                last = mm3(banks[g % 4][:], w_hi[:, slot, w], w_lo[:, slot, w], c_hi[:, 2, :],
                                           c_lo[:, 2, :])
                            last.then_inc(u["ready"] if n < (3 if j < 2 else 7) else used, 1)
                    else:
                        for tb in range(TB):
                            at = slice(tb * P, (tb + 1) * P)
                            last = mm3(banks[4 + tb][:], c_hi[:, 2, at], c_lo[:, 2, at], w_hi[:, slot, 0:S],
                                       w_lo[:, slot, 0:S])
                        last.then_inc(used, 1)

            def up_act(act):
                for j in range(2):
                    ahead(high_part, act, fu, j)
                act.wait_ge(u["rope_dve"], 8)
                nc.scalar.activation(rope_s[64:P, :], rope_a[64:P, :], ACT.Sin).then_inc(u["rope_act"], 1)
                act.wait_ge(u["rope_dve"], 10)
                nc.scalar.activation(rope_c[64:P, :], rope_k[64:P, :], ACT.Sin).then_inc(u["rope_act"], 1)
                ahead(high_part, act, fu, 2)
                act.wait_ge(u["rope_dve"], 14)
                nc.scalar.activation(ks_hi[64:P, :], y1[64:P, 7, :], ACT.Copy).then_inc(u["kr_hi"], 1)
                ahead(high_part, act, fu, 3)
                act.wait_ge(u["copied"], 8)
                for g in range(8, 16):
                    if g < 15:
                        act.wait_ge(u["ready"], g - 1)
                    else:
                        finished(act, fu, 2)
                    nc.scalar.activation(mk[:, g - 8, :], banks[g % 4][:], ACT.Copy).then_inc(u["copied"], 1)

            def up_dve(dve):
                dve.wait_ge(*att[4])
                r = slice(64, P)
                c = [0]

                def step(instruction):
                    instruction.then_inc(u["rope_dve"], 1)
                    c[0] += 1
                    dve.wait_ge(u["rope_dve"], c[0])

                dve.wait_ge(u["pos"], 16)
                step(nc.vector.tensor_copy(rope_a[r, :], rope_i[r, :]))
                step(nc.vector.tensor_scalar(rope_a[r, :], rope_a[r, :], col[r, COLS["freq"]:COLS["freq"] + 1], None,
                                             ALU.mult))
                step(nc.vector.tensor_scalar(rope_k[r, :], rope_a[r, :], 1.0 / TWO_PI[3], MAGIC, ALU.mult, ALU.add))
                step(nc.vector.tensor_scalar(rope_k[r, :], rope_k[r, :], MAGIC, None, ALU.subtract))
                for part in TWO_PI[:3]:
                    step(nc.vector.scalar_tensor_tensor(rope_a[r, :], rope_k[r, :], -part, rope_a[r, :], ALU.mult,
                                                        ALU.add))
                step(nc.vector.tensor_scalar(rope_a[r, :], rope_a[r, :], -PI_BELOW, PI_BELOW, ALU.max, ALU.min))
                step(nc.vector.scalar_tensor_tensor(rope_k[r, :], rope_a[r, :], -1.0, rope_a[r, :], ALU.mult, ALU.max))
                step(nc.vector.tensor_scalar(rope_k[r, :], rope_k[r, :], -1.0, HALF_PI, ALU.mult, ALU.add))
                for j in range(2):
                    ahead(low_part, dve, fu, j)
                    for n in range(4):
                        g = 4 * j + n
                        if n < 3:
                            dve.wait_ge(u["ready"], g + 1 - j)
                        else:
                            finished(dve, fu, j)
                        nc.vector.tensor_copy(mq[:, g, :], banks[g % 4][:]).then_inc(u["copied"], 1)
                    if j == 0:
                        dve.wait_ge(u["rope_act"], 2)
                        step(nc.vector.tensor_scalar(rope_s[r, :], rope_s[r, :], col[r, COLS["sgn"]:COLS["sgn"] + 1],
                                                     None, ALU.mult))
                        step(nc.vector.stream_shuffle(rope_t[r, :], y1[r, 7, :], SWAP16))
                        nc.vector.tensor_tensor(rope_t[r, :], rope_t[r, :], rope_s[r, :], ALU.mult)
                        step(nc.vector.tensor_tensor(y1[r, 7, :], y1[r, 7, :], rope_c[r, :], ALU.mult))
                        step(nc.vector.tensor_tensor(y1[r, 7, :], y1[r, 7, :], rope_t[r, :], ALU.add))
                        step(nc.vector.tensor_copy(rope_c[96:P, :], rope_s[96:P, :]))
                ahead(low_part, dve, fu, 2)
                dve.wait_ge(u["copied"], 8)
                for b in range(2):
                    q = mq[r, 4 * b:4 * b + 4, :]
                    table = rope_c[r, :].rearrange("p (o s) -> p o s", o=1).to_broadcast([64, 4, S])
                    step(nc.vector.tensor_tensor(q, q, table, ALU.mult))
                dve.wait_ge(u["kr_hi"], 1)
                step(nc.vector.tensor_tensor(ks_lo[r, :], y1[r, 7, :], ks_hi[r, :], ALU.subtract))
                ahead(low_part, dve, fu, 3)
                finished(dve, fu, 3)
                for tb in range(TB):
                    nc.vector.tensor_copy(mv[:, tb, :], banks[4 + tb][:]).then_inc(u["v"], 1)

            def up_pool(pool):
                pool.wait_ge(*att[4])
                pool.dma_start(rope_i[64:P, :], pos.partition_broadcast(64)).then_inc(u["pos"], 16)

            up = (up_act, up_pe, up_dve, up_pool)
            lat = attention("b1_b", [(u["rope_dve"], 18), (u["copied"], 16), (u["v"], 4)], mq, mk,
                            mv, y1, 4, 96.0 ** -0.5, True)
            return front, att, up, lat

        def merge(name, start, m_hi, m_lo, temps, branches, per, bias, raw_gates=None):
            def gate_tile(i, t, g):
                return raw_gates[g][:, i * turns + t, :] if raw_gates else temps[:, t % 2, g, :]

            gate_chunks = 0 if raw_gates else 2
            s = {k: sem(f"{name}_merge_{k}") for k in ("y_hi", "y_lo", "gate", "gated", "sum", "hi", "lo", "x")}
            fm, fo = FIRST[f"{name}_merge"], FIRST[f"{name}_out"]
            turns = 4 if per == 1 else 2
            N = per * turns
            ny = sum(b[3].shape[1] for b in branches)

            def pe_part(pe):
                for w in start:
                    pe.wait_ge(*w)
                with pe.Fori(0, KT // turns) as i:
                    for t in range(turns):
                        base = 4 * (t % 2)
                        pe.wait_ge(s["gated"], 2 * turns * i + 2 * (t + 1))
                        for g in range(gate_chunks):
                            slot = ready(pe, fm, per * t + g, i, N)
                            tile_chunk(slot, banks[base + g][:], xn_hi, xn_lo).then_inc(used, 1)
                        pe.wait_ge(s["y_lo"], ny)
                        for chunk, at, bank, raw, y_hi, y_lo in branches:
                            tiles = raw.shape[1]
                            slot = ready(pe, fm, per * t + chunk, i, N)
                            last = tile_chunk(slot, banks[base + bank][:], y_hi, y_lo, at, tiles)
                            if at + tiles == KT:
                                last.then_inc(used, 1)
                with pe.Fori(0, 2) as i:
                    for j in range(4):
                        slot = ready(pe, fo, j, i, 4)
                        if j == 0:
                            pe.wait_ge(s["lo"], KT + 2)
                            pe.wait_ge(s["gated"], 2 * KT + 4)
                        pe.wait_ge(s["x"], 4 * i + (j + 1))
                        tile_chunk(slot, banks[j][:], m_hi, m_lo).then_inc(used, 1)

            def act_part(act):
                for w in start:
                    act.wait_ge(*w)
                for _, _, _, raw, y_hi, _ in branches:
                    for k in range(raw.shape[1]):
                        nc.scalar.activation(y_hi[:, k, :], raw[:, k, :], ACT.Copy).then_inc(s["y_hi"], 1)
                if raw_gates:
                    with act.Fori(0, KT // 4) as i:
                        for t in range(4):
                            for g in range(2):
                                nc.scalar.activation(gate_tile(i, t, g), gate_tile(i, t, g), ACT.Sigmoid,
                                                     bias=col[:, bass.ds(i * 4 + (bias + g * KT + t), 1)]
                                                     ).then_inc(s["gate"], 1)
                with act.Fori(0, KT // turns) as i:
                    for t in range(turns):
                        for g in range(gate_chunks):
                            ahead(high_part, act, fm, per * t + g, i, N)
                            finished(act, fm, per * t + g, i, N)
                            act.wait_ge(s["lo"], turns * i + (t + 1))
                            nc.scalar.activation(gate_tile(i, t, g), banks[4 * (t % 2) + g][:],
                                                 ACT.Sigmoid).then_inc(s["gate"], 1)
                        for c in range(gate_chunks, per):
                            ahead(high_part, act, fm, per * t + c, i, N)
                        act.wait_ge(s["sum"], turns * i + (t + 1))
                        nc.scalar.activation(m_hi[:, i * turns + t, :], gate_tile(i, t, 0),
                                             ACT.Copy).then_inc(s["hi"], 1)
                with act.Fori(0, 2) as i:
                    for j in range(4):
                        ahead(high_part, act, fo, j, i, 4)

            def dve_part(dve):
                for w in start:
                    dve.wait_ge(*w)
                dve.sem_inc(s["gated"], 4)
                tile = 0
                for _, _, _, raw, y_hi, y_lo in branches:
                    for k in range(raw.shape[1]):
                        tile += 1
                        dve.wait_ge(s["y_hi"], tile)
                        nc.vector.tensor_tensor(y_lo[:, k, :], raw[:, k, :], y_hi[:, k, :],
                                                ALU.subtract).then_inc(s["y_lo"], 1)
                with dve.Fori(0, KT // turns) as i:
                    for t in range(turns):
                        for c in range(per):
                            ahead(low_part, dve, fm, per * t + c, i, N)
                        dve.wait_ge(s["gate"], 2 * turns * i + 2 * (t + 1))
                        finished(dve, fm, per * t + per - 1, i, N)
                        for g in range(2):
                            nc.vector.tensor_tensor(gate_tile(i, t, g), gate_tile(i, t, g),
                                                    banks[4 * (t % 2) + 2 + g][:], ALU.mult).then_inc(s["gated"], 1)
                dve.sem_inc(s["x"], 4)
                with dve.Fori(0, 2) as i:
                    for j in range(4):
                        ahead(low_part, dve, fo, j, i, 4)
                        finished(dve, fo, j, i, 4)
                        nc.vector.tensor_tensor(x[:, 4 * i + j, :], x[:, 4 * i + j, :], banks[j][:],
                                                ALU.add).then_inc(s["x"], 1)

            def pool_part(pool):
                pool.sem_inc(s["lo"], 2)
                with pool.Fori(0, KT // turns) as i:
                    for t in range(turns):
                        pool.wait_ge(s["gated"], 2 * turns * i + 2 * (t + 1) + 4)
                        nc.gpsimd.tensor_tensor(gate_tile(i, t, 0), gate_tile(i, t, 0), gate_tile(i, t, 1),
                                                ALU.add).then_inc(s["sum"], 1)
                        pool.wait_ge(s["hi"], turns * i + (t + 1))
                        nc.gpsimd.tensor_tensor(m_lo[:, i * turns + t, :], gate_tile(i, t, 0),
                                                m_hi[:, i * turns + t, :], ALU.subtract).then_inc(s["lo"], 1)

            return act_part, pe_part, dve_part, pool_part, (s["x"], 5)

        y1_hi = sb("y1_hi", [P, KT, S], F32R, W0)
        y1_lo = sb("y1_lo", [P, KT, S], F32R, A0 + 52 * K)
        m1_hi = sb("m1_hi", [P, KT, S], F32R, A0 + 32 * K)
        m1_lo = sb("m1_lo", [P, KT, S], F32R, A0 + 16 * K)

        nsa_c = sb("nsa_c", [P, S], F32, A0)
        nsa_s = sb("nsa_s", [P, S], F32, A0 + 2 * K)
        ret_c = sb("ret_c", [P, S], F32, A0 + 4 * K)
        ret_s = sb("ret_s", [P, S], F32, A0 + 6 * K)
        cmp_c = sb("cmp_c", [P, 64], F32, A0 + 8 * K)
        cmp_s = sb("cmp_s", [P, 64], F32, A0 + 8 * K + 256)
        cmp_add = sb("cmp_add", [P, TB, 32], F32, A0 + 8 * K + 512)
        cmp_keep = sb("cmp_keep", [P, TB, 32], F32, A0 + 9 * K)
        gates = sb("gates", [P, TB, 48], F32, A0 + 10 * K)
        kc_hi = sb("kc_hi", [P, 32], F32R, A0 + 11 * K)
        kc_lo = sb("kc_lo", [P, 32], F32R, A0 + 11 * K + 256)
        vc_raw = sb("vc_raw", [P, 2, P], F32, A0 + 12 * K)
        vcs_hi = sb("vcs_hi", [P, P], F32R, A0 + 13 * K)
        vcs_lo = sb("vcs_lo", [P, P], F32R, A0 + 13 * K + 512)
        kc_raw = sb("kc_raw", [P, 64], F32, A0 + 14 * K)
        kc_sw = sb("kc_sw", [P, 64], F32, A0 + 14 * K + 256)
        hidden_k = sb("hidden_k", [P, 2, 64], F32, A0 + 15 * K)
        hidden_v = sb("hidden_v", [P, 2, 2, P], F32, A0 + 16 * K)
        a_raw = sb("a_raw", [P, KT, S], F32, A0 + 16 * K)
        nqk = sb("nqk", [P, 12, S], F32, A0 + 32 * K)
        nv = sb("nv", [P, TB, 256], F32, A0 + 56 * K)
        swapped = sb("swapped", [P, 2, S], F32, A0 + 92 * K)
        ck = sb("ck", [P, 4, S], F32, A0 + 60 * K)
        blk = sb("blk", [P, 2, 16, 64], F32, A0 + 68 * K)
        blk_hi = sb("blk_hi", [P, 2, 16, 64], F32R, A0 + 76 * K)
        blk_lo = sb("blk_lo", [P, 2, 16, 64], F32R, A0 + 84 * K)
        gate_fm = sb("gate_fm", [P, S], F32, A0 + 96 * K)
        nq_hi = sb("nq_hi", [P, 2, S], F32R, A0 + 60 * K)
        nq_lo = sb("nq_lo", [P, 2, S], F32R, A0)
        nk_hi = sb("nk_hi", [P, 2, S], F32R, A0 + 64 * K)
        nk_lo = sb("nk_lo", [P, 2, S], F32R, A0 + 68 * K)
        nvs_hi = sb("nvs_hi", [P, TB, 2, P], F32R, A0 + 72 * K)
        nvs_lo = sb("nvs_lo", [P, TB, 2, P], F32R, A0 + 76 * K)
        nprob = sb("nprob", [P, 2, OFF[TB]], F32, A0 + 80 * K)
        npt_hi = sb("npt_hi", [P, OFF[TB]], F32R, A0 + 90 * K)
        npt_lo = sb("npt_lo", [P, OFF[TB]], F32R, A0 + 95 * K)
        csc = sb("csc", [P, 2, TB, 32], F32, A0 + 100 * K)
        cpad = sb("cpad", [P, 2, TB * (P + 32)], F32, A0 + 101 * K)
        cpt_hi = sb("cpt_hi", [P, S], F32R, 90 * K)
        cpt_lo = sb("cpt_lo", [P, S], F32R, 94 * K)
        c_top, c_total, c_inverse, nguard = (small[:, 32 + 8 * n:40 + 8 * n] for n in range(4))
        r_qk = sb("r_qk", [P, KT, S], F32, A0 + 32 * K)
        r_v = sb("r_v", [P, TB, D], F32, A0 + 48 * K)
        r_raw = sb("r_raw", [P, KT, S], F32, A0 + 64 * K)
        r_swap = sb("r_swap", [P, S], F32, 99 * K)
        rq_hi = sb("rq_hi", [P, S], F32R, A0 + 80 * K)
        rq_lo = sb("rq_lo", [P, S], F32R, A0 + 82 * K)
        rk_hi = sb("rk_hi", [P, S], F32R, A0 + 84 * K)
        rk_lo = sb("rk_lo", [P, S], F32R, A0 + 86 * K)
        rv_hi = sb("rv_hi", [P, TB, 2 * P], F32R, A0 + 88 * K)
        rv_lo = sb("rv_lo", [P, TB, 2 * P], F32R, A0 + 92 * K)
        decay = sb("decay", [P, 2, S], F32, A0 + 96 * K)
        weighted = sb("weighted", [P, OFF[TB]], F32, A0 + 100 * K)
        ws_hi = sb("ws_hi", [P, OFF[TB]], F32R, A0)
        ws_lo = sb("ws_lo", [P, OFF[TB]], F32R, A0 + 5 * K)
        gn_sq = sb("gn_sq", [P, S], F32, A0 + 12 * K)
        gn_r = sb("gn_r", [P, S], F32, A0 + 10 * K)
        a_hi = sb("a_hi", [P, KT, S], F32R, A0 + 32 * K)
        a_lo = sb("a_lo", [P, KT, S], F32R, A0 + 16 * K)
        r_hi = sb("r_hi", [P, KT, S], F32R, A0 + 48 * K)
        r_lo = sb("r_lo", [P, KT, S], F32R, A0 + 64 * K)
        m2_hi = sb("m2_hi", [P, KT, S], F32R, A0 + 80 * K)
        m2_lo = sb("m2_lo", [P, KT, S], F32R, A0)
        m2_temps = sb("m2_temps", [P, 2, 2, S], F32, A0 + 96 * K)

        def mixer2(n_mix2, x_done):
            norm_done = n_mix2[4]
            t = {k: sem(f"b2_{k}") for k in ("tables", "v", "gate", "gate_t", "gates", "blk", "hi", "lo", "hid",
                                             "gelu", "kv", "kc", "pad")}

            def tables_in(pool):
                pool.wait_ge(*x_done)
                at = 0
                for tile in (nsa_c, nsa_s, ret_c, ret_s, cmp_c, cmp_s, cmp_add, cmp_keep):
                    n = int(np.prod(tile.shape[1:]))
                    to = tile[:].rearrange("p a b -> p (a b)") if len(tile.shape) == 3 else tile[:]
                    pool.dma_start(to, rows[:, at:at + n]).then_inc(t["tables"], 16)
                    at += n

            parts.append((skip, skip, skip, tables_in))
            parts.append(n_mix2)
            cmp = copies_out("b2_cmp", FIRST["b2_cmp"], 4, ck, (norm_done, ORDER))
            fv, fg, fm, fk = (FIRST[f"b2_{n}"] for n in ("v", "g", "w1_q", "k"))
            q = {k: sem(f"b2_q_{k}") for k in ("swapped", "sines", "out", "done")}

            def place_of(n):
                return (fm, 2 * n + 1) if n < 8 else (fk, n - 8)

            def pe_part(pe):
                for j in range(2):
                    slot = ready(pe, fv, j)
                    for n in range(4):
                        k, w = 4 * j + n, slice(n * 256, (n + 1) * 256)
                        for tb in range(TB):
                            at = slice(tb * P, (tb + 1) * P)
                            last = mm3(banks[4 + tb][:, 0:256], xn_hi[:, k, at], xn_lo[:, k, at], w_hi[:, slot, w],
                                       w_lo[:, slot, w], k == 0, k == KT - 1)
                    last.then_inc(used, 1)
                slot = ready(pe, fg, 0)
                pe.wait_ge(*cmp[4])
                tile_chunk(slot, banks[0][:], xn_hi, xn_lo).then_inc(used, 1)
                pe.wait_ge(t["gate"], 1)
                pe.wait_ge(t["v"], 4)
                for c in range(8):
                    kv, half, part = c // 4, c % 4 // 2, c % 2
                    slot_1, slot_q = ready(pe, fm, 2 * c), ready(pe, fm, 2 * c + 1)
                    if c % 4 == 0:
                        pe.wait_ge(t["lo"], kv + 1)
                    pe.wait_ge(q["out"], c + 1)
                    for n in range(8):
                        k, w = 8 * part + n, slice(n * P, (n + 1) * P)
                        hidden_in = [banks[4 + c // 2][:, 0:64], blk_hi[:, kv, k, :], blk_lo[:, kv, k, :]]
                        q_in = [banks[c % 4][:], xn_hi[:, n, :], xn_lo[:, n, :]]
                        for m, (a, b) in enumerate(((w_hi, 1), (w_hi, 2), (w_lo, 1))):
                            last_1 = nc.tensor.matmul(hidden_in[0], a[:, slot_1, w], hidden_in[b], start=k + m == 0,
                                                      stop=k == 15 and m == 2, skip_group_check=True)
                            last_q = nc.tensor.matmul(q_in[0], a[:, slot_q, w], q_in[b], start=n + m == 0,
                                                      stop=n == 7 and m == 2, skip_group_check=True)
                            if n == 7 and m == 2:
                                last_1.then_inc(used, 1)
                                last_q.then_inc(used, 1)
                for n in range(8, 12):
                    slot = ready(pe, *place_of(n))
                    pe.wait_ge(q["out"], n + 1)
                    tile_chunk(slot, banks[n % 4][:], xn_hi, xn_lo).then_inc(used, 1)
                pe.wait_ge(q["out"], 12 + 4)
                for tb in range(TB):
                    last = nc.tensor.transpose(banks[2][:, 48 * tb:48 * tb + 48], gate_fm[0:48, tb * P:(tb + 1) * P],
                                               ident[0:48, 0:48])
                last.then_inc(t["gate_t"], 1)
                pe.wait_ge(t["gelu"], 4)
                for half in range(2):
                    last = nc.tensor.matmul(banks[0][:, 0:64], w2_sb[:, half, :], hidden_k[:, half, :],
                                            start=half == 0, stop=half == 1)
                last.then_inc(t["kv"], 1)
                for g in range(2):
                    for half in range(2):
                        last = nc.tensor.matmul(banks[1][:, g * P:(g + 1) * P], hidden_v[:, half, g, :],
                                                w2_sb[:, 2 + half, :], start=half == 0, stop=half == 1,
                                                skip_group_check=True)
                    last.then_inc(t["kv"], 1)

            def act_part(act):
                for j in range(2):
                    ahead(high_part, act, fv, j)
                    act.wait_ge(t["blk"], 8 * (j + 1))
                    nc.scalar.activation(blk_hi[:, j], blk[:, j], ACT.Copy).then_inc(t["hi"], 1)
                ahead(high_part, act, fg, 0)
                finished(act, fg, 0)
                nc.scalar.activation(gate_fm[0:48, :], banks[0][0:48, :], ACT.Sigmoid).then_inc(t["gate"], 1)
                for c in range(8):
                    ahead(high_part, act, fm, 2 * c)
                    ahead(high_part, act, fm, 2 * c + 1)
                    if c % 2:
                        finished(act, fm, 2 * c)
                        half = c % 4 // 2
                        pre = banks[4 + c // 2][:, 0:64]
                        if c < 4:
                            nc.scalar.activation(hidden_k[:, half, :], pre, ACT.Gelu_apprx_tanh).then_inc(t["gelu"], 1)
                        else:
                            nc.scalar.activation(
                                hidden_v[:, half].rearrange("p g (f n) -> p g f n", f=4),
                                pre.rearrange("p (g o n) -> p g o n", g=2, o=1).to_broadcast([P, 2, 4, 32]),
                                ACT.Gelu_apprx_tanh).then_inc(t["gelu"], 1)
                for j in range(4):
                    ahead(high_part, act, fk, j)

            def dve_part(dve):
                dve.sem_inc(q["out"], 4)
                dve.wait_ge(*cmp[4])
                dve.wait_ge(consts_made, 3)
                for kv in range(2):
                    ahead(low_part, dve, fv, kv)
                    for g in range(2):
                        for half in range(2):
                            r = slice(64 * half, 64 * half + 64)
                            view = ck[r, 2 * kv + g, :].rearrange("p (n k two) -> p two k n", k=8, two=2)[:, half]
                            for a in range(2):
                                at = COLS["pos"] + 8 * a
                                emb = col[r, at:at + 8].rearrange("p (k o) -> p k o", o=1).to_broadcast([64, 8, 31])
                                nc.vector.tensor_tensor(blk[r, kv, 8 * a:8 * a + 8, 32 * g:32 * g + 31],
                                                        view[:, :, a:a + 31], emb, ALU.add).then_inc(t["blk"], 1)
                finished(dve, fv, 1)
                for tb in range(TB):
                    nc.vector.tensor_copy(nv[:, tb, :], banks[4 + tb][:, 0:256]).then_inc(t["v"], 1)
                ahead(low_part, dve, fg, 0)
                dve.wait_ge(t["tables"], 128)
                for n in range(12):
                    for c in ((2 * n, 2 * n + 1) if n < 8 else (n - 8,)):
                        ahead(low_part, dve, fm if n < 8 else fk, c)
                    finished(dve, *place_of(n))
                    dve.wait_ge(q["done"], n + 1)
                    nc.vector.stream_shuffle(swapped[:, n % 2, :], banks[n % 4][:], SWAP8).then_inc(q["swapped"], 1)
                    nc.vector.tensor_tensor(nqk[:, n, :], banks[n % 4][:], nsa_c[:], ALU.mult).then_inc(q["out"], 1)
                dve.wait_ge(t["gate_t"], 1)
                nc.vector.tensor_copy(gates[:], banks[2][:, 0:192].rearrange("p (t h) -> p t h", t=TB)
                                      ).then_inc(t["gates"], 1)
                dve.wait_ge(t["kv"], 1)
                nc.vector.stream_shuffle(kc_sw[:], banks[0][:, 0:64], SWAP8).then_inc(t["kc"], 1)
                nc.vector.tensor_tensor(kc_raw[:], banks[0][:, 0:64], cmp_c[:], ALU.mult).then_inc(t["kc"], 1)
                dve.wait_ge(t["kc"], 1)
                nc.vector.tensor_tensor(kc_sw[:], kc_sw[:], cmp_s[:], ALU.mult).then_inc(t["kc"], 1)
                dve.wait_ge(t["kc"], 3)
                nc.vector.tensor_tensor(kc_raw[:], kc_raw[:], kc_sw[:], ALU.add).then_inc(t["kc"], 1)
                dve.wait_ge(t["kv"], 3)
                nc.vector.tensor_copy(vc_raw[:], banks[1][:, 0:256].rearrange("p (g d) -> p g d", g=2)
                                      ).then_inc(t["kc"], 1)

            def pool_part(pool):
                pool.wait_ge(*norm_done)
                nc.gpsimd.memset(blk[:], 0.0).then_inc(consts_made, 1)
                pool.sem_inc(q["done"], 2)
                for kv in range(2):
                    pool.wait_ge(t["hi"], kv + 1)
                    nc.gpsimd.tensor_tensor(blk_lo[:, kv], blk[:, kv], blk_hi[:, kv], ALU.subtract).then_inc(t["lo"], 1)
                for n in range(12):
                    pool.wait_ge(q["swapped"], n + 1)
                    nc.gpsimd.tensor_tensor(swapped[:, n % 2, :], swapped[:, n % 2, :], nsa_s[:],
                                            ALU.mult).then_inc(q["sines"], 1)
                    pool.wait_ge(q["out"], n + 5)
                    pool.wait_ge(q["sines"], n + 1)
                    nc.gpsimd.tensor_tensor(nqk[:, n, :], nqk[:, n, :], swapped[:, n % 2, :],
                                            ALU.add).then_inc(q["done"], 1)
                pool.wait_ge(t["kc"], 5)
                nc.gpsimd.memset(cpad[:], 0.0).then_inc(t["pad"], 1)

            prepare = (act_part, pe_part, dve_part, pool_part)
            nsa_out = sparse_attention([(t["kc"], 5), (t["pad"], 1), (t["v"], 4), (t["gates"], 1), (q["done"], 14)])
            ret = retention([nsa_out[4], nsa_out[5]])
            return [cmp, prepare, nsa_out, *ret]

        def sparse_attention(start):
            s = {k: sem(f"nsa_{k}") for k in ("k_hi", "k_lo", "q_hi", "q_lo", "scored", "biased", "negated", "exp",
                                              "guard", "inverse", "scaled", "turned", "hi", "lo", "summed",
                                              "out", "c_scored", "c_dve", "c_exp", "c_turned", "c_hi", "c_lo", "r_swapped", "zero",
                                              "r_sines", "r_out", "r_done")}
            frqk = FIRST["b2_rqk"]
            units = [(0, 0), (0, 1), (1, 0), (1, 1)]

            def v_twice(g, m):
                return nv[:, :, bass.ds(g * 64 + 128 * m, 64)].rearrange("p t (o d) -> p t o d", o=1).to_broadcast(
                    [P, TB, 2, 64])

            def twice(tile, m):
                return tile[:, :, m, :].rearrange("p t (o d) -> p t o d", o=2)

            def begin(eng):
                for w in start:
                    eng.wait_ge(*w)

            def group_turns(g, body):
                for p in range(4):
                    body(4 * g + p, p < 3, p)

            def pe_part(pe):
                begin(pe)
                pe.sem_inc(s["scored"], 4)
                pe.sem_inc(s["turned"], 8)
                pe.sem_inc(s["summed"], 9)
                pe.sem_inc(s["c_turned"], 1)
                pe.wait_ge(s["zero"], 4)
                with pe.Fori(0, 2) as g:
                    pe.wait_ge(s["k_lo"], 6 * g + 6)
                    apart(pe)
                    def score(i, u):
                        j, m = units[u % 4]
                        for n, qb in enumerate(SCORE_ORDER):
                            pe.wait_ge(s["biased"], 16 * i + (4 * u + max(n, 1) + 1))
                            at = slice(qb * P, (qb + 1) * P)
                            mm3(score_bank(qb), nq_hi[:, j, at], nq_lo[:, j, at], nk_hi[:, m, 0:(qb + 1) * P],
                                nk_lo[:, m, 0:(qb + 1) * P]).then_inc(s["scored"], 1)

                    def turn(i, u, kb):
                        pe.wait_ge(s["lo"], 16 * i + (4 * u + kb + 1))
                        for qb in range(kb, TB):
                            if kb == 0:
                                pe.wait_ge(s["scaled"], 16 * i + (4 * u + qb + 1))
                            last = nc.tensor.transpose(banks[4 + kb % 2][:, (qb - kb) * P:(qb - kb + 1) * P],
                                                       nprob[:, u % 2, OFF[qb] + kb * P:OFF[qb] + (kb + 1) * P],
                                                       ident[:])
                        last.then_inc(s["turned"], 1)

                    def values(i, u, kb):
                        j, m = units[u]
                        pe.wait_ge(s["lo"], 16 * i + (4 * u + kb + 3))
                        at = slice(KOFF[kb], KOFF[kb + 1])
                        mm3(banks[6][:, kb * P:S], nvs_hi[:, kb, m, :], nvs_lo[:, kb, m, :], npt_hi[:, at], npt_lo[:, at], False,
                            m == 1 and kb == TB - 1).then_inc(s["summed"], 1)

                    def compressed_scores(i, n):
                        pe.wait_ge(s["q_lo"], 2 * i + (2 * n + 2))
                        pe.wait_ge(s["c_lo"], 2 * i + (2 * n + 1))
                        for j in range(2):
                            for qb in range(TB):
                                at = slice(qb * P, (qb + 1) * P)
                                last = mm3(banks[7][:, (TB * j + qb) * 32:(TB * j + qb + 1) * 32], nq_hi[:, j, at],
                                           nq_lo[:, j, at], kc_hi[:], kc_lo[:])
                            last.then_inc(s["c_scored"], 1)

                    def compressed_turn(i, j):
                        if j == 0:
                            pe.wait_ge(s["c_dve"], 10 * i + 10)
                        pe.wait_ge(s["c_lo"], 2 * i + (j + 1))
                        for qb in range(TB):
                            last = nc.tensor.transpose(banks[7][:, qb * P:(qb + 1) * P],
                                                       cpad[:, j, qb * P:(qb + 1) * P], ident[:])
                        last.then_inc(s["c_turned"], 1)

                    def compressed_values(i, j):
                        pe.wait_ge(s["c_lo"], 2 * i + (j + 2))
                        pe.wait_ge(s["out"], 2 * i + (j + 1))
                        mm3(banks[6][:], vcs_hi[:], vcs_lo[:], cpt_hi[:], cpt_lo[:], True,
                            False).then_inc(s["summed"], 1)

                    def body(i, more, p):
                        for u in range(4):
                            if u < 2:
                                compressed_turn(i, u)
                            turn(i, u, 0)
                            turn(i, u, 1)
                            if u == 0:
                                slot = ready(pe, frqk, p, g, 4)
                                pe.wait_ge(s["r_out"], i + 1)
                            for k in (2 * u, 2 * u + 1):
                                w = slice(k * P, (k + 1) * P)
                                last = mm3(banks[3][:], w_hi[:, slot, w], w_lo[:, slot, w], xn_hi[:, k, :],
                                           xn_lo[:, k, :], k == 0, k == KT - 1)
                            if u == 3:
                                last.then_inc(used, 1)
                            turn(i, u, 2)
                            turn(i, u, 3)
                            if u == 2 and more:
                                compressed_scores(i, 1)
                            if u < 2 or more:
                                score(i, u + 2)
                            if u % 2 == 0:
                                compressed_values(i, u // 2)
                            for kb in range(TB):
                                values(i, u, kb)

                    compressed_scores(4 * g, 0)
                    score(4 * g, 0)
                    score(4 * g, 1)
                    group_turns(g, body)

            def act_part(act):
                begin(act)
                act.sem_inc(s["out"], 1)
                with act.Fori(0, 2) as g:
                    act.wait_ge(s["summed"], 72 * g + 9)
                    for m in range(2):
                        nc.scalar.activation(nk_hi[:, m, :], nqk[:, g + (8 + 2 * m), :], ACT.Copy).then_inc(s["k_hi"], 1)
                        nc.scalar.activation(twice(nvs_hi, m), v_twice(g, m),
                                             ACT.Copy).then_inc(s["k_hi"], 1)
                    nc.scalar.activation(vcs_hi[:], vc_raw[:, g, :], ACT.Copy).then_inc(s["k_hi"], 1)
                    nc.scalar.activation(kc_hi[:], kc_raw[:, bass.ds(g * 32, 32)], ACT.Copy).then_inc(s["k_hi"], 1)
                    def stage(i, n):
                        act.wait_ge(s["scored"], 16 * i + (16 * n + 4))
                        for j in range(2):
                            r = slice(64 * j, 64 * j + 64)
                            nc.scalar.activation(nq_hi[r, j, :], nqk[r, i + n, :], ACT.Copy).then_inc(s["q_hi"], 1)

                    def compressed_exps(i, n):
                        act.wait_ge(s["c_dve"], 10 * i + (10 * n + 3))
                        nc.scalar.activation(csc[:], csc[:], ACT.Exp, scale=0.125).then_inc(s["c_exp"], 1)

                    def exps(i, u, blocks):
                        act.wait_ge(s["negated"], 4 * i + (u + 1))
                        for qb in blocks:
                            at = nprob[:, u % 2, scores_rows(qb)]
                            n = 4 * (u % 2) + qb
                            nc.scalar.activation(at, at, ACT.Exp, bias=neg_top[:, n:n + 1], scale=0.125,
                                                 accum_out=total[:, n:n + 1]).then_inc(s["exp"], 1)

                    def highs(i, u, blocks):
                        for kb in blocks:
                            act.wait_ge(s["turned"], 16 * i + (4 * u + kb + 9))
                            act.wait_ge(s["summed"], 18 * i + ((6, 11, 15, 20)[u] + kb))
                            nc.scalar.activation(npt_hi[:, KOFF[kb]:KOFF[kb + 1]],
                                                 banks[4 + kb % 2][:, 0:S - kb * P], ACT.Copy).then_inc(s["hi"], 1)

                    def compressed_high(i, j):
                        act.wait_ge(s["c_turned"], 2 * i + (j + 2))
                        act.wait_ge(s["summed"], 18 * i + 9 * j + 1)
                        nc.scalar.activation(cpt_hi[:], banks[7][:], ACT.Copy).then_inc(s["c_hi"], 1)

                    def output(i, j):
                        act.wait_ge(s["summed"], 18 * i + (9 * j + 18))
                        r = slice(64 * j, 64 * j + 64)
                        nc.scalar.activation(a_raw[r, i, :], banks[6][r, :], ACT.Copy).then_inc(s["out"], 1)

                    def body(i, more, p):
                        for u in range(4):
                            if u < 2:
                                compressed_high(i, u)
                            highs(i, u, (0, 1))
                            if u == 2:
                                output(i, 0)
                            if u < 3 or more:
                                exps(i, u + 1, (0, 1, 2))
                            highs(i, u, (2, 3))
                            if u < 3 or more:
                                exps(i, u + 1, (3,))
                            if u == 0:
                                ahead(high_part, act, frqk, p, g, 4)
                            if u == 1 and more:
                                stage(i, 1)
                        if more:
                            compressed_exps(i, 1)
                        output(i, 1)

                    stage(4 * g, 0)
                    compressed_exps(4 * g, 0)
                    exps(4 * g, 0, range(TB))
                    group_turns(g, body)

            def dve_part(dve):
                begin(dve)
                dve.sem_inc(s["biased"], 4)
                dve.sem_inc(s["lo"], 2)
                dve.sem_inc(s["c_lo"], 1)
                dve.sem_inc(s["r_out"], 1)
                for part in (nq_hi, nq_lo):
                    for j in range(2):
                        r = slice(64 - 64 * j, P - 64 * j)
                        nc.vector.memset(part[r, j, :].bitcast(F32), 0.0).then_inc(s["zero"], 1)
                with dve.Fori(0, 2) as g:
                    def biased(i, u):
                        for place_of, qb in enumerate(SCORE_ORDER):
                            dve.wait_ge(s["scored"], 16 * i + (4 * u + max(place_of, 1) + 5))
                            if place_of == 0:
                                dve.wait_ge(s["turned"], 16 * i + (4 * u + 4))
                            apart(dve)
                            n = 4 * (u % 2) + qb
                            width = (qb + 1) * P
                            nc.vector.tensor_tensor_reduce(nprob[:, u % 2, scores_rows(qb)], score_bank(qb),
                                                           bias_tri[:, S - width:S], 1.0, -3.0e38, ALU.add, ALU.max,
                                                           top_s[:, n:n + 1]).then_inc(s["biased"], 1)
                        dve.wait_ge(s["biased"], 16 * i + (4 * u + 8))
                        n = 4 * (u % 2)
                        nc.vector.tensor_scalar(neg_top[:, n:n + 4], top_s[:, n:n + 4], -0.125, None,
                                                ALU.mult).then_inc(s["negated"], 1)

                    def scaled(i, u):
                        j, m = units[u]
                        n = slice(4 * (u % 2), 4 * (u % 2) + 4)
                        dve.wait_ge(s["exp"], 16 * i + (4 * u + 4))
                        nc.vector.tensor_scalar(nguard[:, n], total[:, n], 1e-20, None,
                                                ALU.max).then_inc(s["guard"], 1)
                        dve.wait_ge(s["guard"], 8 * i + (2 * u + 1))
                        nc.vector.reciprocal(nguard[:, n], nguard[:, n]).then_inc(s["guard"], 1)
                        dve.wait_ge(s["guard"], 8 * i + (2 * u + 2))
                        nc.vector.tensor_tensor(inverse[:, n], nguard[:, n],
                                                gates[:, :, i * 6 + (3 * j + 1 + m)],
                                                ALU.mult).then_inc(s["inverse"], 1)
                        dve.wait_ge(s["inverse"], 4 * i + (u + 1))
                        for qb in range(TB):
                            at = nprob[:, u % 2, scores_rows(qb)]
                            n = 4 * (u % 2) + qb
                            nc.vector.tensor_scalar(at, at, inverse[:, n:n + 1], None, ALU.mult).then_inc(s["scaled"], 1)

                    def lows(i, u):
                        for kb in range(TB):
                            dve.wait_ge(s["hi"], 16 * i + (4 * u + kb + 1))
                            at = slice(KOFF[kb], KOFF[kb + 1])
                            nc.vector.tensor_tensor(npt_lo[:, at], banks[4 + kb % 2][:, 0:S - kb * P], npt_hi[:, at],
                                                    ALU.subtract).then_inc(s["lo"], 1)

                    def compressed_low(i, j):
                        dve.wait_ge(s["c_hi"], 2 * i + (j + 1))
                        nc.vector.tensor_tensor(cpt_lo[:], banks[7][:], cpt_hi[:],
                                                ALU.subtract).then_inc(s["c_lo"], 1)

                    add = cmp_add[:].rearrange("p (o t) n -> p o t n", o=1).to_broadcast([P, 2, TB, 32])
                    keep = cmp_keep[:].rearrange("p (o t) n -> p o t n", o=1).to_broadcast([P, 2, TB, 32])
                    over = [t.rearrange("p (h t o) -> p h t o", h=2, o=1).to_broadcast([P, 2, TB, 32])
                            for t in (c_top, c_inverse)]

                    def step(i, n, instruction, count, wait=True):
                        instruction.then_inc(s["c_dve"], 1)
                        if wait:
                            dve.wait_ge(s["c_dve"], 10 * i + (10 * n + count))

                    def compressed_shift(i, n):
                        dve.wait_ge(s["c_scored"], 2 * i + (2 * n + 2))
                        step(i, n, nc.vector.tensor_tensor(
                            csc[:], banks[7][:, 0:256].rearrange("p (h t n) -> p h t n", h=2, t=TB), add, ALU.add), 1)
                        step(i, n, nc.vector.tensor_reduce(c_top.rearrange("p (h t) -> p h t", h=2), csc[:], AX.X,
                                                           ALU.max), 2)
                        step(i, n, nc.vector.tensor_tensor(csc[:], csc[:], over[0], ALU.subtract), 3, False)

                    def compressed_scale(i, n):
                        dve.wait_ge(s["c_exp"], i + (n + 1))
                        step(i, n, nc.vector.tensor_tensor(csc[:], csc[:], keep, ALU.mult), 4)
                        step(i, n, nc.vector.tensor_reduce(c_total.rearrange("p (h t) -> p h t", h=2), csc[:], AX.X,
                                                           ALU.add), 5)
                        step(i, n, nc.vector.tensor_scalar(c_total, c_total, 1e-20, None, ALU.max), 6)
                        step(i, n, nc.vector.reciprocal(c_total, c_total), 7)
                        step(i, n, nc.vector.tensor_tensor(
                            c_inverse.rearrange("p (h t) -> p h t", h=2), c_total.rearrange("p (h t) -> p h t", h=2),
                            gates[:, :, bass.ds(i * 6 + 6 * n, 6)].rearrange("p t (h c) -> p h t c", c=3)[:, :, :, 0],
                            ALU.mult), 8)
                        for j in range(2):
                            diagonal = cpad[:, j, :].rearrange("p (t w) -> p t w", w=P + 32)[:, :, 0:32]
                            step(i, n, nc.vector.tensor_tensor(diagonal, csc[:, j, :, :], over[1][:, j, :, :],
                                                               ALU.mult), 9 + j, False)

                    def body(i, more, p):
                        for u in range(4):
                            scaled(i, u)
                            if u == 3 and more:
                                compressed_shift(i, 1)
                            if u < 3 or more:
                                biased(i, u + 1)
                            if u < 2:
                                compressed_low(i, u)
                            lows(i, u)
                            if u == 1:
                                ahead(low_part, dve, frqk, p, g, 4)
                        rotate(i, p)
                        if more:
                            compressed_scale(i, 1)

                    def rotate(i, p):
                        finished(dve, frqk, p, g, 4)
                        dve.wait_ge(s["r_done"], i + 1)
                        apart(dve)
                        nc.vector.stream_shuffle(r_swap[:], banks[3][:], SWAP16).then_inc(s["r_swapped"], 1)
                        nc.vector.tensor_tensor(r_qk[:, i, :], banks[3][:], ret_c[:], ALU.mult).then_inc(s["r_out"], 1)

                    compressed_shift(4 * g, 0)
                    biased(4 * g, 0)
                    compressed_scale(4 * g, 0)
                    group_turns(g, body)

            def pool_part(pool):
                begin(pool)
                pool.sem_inc(s["r_done"], 1)
                with pool.Fori(0, 2) as g:
                    for m in range(2):
                        pool.wait_ge(s["k_hi"], 6 * g + (2 * m + 1))
                        nc.gpsimd.tensor_tensor(nk_lo[:, m, :], nqk[:, g + (8 + 2 * m), :], nk_hi[:, m, :],
                                                ALU.subtract).then_inc(s["k_lo"], 1)
                        pool.wait_ge(s["k_hi"], 6 * g + (2 * m + 2))
                        nc.gpsimd.tensor_tensor(twice(nvs_lo, m), v_twice(g, m), twice(nvs_hi, m), ALU.subtract).then_inc(s["k_lo"], 1)
                    pool.wait_ge(s["k_hi"], 6 * g + 5)
                    nc.gpsimd.tensor_tensor(vcs_lo[:], vc_raw[:, g, :], vcs_hi[:], ALU.subtract).then_inc(s["k_lo"], 1)
                    pool.wait_ge(s["k_hi"], 6 * g + 6)
                    nc.gpsimd.tensor_tensor(kc_lo[:], kc_raw[:, bass.ds(g * 32, 32)], kc_hi[:],
                                            ALU.subtract).then_inc(s["k_lo"], 1)
                    def stage(i):
                        for j in range(2):
                            r = slice(64 * j, 64 * j + 64)
                            pool.wait_ge(s["q_hi"], 2 * i + (j + 1))
                            nc.gpsimd.tensor_tensor(nq_lo[r, j, :], nqk[r, i, :], nq_hi[r, j, :],
                                                    ALU.subtract).then_inc(s["q_lo"], 1)
                            pool.wait_ge(s["q_lo"], 2 * i + (j + 1))

                    pool.wait_ge(s["k_lo"], 6 * g + 6)
                    stage(4 * g)
                    for p in range(4):
                        i = 4 * g + p
                        if p < 3:
                            pool.wait_ge(s["r_done"], i + 1)
                            stage(4 * g + (p + 1))
                        pool.wait_ge(s["r_swapped"], i + 1)
                        nc.gpsimd.tensor_tensor(r_swap[:], r_swap[:], ret_s[:], ALU.mult).then_inc(s["r_sines"], 1)
                        pool.wait_ge(s["r_out"], i + 2)
                        pool.wait_ge(s["r_sines"], i + 1)
                        apart(pool)
                        nc.gpsimd.tensor_tensor(r_qk[:, i, :], r_qk[:, i, :], r_swap[:], ALU.add).then_inc(s["r_done"], 1)

            return act_part, pe_part, dve_part, pool_part, (s["out"], 17), (s["r_done"], 9)

        def retention(before):
            s = {k: sem(f"ret_{k}") for k in ("v", "staged_hi", "staged_lo", "scored", "weighted", "hi", "lo", "summed",
                                              "out", "mean", "centred", "square", "var", "root", "recip", "done",
                                              "gate", "gated")}
            decay_in = sem("ret_decay_in")
            frv, fgr = FIRST["b2_rv"], FIRST["b2_gr"]

            def v_pe(pe):
                for w in before:
                    pe.wait_ge(*w)
                for c in range(2):
                    for j in range(4):
                        slot = ready(pe, frv, 4 * c + j)
                        if c and j == 0:
                            pe.wait_ge(s["v"], 4)
                        for t in range(2):
                            k, w = 2 * j + t, slice(t * S, (t + 1) * S)
                            for tb in range(TB):
                                at = slice(tb * P, (tb + 1) * P)
                                last = mm3(banks[4 + tb][:], xn_hi[:, k, at], xn_lo[:, k, at], w_hi[:, slot, w],
                                           w_lo[:, slot, w], k == 0, k == KT - 1)
                        last.then_inc(used, 1)

            def v_act(act):
                for j in range(8):
                    ahead(high_part, act, frv, j)

            def v_dve(dve):
                for c in range(2):
                    for j in range(4):
                        ahead(low_part, dve, frv, 4 * c + j)
                    finished(dve, frv, 4 * c + 3)
                    for tb in range(TB):
                        nc.vector.tensor_copy(r_v[:, tb, c * S:(c + 1) * S], banks[4 + tb][:]).then_inc(s["v"], 1)

            start = [*before, (s["v"], 8)]
            ORDER_K = (0, 1, 3, 2)

            def begin(eng):
                for w in start:
                    eng.wait_ge(*w)

            def score_bank(kb):
                return (banks[0][:], banks[1][:, 0:384], banks[2][:, 0:256], banks[1][:, 384:S])[kb]

            def pe_part(pe):
                begin(pe)
                pe.sem_inc(s["summed"], 8)
                with pe.Fori(0, 2) as t:
                    def score(c):
                        r = slice(64 * (c % 2), 64 * (c % 2) + 64)
                        for n, kb in enumerate(ORDER_K):
                            pe.wait_ge(s["weighted"], 16 * t + (4 * c + (1, 3, 3, 4)[n]))
                            mm3(score_bank(kb), rk_hi[r, kb * P:(kb + 1) * P], rk_lo[r, kb * P:(kb + 1) * P],
                                rq_hi[r, kb * P:S], rq_lo[r, kb * P:S]).then_inc(s["scored"], 1)

                    def values(c):
                        pe.wait_ge(s["out"], 4 * t + (c + 1))
                        w = slice(P * (c % 2), P * (c % 2) + P)
                        for n, kb in enumerate(ORDER_K):
                            pe.wait_ge(s["lo"], 16 * t + (4 * c + n + 5))
                            mm3(banks[6 + c % 2][:, kb * P:S], rv_hi[:, kb, w], rv_lo[:, kb, w],
                                ws_hi[:, KOFF[kb]:KOFF[kb + 1]], ws_lo[:, KOFF[kb]:KOFF[kb + 1]], n == 0,
                                n == TB - 1).then_inc(s["summed"], 1)

                    def gates_half(slot, half):
                        for k in range(4 * half, 4 * half + 4):
                            w = slice(k * P, (k + 1) * P)
                            last = mm3(banks[3][:], w_hi[:, slot, w], w_lo[:, slot, w], xn_hi[:, k, :], xn_lo[:, k, :],
                                       k == 0, k == KT - 1)
                        return last

                    pe.wait_ge(s["staged_lo"], 6 * t + 3)
                    score(0)
                    for c in range(4):
                        if c == 1:
                            pe.wait_ge(s["staged_lo"], 6 * t + 5)
                        if c == 2:
                            pe.wait_ge(s["staged_lo"], 6 * t + 6)
                        if c < 3:
                            score(c + 1)
                        slot = ready(pe, fgr, c, t, 4)
                        values(c)
                        pe.wait_ge(s["gate"], 4 * t + (c + 1))
                        gates_half(slot, 0)
                        pe.wait_ge(s["out"], 4 * t + (c + 3))
                        nc.tensor.matmul(banks[4][:], ones[:], r_raw[:, 4 * t + c, :], start=True,
                                         stop=True).then_inc(s["mean"], 1)
                        gates_half(slot, 1).then_inc(used, 1)
                        pe.wait_ge(s["square"], 4 * t + (c + 1))
                        pe.wait_ge(s["root"], 4 * t + (c + 1))
                        nc.tensor.matmul(banks[5][:], ones[:], gn_sq[:], start=True, stop=True).then_inc(s["var"], 1)

            def act_part(act):
                begin(act)
                act.sem_inc(s["out"], 2)
                act.sem_inc(s["root"], 1)
                act.sem_inc(s["gate"], 1)
                with act.Fori(0, 2) as t:
                    def stage_qk(pair):
                        nc.scalar.activation(rq_hi[:], r_qk[:, 2 * t + pair, :], ACT.Copy).then_inc(s["staged_hi"], 1)
                        nc.scalar.activation(rk_hi[:], r_qk[:, 2 * t + (4 + pair), :], ACT.Copy).then_inc(s["staged_hi"], 1)

                    def stage_v(pair):
                        nc.scalar.activation(rv_hi[:], r_v[:, :, bass.ds(t * 4 * P + pair * 2 * P, 2 * P)],
                                             ACT.Copy).then_inc(s["staged_hi"], 1)

                    act.wait_ge(s["summed"], 16 * t + 8)
                    stage_qk(0)
                    stage_v(0)
                    def highs(c):
                        for n, kb in enumerate(ORDER_K):
                            act.wait_ge(s["weighted"], 16 * t + (4 * c + n + 5))
                            act.wait_ge(s["summed"], 16 * t + (4 * c + n + 5))
                            nc.scalar.activation(ws_hi[:, KOFF[kb]:KOFF[kb + 1]], weighted[:, KOFF[kb]:KOFF[kb + 1]],
                                                 ACT.Copy).then_inc(s["hi"], 1)

                    highs(0)
                    for c in range(4):
                        if c == 0:
                            act.wait_ge(s["scored"], 16 * t + 8)
                            stage_qk(1)
                        ahead(high_part, act, fgr, c, t, 4)
                        act.wait_ge(s["summed"], 16 * t + (4 * c + 12))
                        nc.scalar.activation(r_raw[:, 4 * t + c, :], banks[6 + c % 2][:], ACT.Copy).then_inc(s["out"], 1)
                        if c == 1:
                            stage_v(1)
                        act.wait_ge(s["centred"], 4 * t + (c + 1))
                        apart(act)
                        nc.scalar.activation(gn_sq[:], r_raw[:, 4 * t + c, :], ACT.Square).then_inc(s["square"], 1)
                        if c < 3:
                            highs(c + 1)
                        act.wait_ge(s["var"], 4 * t + (c + 1))
                        act.wait_ge(s["done"], 4 * t + (c + 1))
                        nc.scalar.activation(gn_r[:], banks[5][:], ACT.Sqrt, bias=col[:, COLS["gneps"]:COLS["gneps"] + 1],
                                             scale=1.0 / P).then_inc(s["root"], 1)
                        finished(act, fgr, c, t, 4)
                        apart(act)
                        nc.scalar.activation(r_qk[:, 2 * t + (c // 2 + 4 * (c % 2)), :], banks[3][:],
                                             ACT.Copy).then_inc(s["gate"], 1)
                for c in range(8):
                    tile = c // 2 + 4 * (c % 2)
                    act.wait_ge(s["gate"], c + 2)
                    nc.scalar.activation(r_qk[:, tile, :], r_qk[:, tile, :], ACT.Silu).then_inc(s["gate"], 1)

            def dve_part(dve):
                begin(dve)
                dve.sem_inc(s["weighted"], 4)
                dve.sem_inc(s["done"], 1)
                with dve.Fori(0, 2) as t:
                    def weigh(c, blocks):
                        for n in blocks:
                            kb = ORDER_K[n]
                            if n == 0:
                                dve.wait_ge(decay_in, 64 * t + (16 * c + 16))
                            dve.wait_ge(s["scored"], 16 * t + (4 * c + (1, 3, 3, 4)[n]))
                            dve.wait_ge(s["lo"], 16 * t + (4 * c + n + 1))
                            nc.vector.tensor_tensor(weighted[:, KOFF[kb]:KOFF[kb + 1]], score_bank(kb),
                                                    decay[:, c % 2, 0:S - kb * P], ALU.mult).then_inc(s["weighted"], 1)

                    weigh(0, range(TB))
                    for c in range(4):
                        ahead(low_part, dve, fgr, c, t, 4)
                        dve.wait_ge(s["mean"], 4 * t + (c + 1))
                        nc.vector.scalar_tensor_tensor(r_raw[:, 4 * t + c, :], banks[4][:], -1.0 / P,
                                                       r_raw[:, 4 * t + c, :], ALU.mult, ALU.add).then_inc(s["centred"], 1)
                        if c < 3:
                            weigh(c + 1, range(TB))
                        dve.wait_ge(s["root"], 4 * t + (c + 2))
                        nc.vector.reciprocal(gn_r[:], gn_r[:]).then_inc(s["recip"], 1)
                        dve.wait_ge(s["recip"], 4 * t + (c + 1))
                        nc.vector.scalar_tensor_tensor(r_raw[:, 4 * t + c, :], r_raw[:, 4 * t + c, :],
                                                       col[:, bass.ds(t * 4 + (COLS["ret"] + c), 1)], gn_r[:], ALU.mult,
                                                       ALU.mult).then_inc(s["done"], 1)
                for c in range(8):
                    dve.wait_ge(s["gate"], 10 + c)
                    dve.wait_ge(s["done"], c + 2)
                    nc.vector.tensor_tensor(r_raw[:, c, :], r_raw[:, c, :], r_qk[:, c // 2 + 4 * (c % 2), :],
                                            ALU.mult).then_inc(s["gated"], 1)

            def pool_part(pool):
                begin(pool)
                pool.sem_inc(s["lo"], 4)
                with pool.Fori(0, 2) as t:
                    def decays_in(c):
                        pool.wait_ge(s["weighted"], 16 * t + (4 * c + 1))
                        pool.dma_start(decay[:, c % 2, :], decays[4 * t + c]).then_inc(decay_in, 16)

                    def stage_qk(pair):
                        for n, (to, hi) in enumerate(((rq_lo, rq_hi), (rk_lo, rk_hi))):
                            pool.wait_ge(s["staged_hi"], 6 * t + (3 * pair + n + 1))
                            nc.gpsimd.tensor_tensor(to[:], r_qk[:, 2 * t + (4 * n + pair), :], hi[:],
                                                    ALU.subtract).then_inc(s["staged_lo"], 1)

                    def stage_v(pair):
                        pool.wait_ge(s["staged_hi"], 6 * t + (3 * pair + 3))
                        nc.gpsimd.tensor_tensor(rv_lo[:], r_v[:, :, bass.ds(t * 4 * P + pair * 2 * P, 2 * P)], rv_hi[:],
                                                ALU.subtract).then_inc(s["staged_lo"], 1)

                    decays_in(0)
                    stage_qk(0)
                    stage_v(0)
                    for c in range(4):
                        if c < 3:
                            decays_in(c + 1)
                        if c == 2:
                            stage_v(1)
                        for n, kb in enumerate(ORDER_K):
                            pool.wait_ge(s["hi"], 16 * t + (4 * c + n + 1))
                            nc.gpsimd.tensor_tensor(ws_lo[:, KOFF[kb]:KOFF[kb + 1]], weighted[:, KOFF[kb]:KOFF[kb + 1]],
                                                    ws_hi[:, KOFF[kb]:KOFF[kb + 1]], ALU.subtract).then_inc(s["lo"], 1)
                        if c == 0:
                            stage_qk(1)

            return [(v_act, v_pe, v_dve, skip), (act_part, pe_part, dve_part, pool_part, (s["gated"], 8))]

        split = (xn_hi, xn_lo)
        natural = list(range(KT))

        def first_splits(act):
            for c in range(LOOKAHEAD):
                high_part(act, *place(0, c))

        n_mix1 = norm("n_mix1", x, natural, COLS["mix1"], None, 7, D, split, first_splits)
        parts.append(n_mix1)
        front = mixer1(n_mix1[4])
        parts.extend(front)
        m_b1 = merge("b1", [front[-1][4], front[-1][5]], m1_hi, m1_lo, None,
                     [(0, 0, 2, y1[:, 0:4, :], y1_hi[:, 0:4, :], y1_lo[:, 0:4, :]),
                      (0, 4, 3, y1[:, 4:8, :], y1_hi[:, 4:8, :], y1_lo[:, 4:8, :])], 1, COLS["bgate"], (mq, mk))
        f0 = feed_forward("f0", 1.0, COLS["ffn0"], m_b1[4], natural)
        n_fin1 = norm("n_fin1", x, ORDER, COLS["fin1"], f0[4], 7, D)
        f1 = feed_forward("f1", 0.5, COLS["ffn1"], (n_fin1[4][0], n_fin1[4][1] - KT + 1), ORDER)
        parts.extend([m_b1, f0, n_fin1, f1])
        n_mix2 = norm("n_mix2", x, ORDER, COLS["mix2"], f1[4], 7, D, split)
        second = mixer2(n_mix2, f1[4])
        parts.extend(second)
        m_b2 = merge("b2", [second[-1][4]], m2_hi, m2_lo, m2_temps,
                     [(2, 0, 2, a_raw[:, :, :], a_hi, a_lo), (3, 0, 3, r_raw[:, :, :], r_hi, r_lo)], 4, None)
        f2 = feed_forward("f2", 0.5, COLS["ffn2"], m_b2[4], natural)
        n_fin2 = norm("n_fin2", x, ORDER, COLS["fin2"], f2[4], 7, D)
        parts.extend([m_b2, f2, n_fin2])
        final_done = n_fin2[4]

        block = top.enter_context(nc.Block())

        @block.sync
        def _(sp):
            sp.dma_start(col[:], cols[:, P:2 * P]).then_inc(x_in[0], 16)
            for half in range(2):
                tiles = slice(4 * half, 4 * half + 4)
                sp.dma_start(x[:, tiles], xt.rearrange("p (k s) -> p k s", s=S)[:, tiles]).then_inc(x_in[half], 16)
            for slot in range(2):
                sp.dma_start(w_raw[:, slot, :], stream[slot]).then_inc(loaded[slot], 16)
            sp.dma_start(ident[:], cols[:, 0:P]).then_inc(consts_in, 16)
            sp.dma_start(bias_tri[:], tables[:, S:2 * S]).then_inc(consts_in, 16)
            sp.dma_start(bias_chunk[:], tables[:, 2 * S:3 * S]).then_inc(consts_in, 16)
            sp.dma_start(cumul_raw[:], tables[:, 0:S]).then_inc(consts_in, 16)
            sp.dma_start(w2_sb[:], w2.rearrange("p (t d) -> p t d", d=P)).then_inc(consts_in, 16)
            with sp.Fori(1, CHUNKS // 2) as i:
                for slot in range(2):
                    sp.wait_ge(split_lo, 2 * i + (slot - 1))
                    sp.dma_start(w_raw[:, slot, :], stream[2 * i + slot]).then_inc(loaded[slot], 16)
            if CHUNKS % 2:
                sp.wait_ge(split_lo, CHUNKS - 2)
                sp.dma_start(w_raw[:, 0, :], stream[CHUNKS - 1]).then_inc(loaded[0], 16)
            for k, tiles in enumerate((slice(7, 8), slice(0, 3), slice(3, 5), slice(5, 7))):
                sp.wait_ge(final_done[0], final_done[1] - KT + (1, 4, 6, 8)[k])
                sp.dma_start(out.rearrange("p (k s) -> p k s", s=S)[:, tiles], x[:, tiles]).then_inc(stored, 16)
            sp.wait_ge(stored, 64)

        @block.scalar
        def _(act):
            parts[0][0](act)
            act.wait_ge(consts_in, 80)
            for part in parts[1:]:
                part[0](act)

        @block.tensor
        def _(pe):
            pe.sem_inc(used, RING)
            pe.wait_ge(consts_made, 1)
            parts[0][1](pe)
            pe.wait_ge(consts_in, 80)
            pe.wait_ge(consts_made, 2)
            for part in parts[1:]:
                part[1](pe)

        @block.vector
        def _(dve):
            nc.vector.memset(ones[:], 1.0).then_inc(consts_made, 1)
            for half in range(2):
                dve.wait_ge(x_in[half], (32, 16)[half])
            for c in range(LOOKAHEAD):
                low_part(dve, *place(0, c))
            parts[0][2](dve)
            dve.wait_ge(consts_in, 80)
            for part in parts[1:]:
                part[2](dve)

        @block.gpsimd
        def _(pool):
            pool.wait_ge(consts_in, 80)
            pool.wait_ge(consts_made, 1)
            nc.gpsimd.tensor_copy(cumul[:], cumul_raw[:]).then_inc(consts_made, 1)
            for part in parts:
                part[3](pool)


def _tiles(w):
    k, n = w.shape
    return w.reshape(k // P, P, n // P, P).transpose(2, 1, 0, 3).reshape(n // P, P, k)


def _token_major(w):
    k, n = w.shape
    per = CW // n
    return w.reshape(k // P // per, per, P, n).transpose(0, 2, 1, 3).reshape(-1, P, CW)


def _pad(w, n=P):
    return np.concatenate([w, np.zeros((w.shape[0], n - w.shape[1]), w.dtype)], 1)


def _gate_up(gate, up):
    return np.stack([_tiles(gate), _tiles(up)], 1).reshape(-1, P, CW)


def _column(v):
    return v.reshape(-1, P).T


def pack_first(a):
    w = a["w_in"][0]
    at = np.cumsum([0, 512, 512, 512, 8, 256, 128, 32, D, D])
    qa, ka, va, fa, cq, ckv, kr, ga, gb = (w[:, i:j] for i, j in zip(at[:-1], at[1:]))
    fk = np.concatenate([_pad(fa, 64), kr, kr], 1)
    wq = a["w_q_up"][0].reshape(256, 8, 96)
    q_up = np.concatenate([wq, wq[:, :, 80:], wq[:, :, 64:80]], 2).reshape(256, D)
    wkv = a["w_kv_up"][0].reshape(P, 8, P)
    k_up = np.concatenate([wkv[:, :, :64], np.zeros((P, 8, 64), w.dtype)], 2).reshape(P, CW)
    v_up = _pad(wkv[:, :, 64:].reshape(P, 512), CW)
    gates = np.stack([_tiles(ga), _tiles(gb)], 1).reshape(-1, P, CW)
    merge = np.concatenate([_tiles(a["w_branch_a"][0]), _tiles(a["w_branch_b"][0])], 2)
    return [_tiles(qa), _tiles(ka), _tiles(cq), _tiles(ckv), _tiles(fk), _token_major(va),
            _tiles(q_up).reshape(2, 4, P, 256).transpose(0, 2, 1, 3).reshape(2, P, CW), k_up[None], v_up[None],
            gates, merge, _tiles(a["w_out"][0]),
            _gate_up(a["w_ffn_gate"][0], a["w_ffn_up"][0]), a["w_ffn_down"][0].reshape(FT, P, CW)]


def pack_cols(a):
    cols = np.zeros((P, P), np.float32)

    def put(name, v):
        cols[:v.shape[0], COLS[name]:COLS[name] + v.shape[1]] = v

    for name, key in (("mix1", "norm_mix_g"), ("qa", "q_a_norm_g"), ("kva", "kv_a_norm_g"), ("bgate", "b_gate"),
                      ("ffn0", "norm_ffn_g"), ("fin1", "norm_final_g"), ("ffn1", "ffn1_norm_2"),
                      ("mix2", "mix_norm_2"), ("ret", "ret_gn_gain_2"), ("ffn2", "ffn2_norm_2"),
                      ("fin2", "final_norm_2")):
        put(name, _column(a[key].reshape(-1)))
    cols[0:8, COLS["bf"]] = a["b_forget"].reshape(-1)
    half = np.float32(10000.0) ** (-np.arange(16, dtype=np.float32) / 16)
    cols[64:, COLS["freq"]] = np.tile(half, 4)
    cols[64:, COLS["sgn"]] = np.tile(np.repeat(np.float32([-1, 1]), 16), 2)
    cols[:, COLS["eps"]] = EPS
    cols[:, COLS["gneps"]] = GN_EPS
    cols[:, COLS["one"]] = 1.0
    put("pos", a["cmp_pos_emb_2"][0].reshape(16, P).T)
    return np.concatenate([np.eye(P, dtype=np.float32), cols], 1)


def shape_tables():
    row, at = np.arange(P)[:, None], np.arange(S)[None, :]
    cumul = np.where(at >= row, -8.0, 0.0)
    tri = np.where(at - (S - P) > row, -1e30, 0.0)
    chunk = np.where((at - (S - P)) // 64 > row // 64, -1e30, 0.0)
    return np.concatenate([cumul, tri, chunk], 1).astype(np.float32)


def _twice(w):
    return np.concatenate([w, w], 1)


def pack_second(a):
    w = a["w_in_2"][0]
    at = np.cumsum([0, D, P, P, P, P, P, P, 48, S, S, D, D, D, D])
    (q, kc, vc, ks, vs, kw, vw, g, rq, rk, rv, rg, ga, gr) = (w[:, i:j] for i, j in zip(at[:-1], at[1:]))

    def groups(w):
        return np.concatenate([_twice(w[:, :64]), _twice(w[:, 64:])], 1)

    order = np.concatenate([np.arange(0, 16), np.arange(32, 48), np.arange(16, 32), np.arange(48, 64)])
    order = (64 * np.arange(8)[:, None] + order).reshape(-1)
    merge = np.stack([_tiles(ga), _tiles(gr), _tiles(a["w_branch_nsa_2"][0]), _tiles(a["w_branch_ret_2"][0])], 1)

    def hidden(w):
        return _tiles(w).reshape(2, P, 2, CW).transpose(0, 2, 1, 3).reshape(4, P, CW)

    w1 = np.concatenate([hidden(a["cmp_k_w1_2"][0]), hidden(a["cmp_v_w1_2"][0])])
    w1_q = np.stack([w1, _tiles(q)], 1).reshape(-1, P, CW)
    return [_gate_up(a["ffn1_w_gate_2"][0], a["ffn1_w_up_2"][0]), a["ffn1_w_down_2"][0].reshape(FT, P, CW),
            _tiles(groups(kc)), _tiles(groups(vc)), _token_major(np.concatenate([vs, vw], 1)), _tiles(_pad(g)),
            w1_q, _tiles(groups(ks)), _tiles(groups(kw)), _tiles(rq[:, order]), _tiles(rk[:, order]), _token_major(rv[:, :S]),
            _token_major(rv[:, S:]), _tiles(rg), merge.reshape(-1, P, CW), _tiles(a["w_out_2"][0]),
            _gate_up(a["ffn2_w_gate_2"][0], a["ffn2_w_up_2"][0]), a["ffn2_w_down_2"][0].reshape(FT, P, CW)]


def second_tables():
    row = np.arange(P) % 64

    def rope(positions, freq, sign, rotated):
        angle = positions.astype(np.float32)[None, :] * freq[:, None]
        cos = np.where(rotated[:, None], np.cos(angle), 1.0)
        sin = np.where(rotated[:, None], sign[:, None] * np.sin(angle), 0.0)
        return [cos, sin]

    f16 = np.float32(500000.0) ** (-(np.arange(8, dtype=np.float32) * np.float32(2.0) / np.float32(16)))
    f64 = np.float32(10000.0) ** (-(np.arange(32, dtype=np.float32) * np.float32(2.0) / np.float32(64)))
    nsa = (f16[row % 8], np.where(row < 8, -1.0, 1.0), row < 16)
    ret = (f64[(row // 32) * 16 + row % 16], np.where(row % 32 < 16, -1.0, 1.0), row < 64)
    tokens, windows = np.arange(S), np.tile(16 * np.arange(32) + 31, 2)
    query = np.arange(P)[:, None, None] + P * np.arange(TB)[None, :, None]
    seen = (16 * np.arange(32) + 31 <= query) & (np.arange(32) < 31)
    rows = [*rope(tokens, *nsa), *rope(tokens, *ret), *rope(windows, *nsa),
            np.where(seen, 0.0, -1e30).reshape(P, P), seen.reshape(P, P)]
    return np.concatenate([r.astype(np.float32) for r in rows], 1)


def decay_tables():
    head = np.arange(8)[:, None, None]
    gap = np.arange(S)[None, None, :] - np.arange(P)[None, :, None]
    return np.where(gap >= 0, 0.125 * (1.0 - 2.0 ** (-5.0 - head)) ** np.maximum(gap, 0), 0.0).astype(np.float32)


def kernel(**inputs):
    from concourse import bacc
    from concourse.bass_utils import run_bass_kernel_spmd

    a = {k: np.asarray(v) for k, v in inputs.items()}
    nc = bacc.Bacc("TRN2", target_bir_lowering=False, num_devices=1)
    data = {
        "stream": np.concatenate(pack_first(a) + pack_second(a)),
        "xt": np.ascontiguousarray(a["x"][0].T.reshape(KT, P, S).transpose(1, 0, 2).reshape(P, -1)),
        "cols": pack_cols(a),
        "tables": shape_tables(),
        "rows": second_tables(),
        "decays": decay_tables(),
        "pos": np.ascontiguousarray(a["positions"].reshape(-1)),
        "w2": np.concatenate([_twice(w[0].reshape(2, P, 64)[half]) for w in (a["cmp_k_w2_2"], a["cmp_v_w2_2"])
                              for half in range(2)], 1),
    }
    args = {n: nc.dram_tensor(n, v.shape, mybir.dt.from_np(v.dtype), kind="ExternalInput").ap()
            for n, v in data.items()}
    out = nc.dram_tensor("out", (P, KT * S), F32, kind="ExternalOutput").ap()
    build_program(nc, **args, out=out)
    got = run_bass_kernel_spmd(nc, [data], core_ids=[0]).results[0]["out"]
    return np.ascontiguousarray(got.reshape(P, KT, S).transpose(2, 1, 0).reshape(1, S, D))
```
